# Optimizing a Trainium2 kernel written in Bass

```python
import jax, jax.numpy as jnp
from jax import lax
import numpy as np

D_MODEL = 1024
BATCH = 1
SEQ = 512
DEPTH = 1
DEC_BATCH = 8
DEC_SEQ = 8
PAST_LEN = 1024
PAGE_SIZE = 128

HEAD_DIM = 64
N_Q_HEADS = 8
N_KV_HEADS = 2
GQA_GROUP = N_Q_HEADS // N_KV_HEADS
ATTN_WIDTH = N_Q_HEADS * HEAD_DIM
WINDOW = 128
ATTN_BLOCK = WINDOW
ROPE_THETA = 10000.0
N_GMLP_HEADS = 8
GMLP_HEAD_DIM = 64
GMLP_WIDTH = N_GMLP_HEADS * GMLP_HEAD_DIM
CHUNK = 128
MIX_WIDTH = ATTN_WIDTH + GMLP_WIDTH
Q_END = ATTN_WIDTH
K_END = Q_END + N_KV_HEADS * HEAD_DIM
V_END = K_END + N_KV_HEADS * HEAD_DIM
GU_END = V_END + GMLP_WIDTH
IN_WIDTH = GU_END + GMLP_WIDTH
N_MEM = 256
MEM_HEADS = 4
MEM_HEAD_DIM = 64
MEM_WIDTH = MEM_HEADS * MEM_HEAD_DIM
PEER_HEADS = 8
N_KEYS = 128
N_EXPERTS = N_KEYS * N_KEYS
PEER_TOPK = 16
D_KEY = 256
D_HALF = D_KEY // 2
PEER_BLOCK = 128
EPS = 1e-6
NEG_INF = -1e30

kernel_name = 'hymba_swa_sgu_peer_decode_step'

def rms_norm(x, g):
    xf = x.astype(jnp.float32)
    y = xf * lax.rsqrt(jnp.mean(xf * xf, axis=-1, keepdims=True) + EPS)
    return (y * g.astype(jnp.float32)).astype(x.dtype)

def rope(x, pos):
    half = HEAD_DIM // 2
    inv = ROPE_THETA ** (-jnp.arange(half, dtype=jnp.float32) / half)
    ang = pos.astype(jnp.float32)[:, None] * inv[None, :]
    cos = jnp.cos(ang)[:, None, :]
    sin = jnp.sin(ang)[:, None, :]
    x1 = x[..., :half].astype(jnp.float32)
    x2 = x[..., half:].astype(jnp.float32)
    return jnp.concatenate([x1 * cos - x2 * sin, x2 * cos + x1 * sin], axis=-1).astype(x.dtype)

def sink_attention(q, k, v, qpos, kpos, sinks):
    s = jnp.einsum('...qhgd,...khd->...hgqk', q, k).astype(jnp.float32) * (HEAD_DIM ** -0.5)
    diff = qpos[..., :, None] - kpos[..., None, :]
    valid = (kpos[..., None, :] >= 0) & (diff >= 0) & (diff < WINDOW)
    s = jnp.where(valid[..., None, None, :, :], s, NEG_INF)
    sink = sinks.astype(jnp.float32)[:, :, None, None]
    m = jnp.maximum(jnp.max(s, axis=-1, keepdims=True), sink)
    p = jnp.exp(s - m)
    probs = p / (jnp.sum(p, axis=-1, keepdims=True) + jnp.exp(sink - m))
    return jnp.einsum('...hgqk,...khd->...qhgd', probs.astype(v.dtype), v)

def swa_prompt(q, k, v, sinks):
    B, S = q.shape[0], q.shape[1]
    nb = S // ATTN_BLOCK
    qb = q.reshape(B, nb, ATTN_BLOCK, N_KV_HEADS, GQA_GROUP, HEAD_DIM)
    kb = k.reshape(B, nb, ATTN_BLOCK, N_KV_HEADS, HEAD_DIM)
    vb = v.reshape(B, nb, ATTN_BLOCK, N_KV_HEADS, HEAD_DIM)
    pad = ((0, 0), (1, 0), (0, 0), (0, 0), (0, 0))
    k_band = jnp.concatenate([jnp.pad(kb[:, :-1], pad), kb], axis=2)
    v_band = jnp.concatenate([jnp.pad(vb[:, :-1], pad), vb], axis=2)
    starts = jnp.arange(nb, dtype=jnp.int32) * ATTN_BLOCK
    qpos = starts[:, None] + jnp.arange(ATTN_BLOCK, dtype=jnp.int32)[None, :]
    kpos = starts[:, None] - ATTN_BLOCK + jnp.arange(2 * ATTN_BLOCK, dtype=jnp.int32)[None, :]
    o = sink_attention(qb, k_band, v_band, qpos, kpos, sinks.reshape(N_KV_HEADS, GQA_GROUP))
    return o.reshape(B, S, ATTN_WIDTH)

def swa_sample(q, k, v, k_buf, v_buf, sinks):
    DB, T = q.shape[0], q.shape[1]
    W = k_buf.shape[1]
    qg = q.reshape(DB, T, N_KV_HEADS, GQA_GROUP, HEAD_DIM)
    kc = jnp.concatenate([k_buf, k], axis=1)
    vc = jnp.concatenate([v_buf, v], axis=1)
    qpos = PAST_LEN + jnp.arange(T, dtype=jnp.int32)
    kpos = PAST_LEN - W + jnp.arange(W + T, dtype=jnp.int32)
    o = sink_attention(qg, kc, vc, qpos, kpos, sinks.reshape(N_KV_HEADS, GQA_GROUP))
    return o.reshape(DB, T, ATTN_WIDTH), kc[:, T:], vc[:, T:]

def spatial_gate(u, v, w_s, b_s):
    L = u.shape[-3]
    w = jnp.tril(w_s[:, :L, :L]).astype(v.dtype)
    mixed = jnp.einsum('htr,...rhd->...thd', w, v) + b_s[:, :L].T[:, :, None].astype(v.dtype)
    return u * mixed

def token_mixer(xn, pos, w_in, sinks, g_sgu, w_s, b_s, g_attn_out, g_gmlp_out, w_out,
                k_buf=None, v_buf=None):
    B, T = xn.shape[0], xn.shape[1]
    proj = xn @ w_in
    q, k, v, gu, gv = jnp.split(proj, [Q_END, K_END, V_END, GU_END], axis=-1)
    q = rope(q.reshape(B, T, N_Q_HEADS, HEAD_DIM), pos)
    k = rope(k.reshape(B, T, N_KV_HEADS, HEAD_DIM), pos)
    v = v.reshape(B, T, N_KV_HEADS, HEAD_DIM)
    gu = jax.nn.gelu(gu, approximate=False).reshape(B, T, N_GMLP_HEADS, GMLP_HEAD_DIM)
    gv = rms_norm(jax.nn.gelu(gv, approximate=False).reshape(B, T, N_GMLP_HEADS, GMLP_HEAD_DIM), g_sgu)
    if k_buf is None:
        attn = swa_prompt(q, k, v, sinks)
        keep = min(WINDOW, T)
        new_k, new_v = k[:, T - keep:], v[:, T - keep:]
        nc = T // CHUNK
        sgu = spatial_gate(gu.reshape(B, nc, CHUNK, N_GMLP_HEADS, GMLP_HEAD_DIM),
                           gv.reshape(B, nc, CHUNK, N_GMLP_HEADS, GMLP_HEAD_DIM), w_s, b_s)
    else:
        attn, new_k, new_v = swa_sample(q, k, v, k_buf, v_buf, sinks)
        sgu = spatial_gate(gu, gv, w_s, b_s)
    sgu = sgu.reshape(B, T, GMLP_WIDTH)
    merged = jnp.concatenate([rms_norm(attn, g_attn_out), rms_norm(sgu, g_gmlp_out)], axis=-1)
    return merged @ w_out, new_k, new_v, gv

def memory_kv(mem, g_mem, w_mk, w_mv):
    B, M = mem.shape[0], mem.shape[1]
    mn = rms_norm(mem, g_mem)
    return ((mn @ w_mk).reshape(B, M, MEM_HEADS, MEM_HEAD_DIM),
            (mn @ w_mv).reshape(B, M, MEM_HEADS, MEM_HEAD_DIM))

def memory_attention(xn, mem_k, mem_v, w_cq, w_co):
    B, T = xn.shape[0], xn.shape[1]
    q = (xn @ w_cq).reshape(B, T, MEM_HEADS, MEM_HEAD_DIM)
    s = jnp.einsum('bqhd,bkhd->bhqk', q, mem_k).astype(jnp.float32) * (MEM_HEAD_DIM ** -0.5)
    p = jax.nn.softmax(s, axis=-1).astype(mem_v.dtype)
    o = jnp.einsum('bhqk,bkhd->bqhd', p, mem_v).reshape(B, T, MEM_WIDTH)
    return o @ w_co

def peer_ffn(xn, w_pq, sub_keys, u_tab, v_tab):
    lead = xn.shape[:-1]
    xf = xn.reshape(-1, D_MODEL)
    T = xf.shape[0]
    pad = (-T) % PEER_BLOCK
    xb = jnp.pad(xf, ((0, pad), (0, 0))).reshape(-1, PEER_BLOCK, D_MODEL)

    def block(xt):
        q = (xt @ w_pq).reshape(PEER_BLOCK, PEER_HEADS, 2, D_HALF)
        s = jnp.einsum('thcd,hckd->thck', q, sub_keys).astype(jnp.float32)
        s1, i1 = lax.top_k(s[:, :, 0], PEER_TOPK)
        s2, i2 = lax.top_k(s[:, :, 1], PEER_TOPK)
        cand = (s1[..., :, None] + s2[..., None, :]).reshape(PEER_BLOCK, PEER_HEADS, PEER_TOPK * PEER_TOPK)
        cidx = (i1[..., :, None] * N_KEYS + i2[..., None, :]).reshape(PEER_BLOCK, PEER_HEADS, PEER_TOPK * PEER_TOPK)
        top, sel = lax.top_k(cand, PEER_TOPK)
        idx = jnp.take_along_axis(cidx, sel, axis=-1)
        gate = jax.nn.softmax(top, axis=-1)
        h = jnp.einsum('td,thkd->thk', xt, u_tab[idx]).astype(jnp.float32)
        a = (jax.nn.gelu(h, approximate=False) * gate).astype(xt.dtype)
        return jnp.einsum('thk,thkd->td', a, v_tab[idx])

    out = lax.map(block, xb).reshape(-1, D_MODEL)[:T]
    return out.reshape(*lead, D_MODEL)

def setup_inputs(seed: int = 0) -> dict:
    key = jax.random.key(seed)
    ks = jax.random.split(key, 32)
    f32 = jnp.float32

    def nrm(k, shape, scale):
        return jax.random.normal(k, shape, f32) * scale

    def gain(k, shape):
        return 1.0 + 0.05 * jax.random.normal(k, shape, f32)

    swa_buf = min(WINDOW, PAST_LEN)
    L = DEPTH
    return {
        'x_prompt': nrm(ks[0], (BATCH, SEQ, D_MODEL), 1.0),
        'x_sample': nrm(ks[1], (DEC_BATCH, DEC_SEQ, D_MODEL), 1.0),
        'mem_prompt': nrm(ks[2], (BATCH, N_MEM, D_MODEL), 1.0),
        'cache_swa_k': nrm(ks[3], (L, DEC_BATCH, swa_buf, N_KV_HEADS, HEAD_DIM), 1.0),
        'cache_swa_v': nrm(ks[4], (L, DEC_BATCH, swa_buf, N_KV_HEADS, HEAD_DIM), 1.0),
        'cache_mem_k': nrm(ks[5], (L, DEC_BATCH, N_MEM, MEM_HEADS, MEM_HEAD_DIM), 1.0),
        'cache_mem_v': nrm(ks[6], (L, DEC_BATCH, N_MEM, MEM_HEADS, MEM_HEAD_DIM), 1.0),
        'g_mix': gain(ks[7], (L, D_MODEL)),
        'w_in': nrm(ks[8], (L, D_MODEL, IN_WIDTH), D_MODEL ** -0.5),
        'attn_sinks': nrm(ks[9], (L, N_Q_HEADS), 0.5),
        'g_sgu': gain(ks[10], (L, N_GMLP_HEADS, GMLP_HEAD_DIM)),
        'w_spatial': nrm(ks[11], (L, N_GMLP_HEADS, CHUNK, CHUNK), CHUNK ** -0.5),
        'b_spatial': gain(ks[12], (L, N_GMLP_HEADS, CHUNK)),
        'g_attn_out': gain(ks[13], (L, ATTN_WIDTH)),
        'g_gmlp_out': gain(ks[14], (L, GMLP_WIDTH)),
        'w_out': nrm(ks[15], (L, MIX_WIDTH, D_MODEL), MIX_WIDTH ** -0.5),
        'g_cross': gain(ks[16], (L, D_MODEL)),
        'g_mem': gain(ks[17], (L, D_MODEL)),
        'w_cq': nrm(ks[18], (L, D_MODEL, MEM_WIDTH), D_MODEL ** -0.5),
        'w_mk': nrm(ks[19], (L, D_MODEL, MEM_WIDTH), D_MODEL ** -0.5),
        'w_mv': nrm(ks[20], (L, D_MODEL, MEM_WIDTH), D_MODEL ** -0.5),
        'w_co': nrm(ks[21], (L, MEM_WIDTH, D_MODEL), MEM_WIDTH ** -0.5),
        'g_ffn': gain(ks[22], (L, D_MODEL)),
        'w_peer_q': nrm(ks[23], (L, D_MODEL, PEER_HEADS * D_KEY), D_MODEL ** -0.5),
        'peer_sub_keys': nrm(ks[24], (L, PEER_HEADS, 2, N_KEYS, D_HALF), D_HALF ** -0.5),
        'peer_u': nrm(ks[25], (L, N_EXPERTS, D_MODEL), D_MODEL ** -0.5),
        'peer_v': nrm(ks[26], (L, N_EXPERTS, D_MODEL), PEER_HEADS ** -0.5),
        'g_final': gain(ks[27], (D_MODEL,)),
    }

def reference(x_prompt, x_sample, mem_prompt, cache_swa_k, cache_swa_v, cache_mem_k, cache_mem_v,
              g_mix, w_in, attn_sinks, g_sgu, w_spatial, b_spatial, g_attn_out, g_gmlp_out, w_out,
              g_cross, g_mem, w_cq, w_mk, w_mv, w_co, g_ffn, w_peer_q, peer_sub_keys, peer_u, peer_v,
              g_final):
    pos_p = jnp.arange(x_prompt.shape[1], dtype=jnp.int32)
    pos_s = PAST_LEN + jnp.arange(x_sample.shape[1], dtype=jnp.int32)
    xp, xs = x_prompt, x_sample
    swa_k_p, swa_v_p, mem_k_p, mem_v_p = [], [], [], []
    swa_k_s, swa_v_s, sgu_v_s = [], [], []
    for l in range(DEPTH):
        mix_w = (w_in[l], attn_sinks[l], g_sgu[l], w_spatial[l], b_spatial[l],
                 g_attn_out[l], g_gmlp_out[l], w_out[l])
        mp, kp, vp, _ = token_mixer(rms_norm(xp, g_mix[l]), pos_p, *mix_w)
        ms, ks_, vs_, gvs = token_mixer(rms_norm(xs, g_mix[l]), pos_s, *mix_w,
                                        cache_swa_k[l], cache_swa_v[l])
        xp = xp + mp
        xs = xs + ms
        mk, mv = memory_kv(mem_prompt, g_mem[l], w_mk[l], w_mv[l])
        xp = xp + memory_attention(rms_norm(xp, g_cross[l]), mk, mv, w_cq[l], w_co[l])
        xs = xs + memory_attention(rms_norm(xs, g_cross[l]), cache_mem_k[l], cache_mem_v[l],
                                   w_cq[l], w_co[l])
        peer_w = (w_peer_q[l], peer_sub_keys[l], peer_u[l], peer_v[l])
        xp = xp + peer_ffn(rms_norm(xp, g_ffn[l]), *peer_w)
        xs = xs + peer_ffn(rms_norm(xs, g_ffn[l]), *peer_w)
        swa_k_p.append(kp)
        swa_v_p.append(vp)
        mem_k_p.append(mk)
        mem_v_p.append(mv)
        swa_k_s.append(ks_)
        swa_v_s.append(vs_)
        sgu_v_s.append(gvs)
    y_prompt = rms_norm(xp, g_final)
    y_sample = rms_norm(xs, g_final)
    return (y_prompt, y_sample,
            jnp.stack(swa_k_p), jnp.stack(swa_v_p), jnp.stack(mem_k_p), jnp.stack(mem_v_p),
            jnp.stack(swa_k_s), jnp.stack(swa_v_s), jnp.stack(sgu_v_s))


_drawn_inputs = setup_inputs


def setup_inputs(seed=0):
    import zlib

    import numpy as np

    out = dict(_drawn_inputs(seed))
    spreads = {}
    factors = {'attn_sinks': 4.264, 'g_cross': 5.847}
    for name, (base, spread) in spreads.items():
        noise = np.random.default_rng([zlib.crc32(name.encode()), seed]).standard_normal(out[name].shape)
        drawn = base * np.exp(spread * noise) if base else spread * noise
        out[name] = __import__('jax').numpy.asarray(drawn.astype(out[name].dtype))
    for name, factor in factors.items():
        out[name] = (out[name] * factor).astype(out[name].dtype)
    return out
```

```python
from contextlib import ExitStack

import numpy as np

import concourse.bass as bass
from concourse import mybir

F32 = mybir.dt.float32
BF16 = mybir.dt.bfloat16
U32 = mybir.dt.uint32
ALU = mybir.AluOpType
ACT = mybir.ActivationFunctionType
AX_X = mybir.AxisListType.X

P = 128
D = 1024
KD = D // P
TILES = 5
NTOK = TILES * P
SAMPLES, SAMPLE_LEN = 8, 8
NS = SAMPLES * SAMPLE_LEN
PAST = 1024
HD = 64
HEADS, KV, GROUP = 8, 2, 4
NMEM = 256
MHEADS = 4
PHEADS, NKEYS, TOPK = 8, 128, 16
EPS = 1e-6
NEG = -1e30
LOWEST = -3.4028235e38
BLOCKS = 4 + 4 * PHEADS
RING = 4
INW = 1792


def shape_tables():
    t = {}
    r = np.arange(P)
    t["ident"] = np.eye(P)
    c = np.arange(2 * P)
    t["band"] = np.where((c[None] > r[:, None]) & (c[None] <= r[:, None] + P), 0.0, NEG)
    t["eps"] = np.full((P, 1), EPS)
    t["iota"] = np.broadcast_to(np.arange(TOPK), (P, TOPK))
    seq, head, tok = r // 32, (r // 8) % 4, r % 8
    t["headsel"] = (head[:, None] == np.arange(4)[None]) * 1.0
    gather = np.zeros((P, 2, P))
    for bg in range(2):
        for m in range(P):
            gather[:, bg, m] = ((bg * 4 + seq) * 8 + tok) == m % NS
    t["gather"] = gather.reshape(P, 2 * P)
    half = HD // 2
    inv = np.float32(10000.0) ** (-np.arange(half, dtype=np.float32) / np.float32(half))
    pos = np.stack([PAST + r % 8] + [i * P + r for i in range(TILES - 1)], 1).astype(np.float32)
    ang = pos[:, :, None] * inv[None, None, :].astype(np.float32)
    rot = np.concatenate([np.cos(ang), np.cos(ang), -np.sin(ang), np.sin(ang)], -1)
    t["rot"] = rot.reshape(P, TILES * 4 * half)
    sm = np.full((P, 2, P + NS), NEG)
    for bg in range(2):
        key = np.arange(P)
        sm[:, bg, :P] = np.where(key[None] > tok[:, None], 0.0, NEG)
        new = np.arange(NS)
        ok = (new[None] // 8 == (bg * 4 + seq)[:, None]) & (new[None] % 8 <= tok[:, None])
        sm[:, bg, P:] = np.where(ok, 0.0, NEG)
    t["smask"] = sm.reshape(P, 2 * (P + NS))
    t["blocks"] = ((r[:, None] // 8 == r[None] // 8) & (r[None] % 8 <= r[:, None] % 8)) * 1.0
    t["tril"] = np.tril(np.ones((P, P)))
    t["fold"] = (r[:, None] % NS == r[None] % NS) * 1.0
    return {k: np.ascontiguousarray(v, dtype=np.float32) for k, v in t.items()}


TABLES = {"ident": P, "band": 2 * P, "eps": 1, "iota": TOPK, "headsel": 4, "gather": 2 * P,
          "rot": TILES * P, "smask": 2 * (P + NS), "blocks": P, "tril": P, "fold": P}


def hybrid_step(nc, I, O):
    ctx = ExitStack()
    with ctx:
        def sb(name, n, dt=F32):
            return ctx.enter_context(nc.sbuf_tensor(name, [P, n], dt))

        def sem(name):
            return ctx.enter_context(nc.semaphore(name))

        x_res = sb("x_res", TILES * D)
        xT = sb("xT", KD * NTOK)
        A = sb("A", 16384)
        R = sb("R", 24960)
        ident = sb("ident", P)
        band = sb("band", 2 * P)
        eps = sb("eps", 1)
        iota = sb("iota", TOPK)
        headsel = sb("headsel", 4)
        gather = sb("gather", 2 * P)
        g_sgu = sb("g_sgu", 512)
        gains = sb("gains", 48)
        sinks = sb("sinks", HEADS)
        sinks_s = sb("sinks_s", KV)
        bias_p, bias_s = gains[:, 32:40], gains[:, 40:48]
        stat = sb("stat", 96)
        ps = ctx.enter_context(nc.psum_tensor("ps", [P, 8 * 512], F32))

        def bank(n, w=512, k=1):
            return ps[:, n * 512:n * 512 + w]

        def v3(ap, a):
            return ap.rearrange("p (a b) -> p a b", a=a)

        def xr(t):
            return x_res[:, bass.ds(t * D, D)] if not isinstance(t, int) else x_res[:, t * D:(t + 1) * D]

        xTv = v3(xT[:, :], KD)
        w_in = v3(A[:, 0:KD * INW], KD)
        rot = v3(A[:, 14336:14336 + TILES * P], TILES)
        tmp = A[:, 15872:16384]
        rows48 = A[0:48, 15000:15128]
        s_sb = v3(A[:, 0:2048], HEADS)
        pT = v3(A[:, 2048:4096], 16)
        w_smp = v3(A[:, 2048:3072], HEADS)
        qT = v3(A[:, 4096:4608], 4)
        wsp = v3(A[:, 5120:6144], HEADS)
        wT_p = v3(A[:, 6144:7168], HEADS)
        wT_s = v3(A[:, 7168:8192], HEADS)
        kc = v3(A[:, 8192:9216], SAMPLES)
        vc = v3(A[:, 9216:10240], SAMPLES)
        kcT = v3(A[:, 10240:11264], SAMPLES)
        smask = v3(A[:, 11264:11648], 2)
        blocks = A[:, 11648:11776]
        tril = A[:, 11776:11904]
        w8 = v3(A[:, 12288:12352], HEADS)
        qTr = v3(A[:, 12352:12608], 2)
        s_smp = v3(A[:, 12608:13376], 4)
        pTc = v3(A[:, 13376:13888], 4)
        pTn = v3(A[:, 13888:14400], 4)
        o_exp = v3(A[:, 14400:15424], 4)
        w_pq = v3(A[:, :], KD)
        w_out = v3(R[:, 0:8192], KD)
        PB = 8192

        def proj(t, a, b):
            return R[:, PB + t * INW + a:PB + t * INW + b]

        mem_x = v3(R[:, PB:PB + 2048], 2)
        mem_T = v3(R[:, PB + 2048:PB + 4096], KD)
        w_mk = v3(R[:, PB + 4096:PB + 6144], KD)
        w_mv = v3(R[:, PB + 6144:PB + 8192], KD)
        mk = v3(R[:, PB + 8192:PB + 8704], 2)
        w_cq = v3(R[:, 17152:19200], KD)
        w_co = v3(R[:, 19200:21248], 2)
        mv = v3(R[:, 21248:21760], 2)
        mkT = v3(R[:, 21760:22272], 2)
        kT = R[:, 22272:22912]
        xs = [R[:, 22912:23936], R[:, 23936:24960]]
        kmT = R[:, 0:4096].rearrange("p (b c k) -> p b c k", b=SAMPLES, c=2)
        s_c = v3(R[:, 4096:5120], MHEADS)
        pT_c = v3(R[:, 5120:6144], 8)
        qcT = v3(R[:, 6144:7424], 2)
        q_bd = v3(R[:, 7424:7936], 2)
        oT_c = v3(R[:, 7936:8192], 2)
        kmem = R[:, PB:PB + 4096].rearrange("p (b c k) -> p b c k", b=SAMPLES, c=2)
        vmem = R[:, PB + 4096:PB + 8192].rearrange("p (b c k) -> p b c k", b=SAMPLES, c=2)
        o_c = R[:, PB + 8192:PB + 8448]
        o_m = v3(R[:, PB + 8448:PB + 8960], 2)
        xn = R[:, 0:5120]
        u_ring = [R[:, 5120 + i * D:5120 + (i + 1) * D] for i in range(RING)]
        v_ring = [R[:, 9216 + i * D:9216 + (i + 1) * D] for i in range(RING)]
        sk_raw = v3(R[:, 5120:7168], 16)
        g_fin = R[:, 5120:6144]
        y_out = [R[:, 6144:7168], R[:, 7168:8192]]
        skT = R[:, 13312:15360]
        xn_cur = [R[:, 15360 + i * D:15360 + (i + 1) * D] for i in range(2)]
        xT_cur = [v3(R[:, 17408 + i * D:17408 + (i + 1) * D], KD) for i in range(2)]
        g_ffn = R[:, 19456:20480]
        fold = R[:, 20480:20608]
        diag = v3(R[:, 20608:21120], RING)
        ss = v3(R[:, 21632:21888], 2)
        ss2 = v3(R[:, 21888:22144], 2)
        cand = R[:, 22144:22400]
        onehot = R[:, 22400:22912]
        cand2 = R[:, 22912:23168]
        q_sb = R[:, 23168:23680]
        qT_sb = v3(R[:, 23680:24192], 4)
        idx = v3(R[:, 24192:24256].bitcast(U32), 4)
        gate = v3(R[:, 24256:24320], 4)
        topv = v3(R[:, 24320:24352], 2)
        topi = v3(R[:, 24352:24384].bitcast(U32), 2)
        bestv = R[:, 24384:24400]
        besti = R[:, 24400:24416].bitcast(U32)
        parts = v3(R[:, 24416:24448].bitcast(U32), 2)
        chosen = v3(R[:, 24448:24480], 2)
        hdot = v3(R[:, 24480:24512], 2)
        hgelu = v3(R[:, 24512:24544], 2)
        coef = v3(R[:, 24544:24576], 2)
        negtop = R[:, 24576:24577]
        esum = R[:, 24577:24578]
        rsum = R[:, 24578:24579]

        ssq = [stat[:, 0:2], stat[:, 2:4]]
        rstd = [stat[:, 4:6], stat[:, 6:8]]
        mx = stat[:, 8:16]
        nmx = stat[:, 16:24]
        rs = stat[:, 24:32]
        es = stat[:, 32:40]
        rden = stat[:, 40:48]
        gv_ss = stat[:, 48:56]
        gv_r = stat[:, 56:64]

        ld_tab, ld_mem, ld_wmkv, ld_small = (sem(n) for n in ("ld_tab", "ld_mem", "ld_wmkv", "ld_small"))
        ld_x = [sem(f"ld_x{t}") for t in range(TILES)]
        ld_win = [sem(f"ld_win{c}") for c in range(4)]
        ld_wout, ld_wc, ld_swa, ld_gating, ld_mcache, ld_wpq, ld_sk, ld_ffn, ld_fin = (
            sem(n) for n in ("ld_wout", "ld_wc", "ld_swa", "ld_gating", "ld_mcache", "ld_wpq", "ld_sk",
                             "ld_ffn", "ld_fin"))
        ld_rows, gT_done, gT_out = sem("ld_rows"), sem("gT_done"), sem("gT_out")
        stored = sem("stored")
        y_stored = [sem("y_stored0"), sem("y_stored1")]
        std_ready = sem("std_ready")
        xs_ready = sem("xs_ready")
        tr_done = sem("tr_done")
        xT_ready = sem("xT_ready")
        chain_v = sem("chain_v")
        chain_a = sem("chain_a")
        mkv_done, mkv_out, mkT_done, mkT_out = (sem(n) for n in ("mkv_done", "mkv_out", "mkT_done", "mkT_out"))
        pq_done, pkv_done, pgu_done, pgv_done = (sem(n) for n in ("pq_done", "pkv_done", "pgu_done", "pgv_done"))
        q_out, kv_out, gu_out, gv_out = (sem(n) for n in ("q_out", "kv_out", "gu_out", "gv_out"))
        w_masked, wT_done, wT_out = (sem(n) for n in ("w_masked", "wT_done", "wT_out"))
        qkT_done, qkT_out = sem("qkT_done"), sem("qkT_out")
        kcT_done, kcT_out, qTr_out = sem("kcT_done"), sem("kcT_out"), sem("qTr_out")
        sc_done, sc_max, sc_exp, pT_done, pT_out, pv_done, attn_out = (
            sem(n) for n in ("sc_done", "sc_max", "sc_exp", "pT_done", "pT_out", "pv_done", "attn_out"))
        so_exp, so_done = sem("so_exp"), sem("so_done")
        gv_ssq, gv_std, gvn_out, mixed_done, sgu_out = (
            sem(n) for n in ("gv_ssq", "gv_std", "gvn_out", "mixed_done", "sgu_out"))
        wo_done, x1_out = sem("wo_done"), sem("x1_out")
        qc_done, qc_out, kmT_done, kmT_out, qbd_out, qbd_zero = (
            sem(n) for n in ("qc_done", "qc_out", "kmT_done", "kmT_out", "qbd_out", "qbd_zero"))
        c_sc, c_max, c_exp, c_pT, c_pTo, c_pv, c_o, c_oT, c_oTo, c_wo, x2_out = (
            sem(n) for n in ("c_sc", "c_max", "c_exp", "c_pT", "c_pTo", "c_pv", "c_o", "c_oT", "c_oTo",
                             "c_wo", "x2_out"))
        c_sel, c_om = sem("c_sel"), sem("c_om")
        skT_done, skT_out = sem("skT_done"), sem("skT_out")
        xn_ready = sem("xn_ready")
        xcur_ready, xTcur_ready = sem("xcur_ready"), sem("xTcur_ready")
        pq_q, pq_qo, pq_t, pq_to, pq_s, pq_so = (sem(n) for n in ("pq_q", "pq_qo", "pq_t", "pq_to", "pq_s", "pq_so"))
        best_ready, gexp_ready, idx_ready = sem("best_ready"), sem("gexp_ready"), sem("idx_ready")
        u_landed = [sem(f"u_landed{i}") for i in range(RING)]
        v_landed = [sem(f"v_landed{i}") for i in range(RING)]
        u_used, v_used = sem("u_used"), sem("v_used")
        gelu_ready, coef_ready, diag_ready, acc_added = (
            sem(n) for n in ("gelu_ready", "coef_ready", "diag_ready", "acc_added"))
        apart_v, apart_p = sem("apart_v"), sem("apart_p")
        fin_std, fin_y = sem("fin_std"), sem("fin_y")

        block = ctx.enter_context(nc.Block())

        N_MIX, N_MRG, N_CRS, N_FFN = 2, 7, 12, 17
        G_MIX, G_MEM, G_MRG, G_CRS = range(4)
        STORES = []

        def chain_of(eng, s):
            state = [0, 0]

            def count(ins):
                ins.then_inc(s, 1)
                state[1] += 1

            def hold():
                eng.wait_ge(s, state[0] + state[1])

            def chain(ins):
                count(ins)
                hold()

            return chain, count, hold, state

        def run_blocks(eng, one):
            for b in range(5):
                one(b, b % 4, True, b >= 1)
            with eng.Fori(5, 30, 4) as b0:
                for j in range(4):
                    one(b0 + j, (5 + j) % 4, True, True)
            for b in range(33, BLOCKS + 1):
                one(b, b % 4, b < BLOCKS, True)

        def tile_head(b):
            return (b + 4) // 8, (b + 4) % 8

        @block.sync
        def _(sp):
            def load(dst, src, s):
                sp.dma_start(dst, src).then_inc(s, 16)

            def store(dst, src):
                STORES.append(1)
                sp.dma_start(dst, src).then_inc(stored, 16)

            load(mem_x, I["mem_prompt"][0].rearrange("(t p) d -> p t d", p=P), ld_mem)
            for name, dst in (("ident", ident), ("eps", eps), ("band", band), ("iota", iota),
                              ("headsel", headsel), ("gather", gather)):
                load(dst[:, :], I["tab_" + name][:, :], ld_tab)
            load(w_mk, I["w_mk"][0].rearrange("(k p) n -> p k n", p=P), ld_wmkv)
            load(w_mv, I["w_mv"][0].rearrange("(k p) n -> p k n", p=P), ld_wmkv)
            load(rot, v3(I["tab_rot"][:, :], TILES), ld_tab)
            for t in range(TILES):
                if t == 0:
                    flat = I["x_sample"].rearrange("a b d -> (a b) d")
                    load(xr(0)[0:NS], flat, ld_x[0])
                    load(xr(0)[NS:P], flat, ld_x[0])
                else:
                    load(xr(t), I["x_prompt"][0, (t - 1) * P:t * P, :], ld_x[t])
            win = I["w_in"][0].rearrange("(k p) n -> p k n", p=P)
            for c, (a, b) in enumerate(((0, 512), (512, 768), (768, 1280), (1280, 1792))):
                load(w_in[:, :, a:b], win[:, :, a:b], ld_win[c])
            load(w_out, I["w_out"][0].rearrange("(k p) n -> p k n", p=P), ld_wout)
            load(w_cq, I["w_cq"][0].rearrange("(k p) n -> p k n", p=P), ld_wc)
            load(w_co, I["w_co"][0].rearrange("(k p) n -> p k n", p=P), ld_wc)
            for name in ("k", "v"):
                store(O[f"swa_{name}_s"][0, :, 0:P - SAMPLE_LEN].rearrange("b w h d -> b (w h d)"),
                      I[f"cache_swa_{name}"][0, :, SAMPLE_LEN:P].rearrange("b w h d -> b (w h d)"))
            sp.wait_ge(mkv_out, 4)
            for j in range(2):
                store(O["mem_k"][0, 0, j * P:(j + 1) * P].rearrange("m h d -> m (h d)"), mk[:, j, :])
                store(O["mem_v"][0, 0, j * P:(j + 1) * P].rearrange("m h d -> m (h d)"), mv[:, j, :])
            sp.wait_ge(pgv_done, TILES)
            sp.wait_ge(kv_out, TILES)
            load(kc, I["cache_swa_k"][0].rearrange("b w h d -> w b (h d)"), ld_swa)
            load(vc, I["cache_swa_v"][0].rearrange("b w h d -> w b (h d)"), ld_swa)
            load(smask, v3(I["tab_smask"][:, :], 2), ld_swa)
            load(wsp, I["w_spatial"][0].rearrange("h t r -> t h r"), ld_gating)
            load(tril, I["tab_tril"][:, :], ld_gating)
            load(blocks, I["tab_blocks"][:, :], ld_gating)
            for c in range(2 * SAMPLES):
                load(w8[c * 8:(c + 1) * 8], I["w_spatial"][0, :, 0:8, 0:8].rearrange("h t r -> t h r"), ld_gating)
            for name, a in (("k", 512), ("v", 640)):
                store(O[f"swa_{name}_p"][0, 0].rearrange("w h d -> w (h d)"), proj(TILES - 1, a, a + P))
                for b in range(SAMPLES):
                    store(O[f"swa_{name}_s"][0, b, P - SAMPLE_LEN:P].rearrange("w h d -> w (h d)"),
                          proj(0, a, a + P)[b * 8:(b + 1) * 8])
            sp.wait_ge(gvn_out, 1)
            store(O["sgu_v"][0].rearrange("b t h d -> (b t) (h d)"), proj(0, 1280, 1792)[0:NS])
            sp.wait_ge(sgu_out, TILES)
            sp.wait_ge(attn_out, TILES)
            load(w_pq, I["w_peer_q"][0].rearrange("(k p) n -> p k n", p=P), ld_wpq)
            sp.wait_ge(xs_ready, N_CRS)
            sp.wait_ge(stored, 16 * len(STORES))
            for b in range(SAMPLES):
                load(kmem[:, b], I["cache_mem_k"][0, b].rearrange("(c p) h d -> p c (h d)", p=P), ld_mcache)
                load(vmem[:, b], I["cache_mem_v"][0, b].rearrange("(c p) h d -> p c (h d)", p=P), ld_mcache)
            sp.wait_ge(x2_out, TILES)
            load(g_ffn, I["g_ffn"][0:1, :].broadcast_to([P, D]), ld_ffn)
            load(fold, I["tab_fold"][:, :], ld_sk)
            load(sk_raw, I["peer_sub_keys"][0].rearrange("h c k d -> k (h c) d"), ld_sk)
            sp.wait_ge(u_used, 16 * BLOCKS)
            load(g_fin, I["g_final"].rearrange("(a d) -> a d", a=1).broadcast_to([P, D]), ld_fin)
            for t in range(TILES):
                sp.wait_ge(fin_y, t + 1)
                if t == 0:
                    dst, src = O["y_s"].rearrange("a b d -> (a b) d"), y_out[0][0:NS]
                else:
                    dst, src = O["y_p"][0, (t - 1) * P:t * P], y_out[t % 2]
                sp.dma_start(dst, src).then_inc(y_stored[t % 2], 16)
            sp.wait_ge(y_stored[0], 16 * 3)
            sp.wait_ge(y_stored[1], 16 * 2)

        @block.gpsimd
        def _(pool):
            def small(dst, src):
                pool.dma_start(dst, src).then_inc(ld_small, 16)

            for r, name in ((8 * G_MIX, "g_mix"), (8 * G_MEM, "g_mem"), (8 * G_MRG, "g_attn_out"),
                            (8 * G_MRG + 4, "g_gmlp_out"), (8 * G_CRS, "g_cross")):
                src = I[name][0].rearrange("(k p) -> k p", p=P)
                pool.dma_start(rows48[r:r + src.shape[0]], src).then_inc(ld_rows, 16)
            pool.dma_start(rows48[32:40], I["b_spatial"][0]).then_inc(ld_rows, 16)
            pool.dma_start(rows48[40:48].rearrange("h (c t) -> h c t", t=8),
                           I["b_spatial"][0, :, 0:8].unsqueeze(1).broadcast_to([HEADS, 16, 8])).then_inc(ld_rows, 16)
            small(g_sgu[:, :], I["g_sgu"].rearrange("a h d -> a (h d)").broadcast_to([P, 512]))
            small(sinks[:, :], I["attn_sinks"][0:1, :].broadcast_to([P, HEADS]))
            pool.wait_ge(x1_out, TILES)
            pool.memset(q_bd, 0.0).then_inc(qbd_zero, 1)

            def gathers(b, m, u, v):
                if u:
                    pool.wait_ge(idx_ready, b + 1)
                for k in range(TOPK):
                    i = k % RING
                    if u:
                        if k >= RING or not isinstance(b, int) or b > 0:
                            pool.wait_ge(u_used, b * TOPK + (k - RING + 1))
                        pool.sem_inc(apart_p, 1)
                        pool.indirect_dma_start(
                            u_ring[i], None, I["peer_u"][0],
                            bass.IndirectOffsetOnAxis(ap=idx[:, m, k:k + 1], axis=0)).then_inc(u_landed[i], 16)
                    if v:
                        if k >= RING or not isinstance(b, int) or b > 1:
                            pool.wait_ge(v_used, b * TOPK + (k - RING + 1 - TOPK))
                        pool.sem_inc(apart_p, 1)
                        pool.indirect_dma_start(
                            v_ring[i], None, I["peer_v"][0],
                            bass.IndirectOffsetOnAxis(ap=idx[:, (m + 3) % 4, k:k + 1], axis=0)).then_inc(v_landed[i], 16)

            pool.wait_ge(skT_out, 1)
            run_blocks(pool, gathers)

        @block.scalar
        def _(act):
            chain, count, hold, _ = chain_of(act, chain_a)

            def norm(n, src, parts=((0, D),)):
                if n >= 2:
                    act.wait_ge(tr_done, n - 1)
                for j, (a, b) in enumerate(parts):
                    ins = act.activation(xs[n % 2][:, a:b], src[j], ACT.Square, accum_out=ssq[n % 2][:, j:j + 1])
                    count(ins)
                hold()
                w = len(parts)
                act.activation(ssq[n % 2][:, 0:w], ssq[n % 2][:, 0:w], ACT.Sqrt, bias=eps[:, 0:1],
                               scale=1.0 / (parts[0][1] - parts[0][0])).then_inc(std_ready, 1)

            act.wait_ge(ld_mem, 16)
            act.wait_ge(ld_tab, 16 * 7)
            for j in range(2):
                norm(j, [mem_x[:, j, :]])
                if j == 0:
                    act.wait_ge(gT_done, 1)
                    act.activation(gains[:, :], bank(3)[:, 0:48], ACT.Copy).then_inc(gT_out, 1)
            for j in range(2):
                act.wait_ge(mkv_done, j + 1)
                act.activation(mk[:, j, :], bank(j)[:, 0:256], ACT.Copy).then_inc(mkv_out, 1)
                act.activation(mv[:, j, :], bank(j)[:, 256:512], ACT.Copy).then_inc(mkv_out, 1)

            def proj_out(t):
                act.wait_ge(pgu_done, t + 1)
                if t == 0:
                    act.wait_ge(stored, 16 * 6)
                act.activation(proj(t, 768, 1280), bank(2), ACT.Gelu).then_inc(gu_out, 1)
                act.wait_ge(pgv_done, t + 1)
                act.activation(proj(t, 1280, 1792), bank(3), ACT.Gelu).then_inc(gv_out, 1)

            for t in range(TILES):
                act.wait_ge(ld_x[t], 32 if t == 0 else 16)
                norm(N_MIX + t, [xr(t)])
                if t == 0:
                    act.wait_ge(mkT_done, 1)
                    act.activation(mkT[:, :, :], v3(bank(2), 2), ACT.Copy).then_inc(mkT_out, 1)
                else:
                    proj_out(t - 1)
            proj_out(TILES - 1)

            act.wait_ge(wT_done, 1)
            act.activation(wT_p, ps[:, 2048:3072].rearrange("p (h t) -> p h t", h=HEADS), ACT.Copy).then_inc(wT_out, 1)
            act.activation(wT_s, ps[:, 3072:4096].rearrange("p (h t) -> p h t", h=HEADS), ACT.Copy).then_inc(wT_out, 1)

            act.wait_ge(kcT_done, 1)
            act.activation(kcT, ps[:, 0:1024].rearrange("p (b k) -> p b k", b=SAMPLES), ACT.Copy).then_inc(kcT_out, 1)
            act.wait_ge(qkT_done, 1)
            act.activation(kT[:, 0:P], bank(5)[:, 0:P], ACT.Copy).then_inc(qkT_out, 1)
            act.activation(qT, v3(bank(4), 4), ACT.Copy).then_inc(qkT_out, 1)
            act.wait_ge(sc_max, 1)
            for j in range(4):
                act.activation(s_smp[:, j, :], s_smp[:, j, :], ACT.Exp, bias=nmx[:, j:j + 1],
                               accum_out=rs[:, j:j + 1])
            act.activation(es[:, 0:4], es[:, 0:4], ACT.Exp).then_inc(sc_exp, 1)
            act.wait_ge(pT_done, 1)
            act.activation(pTc, v3(bank(4), 4), ACT.Copy).then_inc(pT_out, 1)
            act.activation(pTn[0:NS], v3(bank(5), 4)[0:NS], ACT.Copy).then_inc(pT_out, 1)

            for i in range(4):
                act.wait_ge(qkT_done, i + 2)
                if i == 0:
                    act.wait_ge(qTr_out, 1)
                act.activation(kT[:, (i + 1) * P:(i + 2) * P], bank(5)[:, 0:P], ACT.Copy).then_inc(qkT_out, 1)
                act.activation(qT, v3(bank(4), 4), ACT.Copy).then_inc(qkT_out, 1)
                act.wait_ge(sc_max, i + 2)
                lo = P if i == 0 else 0
                for h in range(HEADS):
                    act.activation(s_sb[:, h, lo:], s_sb[:, h, lo:], ACT.Exp, bias=nmx[:, h:h + 1],
                                   accum_out=rs[:, h:h + 1])
                act.activation(es, es, ACT.Exp).then_inc(sc_exp, 1)
                act.wait_ge(pT_done, i + 2)
                act.activation(pT[:, 8:16, :], ps[:, 3072:4096].rearrange("p (a b) -> p a b", a=8), ACT.Copy)\
                   .then_inc(pT_out, 1)

            for t in range(TILES):
                act.wait_ge(gv_ssq, t + 1)
                act.activation(gv_ss, gv_ss, ACT.Sqrt, bias=eps[:, 0:1], scale=1.0 / HD).then_inc(gv_std, 1)
            for t in range(TILES):
                act.wait_ge(attn_out, t + 1)
                act.wait_ge(sgu_out, t + 1)
                norm(N_MRG + t, [proj(t, 0, 512), proj(t, 768, 1280)], ((0, 512), (512, 1024)))
            for t in range(TILES):
                act.wait_ge(x1_out, t + 1)
                norm(N_CRS + t, [xr(t)])

            for c in range(2):
                act.wait_ge(qc_done, c + 1)
                act.activation(qcT[:, c, 0:512], bank(2 * c), ACT.Copy).then_inc(qc_out, 1)
                act.activation(qcT[:, c, 512:640], bank(2 * c + 1)[:, 0:P], ACT.Copy).then_inc(qc_out, 1)
            for g in range(4):
                act.wait_ge(kmT_done, g + 1)
                act.activation(kmT[:, 2 * g:2 * g + 2], ps[:, (4 + 2 * (g % 2)) * 512:(6 + 2 * (g % 2)) * 512]
                               .rearrange("p (b c k) -> p b c k", b=2, c=2), ACT.Copy).then_inc(kmT_out, 1)
            for t in range(TILES):
                act.wait_ge(c_max, t + 1)
                if t == 0:
                    for bg in range(2):
                        act.activation(s_c[:, bg, :], bank(0)[:, bg * 256:(bg + 1) * 256], ACT.Exp,
                                       bias=nmx[:, bg:bg + 1], scale=0.125, accum_out=rs[:, bg:bg + 1])\
                           .then_inc(c_exp, 1)
                    act.wait_ge(c_pT, 1)
                    act.activation(pT_c[:, 0:4, :], v3(bank(2), 4), ACT.Copy).then_inc(c_pTo, 1)
                else:
                    for h in range(MHEADS):
                        act.activation(s_c[:, h, :], ps[:, h * 256:(h + 1) * 256], ACT.Exp,
                                       bias=nmx[:, h:h + 1], scale=0.125, accum_out=rs[:, h:h + 1])\
                           .then_inc(c_exp, 1)
                    act.wait_ge(c_pT, t + 1)
                    act.activation(pT_c[:, :, :], ps[:, 1024:2048].rearrange("p (a b) -> p a b", a=8),
                                   ACT.Copy).then_inc(c_pTo, 1)
                act.wait_ge(c_oT, t + 1)
                act.activation(oT_c, v3(bank(5)[:, 0:256], 2), ACT.Copy).then_inc(c_oTo, 1)
            for t in range(TILES):
                act.wait_ge(x2_out, t + 1)
                norm(N_FFN + t, [xr(t)])
                act.wait_ge(tr_done, N_FFN + t + 1)
                q = 4 + 2 * ((N_FFN + t) % 2)
                act.activation(xTv[:, :, t * P:(t + 1) * P],
                               ps[:, q * 512:(q + 2) * 512].rearrange("p (k t) -> p k t", k=KD), ACT.Copy)\
                   .then_inc(xT_ready, 1)
            act.wait_ge(skT_done, 1)
            act.activation(v3(skT, 4), v3(ps[:, 0:2048], 4), ACT.Copy).then_inc(skT_out, 1)
            act.wait_ge(xT_ready, N_FFN + TILES)
            act.wait_ge(xn_ready, TILES)

            def copy_xT(s):
                t = 0 if isinstance(s, int) and s < 4 else tile_head(s)[0]
                act.wait_ge(pq_q, s - 1) if not isinstance(s, int) or s > 1 else None
                src = xTv[:, :, t * P:(t + 1) * P] if isinstance(t, int) else xTv[:, :, bass.ds(t * P, P)]
                act.activation(xT_cur[cur(s)], src, ACT.Copy).then_inc(xTcur_ready, 1)

            cur_m = [0]

            def cur(s):
                return (s if isinstance(s, int) else cur_m[0]) % 2

            def queries_out(s, w):
                act.wait_ge(pq_q, s + 1)
                act.activation(q_sb[:, 0:w], bank(4)[:, 0:w], ACT.Copy).then_inc(pq_qo, 1)

            def queriesT_out(s, w):
                act.wait_ge(pq_t, s + 1)
                act.activation(qT_sb[:, 0:w // P, :], v3(bank(5)[:, 0:w], w // P), ACT.Copy).then_inc(pq_to, 1)

            def scores_out(s):
                act.wait_ge(pq_s, s + 1)
                if not isinstance(s, int) or s > 0:
                    act.wait_ge(best_ready, s)
                act.activation(ss, v3(bank(6)[:, 0:256], 2), ACT.Copy).then_inc(pq_so, 1)

            def gates(s, m):
                act.wait_ge(best_ready, s + 1)
                act.activation(gate[:, m, :], bestv, ACT.Exp, bias=negtop, accum_out=esum).then_inc(gexp_ready, 1)

            def copy_x(b):
                t = 0 if isinstance(b, int) and b < 4 else tile_head(b)[0]
                if not isinstance(b, int) or b > 1:
                    act.wait_ge(u_used, b * TOPK - TOPK)
                src = xn[:, t * D:(t + 1) * D] if isinstance(t, int) else xn[:, bass.ds(t * D, D)]
                act.activation(xn_cur[cur(b)], src, ACT.Copy).then_inc(xcur_ready, 1)

            for s in range(2):
                copy_xT(s)
                queries_out(s, 512)
                queriesT_out(s, 512)
                scores_out(s)
                gates(s, s)
            copy_x(0)

            def diagonals(b, k0, k1):
                base = fold if isinstance(b, int) and b <= 4 else ident[:, :]
                for k in range(k0, k1):
                    if k >= RING or not isinstance(b, int) or b > 1:
                        act.wait_ge(v_used, b * TOPK + (k - RING + 1 - TOPK))
                    act.activation(diag[:, k % RING, :], base, ACT.Copy,
                                   scale=coef[:, diag_m[0], k:k + 1]).then_inc(diag_ready, 1)

            diag_m = [0]

            def one(b, m, u, v):
                more = u and not (isinstance(b, int) and b + 2 >= BLOCKS)
                w = 512 if isinstance(b, int) and b + 2 < 4 else 256
                if more:
                    cur_m[0] = m + 2
                    copy_xT(b + 2)
                if u and not (isinstance(b, int) and b + 1 >= BLOCKS):
                    cur_m[0] = m + 1
                    copy_x(b + 1)
                diag_m[0] = (m + 1) % 2
                if v:
                    act.wait_ge(coef_ready, b)
                    diagonals(b, 0, 4)
                if more:
                    queries_out(b + 2, w)
                if v:
                    diagonals(b, 4, 8)
                if more:
                    queriesT_out(b + 2, w)
                if v:
                    diagonals(b, 8, 12)
                if more:
                    scores_out(b + 2)
                if v:
                    diagonals(b, 12, 16)
                if u:
                    act.wait_ge(u_used, b * TOPK + TOPK)
                    act.activation(hgelu[:, m % 2, :], hdot[:, m % 2, :], ACT.Gelu).then_inc(gelu_ready, 1)
                if more:
                    gates(b + 2, (m + 2) % 4)

            run_blocks(act, one)
            for t in range(TILES):
                if t >= 2:
                    act.wait_ge(y_stored[t % 2], 16 * (t // 2))
                act.wait_ge(acc_added, BLOCKS)
                act.wait_ge(ld_fin, 16)
                chain(act.activation(y_out[t % 2], xr(t), ACT.Square, accum_out=stat[:, 64 + t:65 + t]))
                act.activation(stat[:, 64 + t:65 + t], stat[:, 64 + t:65 + t], ACT.Sqrt, bias=eps[:, 0:1],
                               scale=1.0 / D).then_inc(fin_std, 1)

        @block.vector
        def _(dve):
            chain, _, _, steps = chain_of(dve, chain_v)

            def scale_rows(n, src, parts=((0, D),), gain=None):
                w = len(parts)
                dve.wait_ge(std_ready, n + 1)
                if n >= 2:
                    dve.wait_ge(tr_done, n - 1)
                chain(dve.reciprocal(rstd[n % 2][:, 0:w], ssq[n % 2][:, 0:w]))
                for j, (a, b) in enumerate(parts):
                    if gain is None:
                        ins = dve.tensor_scalar(xs[n % 2][:, a:b], src[j], rstd[n % 2][:, j:j + 1], None, ALU.mult)
                    else:
                        ins = dve.scalar_tensor_tensor(xs[n % 2][:, a:b], src[j], rstd[n % 2][:, j:j + 1],
                                                       gain, ALU.mult, ALU.mult)
                ins.then_inc(xs_ready, 1)

            def take_T(n, dst, g):
                dve.wait_ge(tr_done, n + 1)
                q = 4 + 2 * (n % 2)
                for j in range(2):
                    ins = dve.tensor_tensor(
                        dst[:, 4 * j:4 * j + 4], v3(bank(q + j), 4),
                        gains[:, g * KD + 4 * j:g * KD + 4 * j + 4].unsqueeze(2).broadcast_to([P, 4, P]), ALU.mult)
                ins.then_inc(xT_ready, 1)

            def tile_T(t):
                return xTv[:, :, t * P:(t + 1) * P]

            dve.wait_ge(ld_mem, 16)
            dve.wait_ge(ld_small, 32)
            dve.wait_ge(ld_tab, 16 * 7)
            for kv in range(KV):
                ins = dve.tensor_tensor(tmp[:, kv * 4:kv * 4 + 4], sinks[:, kv * 4:kv * 4 + 4], headsel[:, :], ALU.mult)
            chain(ins)
            chain(dve.tensor_reduce(sinks_s[:, :], v3(tmp[:, 0:8], 2), AX_X, ALU.add))
            dve.wait_ge(gT_out, 1)
            for j in range(2):
                scale_rows(j, [mem_x[:, j, :]])
                take_T(j, mem_T[:, :, j * P:(j + 1) * P], G_MEM)
            def rope(src, dst, t, n):
                r3 = src.rearrange("p (h d) -> p h d", d=HD)
                t3 = tmp[:, 0:n * HD].rearrange("p (h d) -> p h d", d=HD)
                half = HD // 2

                def ang(a, b):
                    return rot[:, t, a:b].unsqueeze(1).broadcast_to([P, n, b - a])

                dve.tensor_tensor(t3[:, :, 0:half], r3[:, :, half:HD], ang(HD, HD + half), ALU.mult)
                dve.tensor_tensor(t3[:, :, half:HD], r3[:, :, 0:half], ang(HD + half, 2 * HD), ALU.mult)
                ang_c = rot[:, t, 0:HD]
                if n == HEADS:
                    o = dst.rearrange("p (a j d) -> p j a d", j=2, d=HD)
                    for j in range(2):
                        ins = dve.tensor_tensor(o[:, j], r3[:, 4 * j:4 * j + 4],
                                                ang_c.unsqueeze(1).broadcast_to([P, 4, HD]), ALU.mult)
                    chain(ins)
                    for j in range(2):
                        ins = dve.tensor_tensor(o[:, j], o[:, j], t3[:, 4 * j:4 * j + 4], ALU.add)
                else:
                    o = dst.rearrange("p (h d) -> p h d", d=HD)
                    chain(dve.tensor_tensor(o, r3, ang_c.unsqueeze(1).broadcast_to([P, n, HD]), ALU.mult))
                    ins = dve.tensor_tensor(o, o, t3, ALU.add)
                return ins

            def mix_norm(t):
                dve.wait_ge(ld_x[t], 32 if t == 0 else 16)
                scale_rows(N_MIX + t, [xr(t)])
                take_T(N_MIX + t, tile_T(t), G_MIX)

            mix_norm(0)
            for t in range(TILES):
                if t + 1 < TILES:
                    mix_norm(t + 1)
                dve.wait_ge(pq_done, t + 1)
                if t == 0:
                    dve.wait_ge(mkT_done, 1)
                    dve.wait_ge(mkv_done, 2)
                ins = rope(bank(0), proj(t, 0, 512), t, HEADS)
                ins.then_inc(q_out, 1)
                dve.wait_ge(q_out, t + 1)
                dve.wait_ge(pkv_done, t + 1)
                chain(dve.tensor_copy(proj(t, 640, 768), bank(1)[:, P:2 * P]))
                ins = rope(bank(1)[:, 0:P], proj(t, 512, 640), t, KV)
                ins.then_inc(kv_out, 1)
                dve.wait_ge(kv_out, t + 1)

            dve.wait_ge(ld_gating, 16 * 19)
            dve.tensor_tensor(wsp, wsp, tril.unsqueeze(1).broadcast_to([P, HEADS, P]), ALU.mult)
            for h in range(HEADS):
                ins = dve.tensor_tensor(w_smp[:, h, :].rearrange("p (b r) -> p b r", b=16),
                                        blocks.rearrange("p (b r) -> p b r", b=16),
                                        w8[:, h, :].unsqueeze(1).broadcast_to([P, 16, 8]), ALU.mult)
            ins.then_inc(w_masked, 1)

            dve.wait_ge(qkT_out, 2)
            for bg in range(2):
                ins = dve.tensor_copy(qTr[:, bg, :].rearrange("p (b h i) -> p b h i", b=4, h=4),
                                      qT[:, :, bg * 32:(bg + 1) * 32].rearrange("p h (b i) -> p b h i", b=4))
            ins.then_inc(qTr_out, 1)
            dve.wait_ge(sc_done, 1)
            dve.wait_ge(ld_swa, 48)
            for j in range(4):
                ins = dve.scalar_tensor_tensor(s_smp[:, j, :], bank(j // 2)[:, (j % 2) * 192:(j % 2) * 192 + 192],
                                               0.125, smask[:, j % 2, :], ALU.mult, ALU.add)
            chain(ins)
            chain(dve.tensor_reduce(mx[:, 0:4], s_smp, AX_X, ALU.max))
            for kv in range(KV):
                ins = dve.tensor_tensor(mx[:, 2 * kv:2 * kv + 2], mx[:, 2 * kv:2 * kv + 2],
                                        sinks_s[:, kv:kv + 1].broadcast_to([P, 2]), ALU.max)
            chain(ins)
            chain(dve.tensor_scalar(nmx[:, 0:4], mx[:, 0:4], -1.0, None, ALU.mult))
            for kv in range(KV):
                ins = dve.tensor_tensor(es[:, 2 * kv:2 * kv + 2], nmx[:, 2 * kv:2 * kv + 2],
                                        sinks_s[:, kv:kv + 1].broadcast_to([P, 2]), ALU.add)
            ins.then_inc(sc_max, 1)
            dve.wait_ge(sc_exp, 1)
            chain(dve.tensor_tensor(rs[:, 0:4], rs[:, 0:4], es[:, 0:4], ALU.add))
            chain(dve.reciprocal(rden[:, 0:4], rs[:, 0:4]))
            dve.wait_ge(pv_done, 1)
            for j in range(4):
                for h in range(4):
                    ins = dve.tensor_scalar(o_exp[:, j, h * HD:(h + 1) * HD], bank(2)[:, j * HD:(j + 1) * HD],
                                            rden[:, j:j + 1], headsel[:, h:h + 1], ALU.mult, ALU.mult)
            ins.then_inc(so_exp, 1)
            dve.wait_ge(so_done, 1)
            dve.wait_ge(qkT_done, 1)
            dve.tensor_copy(proj(0, 0, 512), bank(3)).then_inc(attn_out, 1)

            for i in range(4):
                lo = P if i == 0 else 0
                dve.wait_ge(sc_done, i + 2)
                if i > 0:
                    dve.wait_ge(pT_done, i + 1)
                chain(dve.scalar_tensor_tensor(
                    s_sb[:, :, lo:], v3(ps[:, 0:2048], HEADS)[:, :, lo:], 0.125,
                    band[:, lo:].unsqueeze(1).broadcast_to([P, HEADS, 2 * P - lo]), ALU.mult, ALU.add))
                chain(dve.tensor_reduce(mx, s_sb[:, :, lo:], AX_X, ALU.max))
                chain(dve.tensor_tensor(mx, mx, sinks[:, :], ALU.max))
                chain(dve.tensor_scalar(nmx, mx, -1.0, None, ALU.mult))
                dve.tensor_tensor(es, nmx, sinks[:, :], ALU.add).then_inc(sc_max, 1)
                dve.wait_ge(pT_done, i + 2)
                dve.tensor_copy(pT[:, 0:8, :], ps[:, 2048:3072].rearrange("p (a b) -> p a b", a=8)).then_inc(pT_out, 1)
                dve.wait_ge(sc_exp, i + 2)
                chain(dve.tensor_tensor(rs, rs, es, ALU.add))
                chain(dve.reciprocal(rden, rs))
                dve.wait_ge(pv_done, i + 2)
                dve.tensor_tensor(proj(i + 1, 0, 512).rearrange("p (h d) -> p h d", d=HD),
                                  v3(bank(0), HEADS), rden.unsqueeze(2).broadcast_to([P, HEADS, HD]), ALU.mult)\
                   .then_inc(attn_out, 1)

            for t in range(TILES):
                gv = proj(t, 1280, 1792).rearrange("p (h d) -> p h d", d=HD)
                t3 = tmp.rearrange("p (h d) -> p h d", d=HD)
                dve.wait_ge(gv_out, t + 1)
                if t > 0:
                    dve.wait_ge(sgu_out, t)
                chain(dve.tensor_tensor(t3, gv, gv, ALU.mult))
                dve.tensor_reduce(gv_ss, t3, AX_X, ALU.add).then_inc(gv_ssq, 1)
                dve.wait_ge(gv_std, t + 1)
                chain(dve.reciprocal(gv_r, gv_ss))
                chain(dve.tensor_tensor(gv, gv, gv_r.unsqueeze(2).broadcast_to([P, HEADS, HD]), ALU.mult))
                dve.tensor_tensor(proj(t, 1280, 1792), proj(t, 1280, 1792), g_sgu[:, :], ALU.mult).then_inc(gvn_out, 1)
                dve.wait_ge(mixed_done, t + 1)
                bias = bias_s if t == 0 else bias_p
                chain(dve.tensor_tensor(t3, v3(bank(1 + t % 2), HEADS), bias.unsqueeze(2).broadcast_to([P, HEADS, HD]),
                                        ALU.add))
                dve.wait_ge(gu_out, t + 1)
                dve.tensor_tensor(proj(t, 768, 1280), proj(t, 768, 1280), tmp, ALU.mult).then_inc(sgu_out, 1)

            def add_out(n, q, done, out):
                dve.wait_ge(done, n + 1)
                dve.tensor_tensor(xr(n), xr(n), ps[:, q * 512:(q + 2) * 512], ALU.add).then_inc(out, 1)

            dve.wait_ge(attn_out, TILES)
            dve.wait_ge(sgu_out, TILES)
            for t in range(TILES):
                scale_rows(N_MRG + t, [proj(t, 0, 512), proj(t, 768, 1280)], ((0, 512), (512, 1024)))
                take_T(N_MRG + t, tile_T(t), G_MRG)
            for t in range(TILES):
                add_out(t, 2 * (t % 2), wo_done, x1_out)
            dve.wait_ge(x1_out, TILES)
            for t in range(TILES):
                dve.wait_ge(wo_done, t + 1)
                scale_rows(N_CRS + t, [xr(t)])
                take_T(N_CRS + t, tile_T(t), G_CRS)

            dve.wait_ge(qc_out, 4)
            dve.wait_ge(qbd_zero, 1)
            for c in range(2):
                for j in range(2):
                    h = 2 * c + j
                    ins = dve.tensor_copy(
                        q_bd[64 * j:64 * j + 64, c, :].rearrange("p (b h i) -> p b h i", b=8, h=4)[:, :, h, :],
                        qcT[64 * j:64 * j + 64, c, 0:NS].rearrange("p (b i) -> p b i", b=8))
            ins.then_inc(qbd_out, 1)
            for t in range(TILES):
                w = 2 if t == 0 else MHEADS
                dve.wait_ge(c_sc, t + 1)
                chain(dve.tensor_reduce(mx[:, 0:w], v3(ps[:, 0:w * 256], w), AX_X, ALU.max))
                dve.tensor_scalar(nmx[:, 0:w], mx[:, 0:w], -0.125, None, ALU.mult).then_inc(c_max, 1)
                dve.wait_ge(c_exp, 2 if t == 0 else 2 + 4 * t)
                chain(dve.reciprocal(rden[:, 0:w], rs[:, 0:w]))
                dve.wait_ge(c_pv, t + 1)
                if t == 0:
                    for bg in range(2):
                        for h in range(MHEADS):
                            ins = dve.tensor_scalar(o_m[:, bg, h * HD:(h + 1) * HD],
                                                    bank(4)[:, bg * 256 + h * HD:bg * 256 + (h + 1) * HD],
                                                    rden[:, bg:bg + 1], headsel[:, h:h + 1], ALU.mult, ALU.mult)
                    ins.then_inc(c_om, 1)
                    dve.wait_ge(c_sel, 1)
                    dve.tensor_copy(o_c, bank(5)[:, 256:512]).then_inc(c_o, 1)
                else:
                    for j in range(2):
                        ins = dve.tensor_tensor(o_c.rearrange("p (c j d) -> p j c d", j=2, d=HD)[:, j],
                                                v3(bank(4)[:, j * P:(j + 1) * P], 2),
                                                rden[:, 2 * j:2 * j + 2].unsqueeze(2).broadcast_to([P, 2, HD]),
                                                ALU.mult)
                    ins.then_inc(c_o, 1)
                add_out(t, 6, c_wo, x2_out)
            dve.wait_ge(x2_out, TILES)
            dve.wait_ge(ld_ffn, 16)
            for t in range(TILES):
                n = N_FFN + t
                scale_rows(n, [xr(t)], gain=g_ffn)
                dve.wait_ge(xs_ready, n + 1)
                dve.tensor_copy(xn[:, t * D:(t + 1) * D], xs[n % 2]).then_inc(xn_ready, 1)

            def apart():
                dve.sem_inc(apart_v, 1)

            def top16(values, vals, inds, rest):
                apart()
                chain(dve.max(vals[:, 0:8], values))
                apart()
                dve.max_index(inds[:, 0:8], vals[:, 0:8], values)
                chain(dve.match_replace(rest, vals[:, 0:8], values, LOWEST))
                apart()
                chain(dve.max(vals[:, 8:16], rest))
                apart()
                return dve.max_index(inds[:, 8:16], vals[:, 8:16], rest)

            def choose(s, m):
                dve.wait_ge(pq_so, s + 1)
                if not isinstance(s, int) or s > 0:
                    dve.wait_ge(gexp_ready, s)
                for c in range(2):
                    chain(top16(ss[:, c, :], topv[:, c, :], topi[:, c, :], ss2[:, c, :]))
                c3 = cand.rearrange("p (a b) -> p a b", a=TOPK)
                chain(dve.tensor_tensor(c3, topv[:, 0, :].unsqueeze(2).broadcast_to([P, TOPK, TOPK]),
                                        topv[:, 1, :].unsqueeze(1).broadcast_to([P, TOPK, TOPK]), ALU.add))
                chain(top16(cand, bestv, besti, cand2))
                dve.tensor_scalar(negtop, bestv[:, 0:1], -1.0, None, ALU.mult).then_inc(best_ready, 1)
                dve.tensor_scalar(parts[:, 0, :], besti, 4, None, ALU.logical_shift_right)
                chain(dve.tensor_scalar(parts[:, 1, :], besti, 15, None, ALU.bitwise_and))
                hot = onehot.rearrange("p (a b) -> p a b", b=TOPK)
                chain(dve.tensor_tensor(hot, parts.rearrange("p c k -> p (c k)").unsqueeze(2)
                                        .broadcast_to([P, 2 * TOPK, TOPK]),
                                        iota[:, :].unsqueeze(1).broadcast_to([P, 2 * TOPK, TOPK]), ALU.is_equal))
                hot4 = onehot.rearrange("p (c a b) -> p c a b", c=2, b=TOPK)
                for c in range(2):
                    ins = dve.tensor_tensor(hot4[:, c], hot4[:, c],
                                            topi[:, c, :].unsqueeze(1).broadcast_to([P, TOPK, TOPK]), ALU.mult)
                chain(ins)
                chain(dve.tensor_reduce(chosen.rearrange("p c k -> p (c k)"), hot, AX_X, ALU.add))
                if not isinstance(s, int) or s >= 4:
                    dve.wait_ge(v_landed[3], 64 * (s - 3))
                dve.scalar_tensor_tensor(idx[:, m, :], chosen[:, 0, :], float(NKEYS), chosen[:, 1, :],
                                         ALU.mult, ALU.add).then_inc(idx_ready, 1)

            dve.wait_ge(xn_ready, TILES)

            def finish_gates(s, m):
                dve.wait_ge(gexp_ready, s + 1)
                chain(dve.reciprocal(rsum, esum))
                chain(dve.tensor_scalar(gate[:, m, :], gate[:, m, :], rsum, None, ALU.mult))

            for s in range(2):
                choose(s, s)
                finish_gates(s, s)

            def add_acc(b, m):
                s = b - 2
                dve.wait_ge(v_used, s * TOPK + TOPK)
                t = 0 if isinstance(s, int) and s < 4 else tile_head(s)[0]
                q = 2 * (m % 2)
                ins = dve.tensor_tensor(xr(t), xr(t), ps[:, q * 512:(q + 2) * 512], ALU.add)
                ins.then_inc(acc_added, 1)

            def one(b, m, u, v):
                more = u and not (isinstance(b, int) and b + 2 >= BLOCKS)
                if u:
                    dve.wait_ge(xcur_ready, b + 1)
                    for k in range(TOPK):
                        dve.wait_ge(u_landed[k % RING], b * 64 + 16 * (k // RING + 1))
                        dve.tensor_tensor_reduce(u_ring[k % RING], u_ring[k % RING], xn_cur[m % 2], 1.0, 0.0, ALU.mult,
                                                 ALU.add, hdot[:, m % 2, k:k + 1]).then_inc(u_used, 1)
                if not isinstance(b, int) or b >= 2:
                    if not isinstance(b, int) or b >= 3:
                        dve.wait_ge(acc_added, b - 2)
                    add_acc(b, m)
                if more:
                    choose(b + 2, (m + 2) % 4)
                if u:
                    dve.wait_ge(gelu_ready, b + 1)
                    dve.tensor_tensor(coef[:, m % 2, :], hgelu[:, m % 2, :], gate[:, m, :], ALU.mult)\
                       .then_inc(coef_ready, 1)
                if more:
                    finish_gates(b + 2, (m + 2) % 4)

            for b in range(5):
                one(b, b % 4, True, b >= 1)
            start, steps[1] = steps[1], 0
            with dve.Fori(5, 30, 4) as b0:
                steps[0] = b0 * CHAIN_PER_BLOCK + (start - 5 * CHAIN_PER_BLOCK)
                for j in range(4):
                    one(b0 + j, (5 + j) % 4, True, True)
                assert steps[1] == 4 * CHAIN_PER_BLOCK, steps
            steps[:] = [0, start + 28 * CHAIN_PER_BLOCK]
            for b in range(33, BLOCKS + 1):
                one(b, b % 4, b < BLOCKS, True)
            dve.wait_ge(acc_added, BLOCKS - 1)
            add_acc(BLOCKS + 1, (BLOCKS + 1) % 4)
            dve.wait_ge(acc_added, BLOCKS)
            dve.wait_ge(ld_fin, 16)
            for t in range(TILES):
                dve.wait_ge(fin_std, t + 1)
                c = stat[:, 72 + t:73 + t]
                chain(dve.reciprocal(c, stat[:, 64 + t:65 + t]))
                dve.scalar_tensor_tensor(y_out[t % 2], xr(t), c, g_fin, ALU.mult, ALU.mult).then_inc(fin_y, 1)

        @block.tensor
        def _(pe):
            def transposes(n):
                pe.wait_ge(xs_ready, n + 1)
                if n >= 2:
                    pe.wait_ge(xT_ready, n - 1)
                q = 4 + 2 * (n % 2)
                for k in range(KD):
                    ins = pe.transpose(bank(q + k // 4)[:, (k % 4) * P:(k % 4 + 1) * P],
                                       xs[n % 2][:, k * P:(k + 1) * P], ident[:, :])
                ins.then_inc(tr_done, 1)

            def product(out, lhs, rhs, n=KD):
                for k in range(n):
                    ins = pe.matmul(out, lhs(k), rhs(k), start=(k == 0), stop=(k == n - 1))
                return ins

            pe.wait_ge(ld_tab, 16 * 7)
            pe.wait_ge(ld_rows, 16 * 7)
            pe.transpose(bank(3)[:, 0:48], rows48, ident[0:48, 0:48]).then_inc(gT_done, 1)
            for j in range(2):
                transposes(j)
                pe.wait_ge(xT_ready, j + 1)
                if j == 0:
                    pe.wait_ge(ld_wmkv, 32)
                product(bank(j)[:, 0:256], lambda k: mem_T[:, k, j * P:(j + 1) * P], lambda k: w_mk[:, k, :])
                product(bank(j)[:, 256:512], lambda k: mem_T[:, k, j * P:(j + 1) * P], lambda k: w_mv[:, k, :]).then_inc(mkv_done, 1)
            transposes(N_MIX)
            for t in range(TILES):
                if t == 0:
                    pe.wait_ge(mkv_out, 4)
                    for c in range(2):
                        for j in range(2):
                            ins = pe.transpose(bank(2)[:, c * 256 + j * P:c * 256 + (j + 1) * P],
                                               mk[:, j, c * P:(c + 1) * P], ident[:, :])
                    ins.then_inc(mkT_done, 1)
                    pe.wait_ge(mkT_out, 1)
                if t + 1 < TILES:
                    transposes(N_MIX + t + 1)
                pe.wait_ge(xT_ready, N_MIX + t + 1)
                for c, (a, b, done, out) in enumerate(((0, 512, pq_done, q_out), (512, 768, pkv_done, kv_out),
                                                       (768, 1280, pgu_done, gu_out), (1280, 1792, pgv_done, gv_out))):
                    if t == 0:
                        pe.wait_ge(ld_win[c], 16)
                    else:
                        pe.wait_ge(out, t)
                    product(bank(c)[:, 0:b - a], lambda k: xTv[:, k, t * P:(t + 1) * P],
                            lambda k: w_in[:, k, a:b]).then_inc(done, 1)

            pe.wait_ge(w_masked, 1)
            for n, w in enumerate((wsp, w_smp)):
                for h in range(HEADS):
                    ins = pe.transpose(ps[:, 2048 + n * 1024 + h * P:2048 + n * 1024 + (h + 1) * P], w[:, h, :],
                                       ident[:, :])
            ins.then_inc(wT_done, 1)

            pe.wait_ge(ld_swa, 48)
            pe.wait_ge(kv_out, TILES)
            pe.wait_ge(q_out, TILES)
            for b in range(SAMPLES):
                ins = pe.transpose(ps[:, b * P:(b + 1) * P], kc[:, b, :], ident[:, :])
            ins.then_inc(kcT_done, 1)

            def heads_T(t):
                for a in range(4):
                    pe.transpose(bank(4)[:, a * P:(a + 1) * P], proj(t, a * P, (a + 1) * P), ident[:, :])
                pe.transpose(bank(5)[:, 0:P], proj(t, 512, 640), ident[:, :]).then_inc(qkT_done, 1)

            pe.wait_ge(wT_out, 2)
            heads_T(0)
            pe.wait_ge(kcT_out, 1)
            pe.wait_ge(qTr_out, 1)
            for j in range(4):
                kv, bg = j // 2, j % 2
                rows = slice(64 * kv, 64 * kv + 64)
                o = bank(j // 2)[:, (j % 2) * 192:(j % 2) * 192 + 192]
                ins = pe.matmul(o[:, P:P + NS], qTr[rows, bg, :], kT[rows, 0:NS], start=True, stop=True)
                for s in range(4):
                    ins = pe.matmul(o[32 * s:32 * s + 32, 0:P], qTr[rows, bg, 32 * s:32 * s + 32],
                                    kcT[rows, bg * 4 + s, :], start=True, stop=True)
            ins.then_inc(sc_done, 1)
            pe.wait_ge(sc_exp, 1)
            for j in range(4):
                pe.transpose(bank(4)[:, j * P:(j + 1) * P], s_smp[:, j, 0:P], ident[:, :])
                ins = pe.transpose(bank(5)[0:NS, j * P:(j + 1) * P], s_smp[:, j, P:P + NS], ident[:, :])
            ins.then_inc(pT_done, 1)
            pe.wait_ge(pT_out, 2)
            pe.wait_ge(gu_out, TILES)
            pe.wait_ge(gv_out, TILES)
            for j in range(4):
                kv, bg = j // 2, j % 2
                o = bank(2)[:, j * HD:(j + 1) * HD]
                pe.matmul(o, pTn[0:NS, j, :], proj(0, 640 + kv * HD, 640 + (kv + 1) * HD)[0:NS],
                          start=True, stop=False, skip_group_check=True)
                for s in range(4):
                    ins = pe.matmul(o[32 * s:32 * s + 32], pTc[:, j, 32 * s:32 * s + 32],
                                    vc[:, bg * 4 + s, kv * HD:(kv + 1) * HD], start=False, stop=(s == 3),
                                    skip_group_check=True)
            ins.then_inc(pv_done, 1)
            pe.wait_ge(so_exp, 1)
            for kv in range(KV):
                for bg in range(2):
                    ins = pe.matmul(bank(3)[:, kv * 256:(kv + 1) * 256], v3(gather[:, :], 2)[:, bg, :],
                                    o_exp[:, kv * 2 + bg, :], start=(bg == 0), stop=(bg == 1))
            ins.then_inc(so_done, 1)

            for i in range(4):
                t = i + 1
                lo = P if i == 0 else 0
                heads_T(t)
                pe.wait_ge(qkT_out, 2 * i + 4)
                if i == 0:
                    pe.wait_ge(attn_out, 1)
                else:
                    pe.wait_ge(attn_out, i + 1)
                for h in range(HEADS):
                    rows = slice(64 * (h // 4), 64 * (h // 4) + 64)
                    ins = pe.matmul(ps[:, h * 256 + lo:(h + 1) * 256], qT[rows, h % 4, :],
                                    kT[rows, (t - 1) * P + lo:(t + 1) * P], start=True, stop=True)
                ins.then_inc(sc_done, 1)
                pe.wait_ge(sc_exp, i + 2)
                for h in range(HEADS):
                    for c in range(2):
                        if c * P >= lo:
                            ins = pe.transpose(ps[:, 2048 + (c * 8 + h) * P:2048 + (c * 8 + h + 1) * P],
                                               s_sb[:, h, c * P:(c + 1) * P], ident[:, :])
                        elif i == 0 and h == 0:
                            for g in range(8):
                                ins = pe.transpose(ps[:, 2048 + g * P:2048 + (g + 1) * P], ident[:, :], ident[:, :])
                ins.then_inc(pT_done, 1)
                pe.wait_ge(pT_out, 2 + 2 * (i + 1))
                for h in range(HEADS):
                    kv = h // 4
                    for c in range(2):
                        if c * P < lo:
                            continue
                        vt = t - 1 + c
                        ins = pe.matmul(bank(0)[:, h * HD:(h + 1) * HD], pT[:, c * 8 + h, :],
                                        proj(vt, 640 + kv * HD, 640 + (kv + 1) * HD),
                                        start=(c * P == lo), stop=(c == 1))
                ins.then_inc(pv_done, 1)

            for t in range(TILES):
                pe.wait_ge(gvn_out, t + 1)
                if t >= 2:
                    pe.wait_ge(sgu_out, t - 1)
                for h in range(HEADS):
                    ins = pe.matmul(bank(1 + t % 2)[:, h * HD:(h + 1) * HD], (wT_s if t == 0 else wT_p)[:, h, :],
                                    proj(t, 1280 + h * HD, 1280 + (h + 1) * HD), start=True, stop=True)
                ins.then_inc(mixed_done, 1)

            pe.wait_ge(ld_wout, 16)
            for t in range(TILES):
                transposes(N_MRG + t)
            pe.wait_ge(attn_out, TILES)
            for t in range(TILES):
                pe.wait_ge(xT_ready, N_MRG + t + 1)
                if t >= 2:
                    pe.wait_ge(x1_out, t - 1)
                else:
                    pe.wait_ge(sgu_out, TILES)
                for c in range(2):
                    ins = product(bank(2 * (t % 2) + c), lambda k: xTv[:, k, t * P:(t + 1) * P],
                                  lambda k: w_out[:, k, c * 512:(c + 1) * 512])
                ins.then_inc(wo_done, 1)
            for t in range(TILES):
                transposes(N_CRS + t)

            pe.wait_ge(ld_wc, 32)
            pe.wait_ge(xT_ready, N_CRS + TILES)
            for c in range(2):
                product(bank(2 * c), lambda k: w_cq[:, k, c * P:(c + 1) * P], lambda k: xTv[:, k, 0:512])
                product(bank(2 * c + 1)[:, 0:P], lambda k: w_cq[:, k, c * P:(c + 1) * P],
                        lambda k: xTv[:, k, 512:640]).then_inc(qc_done, 1)
            pe.wait_ge(ld_mcache, 16 * 16)
            for g in range(4):
                if g >= 2:
                    pe.wait_ge(kmT_out, g - 1)
                for b in range(2):
                    for c in range(2):
                        for j in range(2):
                            o = (4 + 2 * (g % 2)) * 512 + (b * 2 + c) * 256 + j * P
                            ins = pe.transpose(ps[:, o:o + P], kmem[:, 2 * g + b, j, c * P:(c + 1) * P], ident[:, :])
                ins.then_inc(kmT_done, 1)
            for t in range(TILES):
                if t == 0:
                    pe.wait_ge(qc_out, 4)
                    pe.wait_ge(qbd_out, 1)
                    pe.wait_ge(kmT_out, 4)
                    for b in range(SAMPLES):
                        for c in range(2):
                            ins = pe.matmul(bank(0)[32 * (b % 4):32 * (b % 4) + 32, (b // 4) * 256:(b // 4 + 1) * 256],
                                            q_bd[:, c, b * 32:(b + 1) * 32], kmT[:, b, c, :], start=(c == 0),
                                            stop=(c == 1))
                    ins.then_inc(c_sc, 1)
                    pe.wait_ge(c_exp, 2)
                    for bg in range(2):
                        for c in range(2):
                            ins = pe.transpose(bank(2)[:, (bg * 2 + c) * P:(bg * 2 + c + 1) * P],
                                               s_c[:, bg, c * P:(c + 1) * P], ident[:, :])
                    ins.then_inc(c_pT, 1)
                    pe.wait_ge(c_pTo, 1)
                    for b in range(SAMPLES):
                        r = 32 * (b % 4)
                        for c in range(2):
                            ins = pe.matmul(bank(4)[r:r + 32, (b // 4) * 256:(b // 4 + 1) * 256],
                                            pT_c[:, (b // 4) * 2 + c, r:r + 32], vmem[:, b, c, :], start=(c == 0),
                                            stop=(c == 1))
                    ins.then_inc(c_pv, 1)
                    pe.wait_ge(c_om, 1)
                    for bg in range(2):
                        ins = pe.matmul(bank(5)[:, 256:512], v3(gather[:, :], 2)[:, bg, :], o_m[:, bg, :],
                                        start=(bg == 0), stop=(bg == 1))
                    ins.then_inc(c_sel, 1)
                else:
                    for j in range(2):
                        for c in range(2):
                            rows = slice(64 * j, 64 * j + 64)
                            ins = pe.matmul(ps[:, (2 * j + c) * 256:(2 * j + c + 1) * 256],
                                            qcT[rows, c, t * P:(t + 1) * P], mkT[rows, c, :], start=True, stop=True)
                    ins.then_inc(c_sc, 1)
                    pe.wait_ge(c_exp, 2 + 4 * t)
                    for h in range(MHEADS):
                        for c in range(2):
                            ins = pe.transpose(ps[:, 1024 + (h * 2 + c) * P:1024 + (h * 2 + c + 1) * P],
                                               s_c[:, h, c * P:(c + 1) * P], ident[:, :])
                    ins.then_inc(c_pT, 1)
                    pe.wait_ge(c_pTo, t + 1)
                    for n in range(MHEADS):
                        h = 2 * (n % 2) + n // 2
                        for c in range(2):
                            ins = pe.matmul(bank(4)[:, n * HD:(n + 1) * HD], pT_c[:, n * 2 + c, :],
                                            mv[:, c, h * HD:(h + 1) * HD], start=(c == 0), stop=(c == 1))
                    ins.then_inc(c_pv, 1)
                pe.wait_ge(c_o, t + 1)
                for c in range(2):
                    ins = pe.transpose(bank(5)[:, c * P:(c + 1) * P], o_c[:, c * P:(c + 1) * P], ident[:, :])
                ins.then_inc(c_oT, 1)
                pe.wait_ge(c_oTo, t + 1)
                if t > 0:
                    pe.wait_ge(x2_out, t)
                for c in range(2):
                    ins = product(bank(6 + c), lambda k: oT_c[:, k, :], lambda k: w_co[:, k, c * 512:(c + 1) * 512], 2)
                ins.then_inc(c_wo, 1)
            pe.wait_ge(x2_out, TILES)
            for t in range(TILES):
                transposes(N_FFN + t)
            pe.wait_ge(ld_sk, 32)
            for n in range(16):
                ins = pe.transpose(ps[:, n * P:(n + 1) * P], sk_raw[:, n, :], ident[:, :])
            ins.then_inc(skT_done, 1)

            pe.wait_ge(ld_wpq, 16)
            pe.wait_ge(skT_out, 1)

            def heads_of(s):
                return (s, s + 4) if isinstance(s, int) and s < 4 else (tile_head(s)[1],)

            def q_mm(s, m):
                pe.wait_ge(xTcur_ready, s + 1)
                if not isinstance(s, int) or s > 0:
                    pe.wait_ge(pq_qo, s)
                for j, h in enumerate(heads_of(s)):
                    for k in range(KD):
                        rhs = w_pq[:, k, h * 256:(h + 1) * 256] if isinstance(h, int) else w_pq[:, k, bass.ds(h * 256, 256)]
                        ins = pe.matmul(bank(4)[:, j * 256:(j + 1) * 256], xT_cur[m % 2][:, k, :], rhs,
                                        start=(k == 0), stop=(k == KD - 1))
                ins.then_inc(pq_q, 1)

            def q_T(s):
                pe.wait_ge(pq_qo, s + 1)
                if not isinstance(s, int) or s > 0:
                    pe.wait_ge(pq_to, s)
                for j in range(2 * len(heads_of(s))):
                    ins = pe.transpose(bank(5)[:, j * P:(j + 1) * P], q_sb[:, j * P:(j + 1) * P], ident[:, :])
                ins.then_inc(pq_t, 1)

            def scores(s):
                pe.wait_ge(pq_to, s + 1)
                if not isinstance(s, int) or s > 0:
                    pe.wait_ge(pq_so, s)
                hs = heads_of(s)
                for j, h in enumerate(hs):
                    r = slice(0, P) if len(hs) == 1 else slice(j * NS, (j + 1) * NS)
                    for c in range(2):
                        rhs = (skT[:, (2 * h + c) * P:(2 * h + c + 1) * P] if isinstance(h, int)
                               else skT[:, bass.ds(h * 256 + c * P, P)])
                        ins = pe.matmul(bank(6)[r, c * P:(c + 1) * P], qT_sb[:, 2 * j + c, r], rhs, start=True, stop=True)
                ins.then_inc(pq_s, 1)

            for s in range(2):
                q_mm(s, s)
                q_T(s)
                scores(s)

            def experts(b, m, k0, k1):
                q = 2 * ((m + 1) % 2)
                if k0 == 0 and (not isinstance(b, int) or b >= 3):
                    pe.wait_ge(acc_added, b - 2)
                for k in range(k0, k1):
                    pe.wait_ge(diag_ready, b * TOPK + (k + 1 - TOPK))
                    pe.wait_ge(v_landed[k % RING], b * 64 + 16 * (k // RING + 1) - 64)
                    for c in range(2):
                        ins = pe.matmul(bank(q + c), diag[:, k % RING, :], v_ring[k % RING][:, c * 512:(c + 1) * 512],
                                        start=(k == 0), stop=(k == TOPK - 1))
                    ins.then_inc(v_used, 1)

            def one(b, m, u, v):
                more = u and not (isinstance(b, int) and b + 2 >= BLOCKS)
                if more:
                    q_mm(b + 2, m + 2)
                if v:
                    experts(b, m, 0, 4)
                if more:
                    q_T(b + 2)
                if v:
                    experts(b, m, 4, 8)
                if more:
                    scores(b + 2)
                if v:
                    experts(b, m, 8, 16)

            run_blocks(pe, one)


CHAIN_PER_BLOCK = 19

_INS = ['x_prompt', 'x_sample', 'mem_prompt', 'cache_swa_k', 'cache_swa_v', 'cache_mem_k', 'cache_mem_v',
        'g_mix', 'w_in', 'attn_sinks', 'g_sgu', 'w_spatial', 'b_spatial', 'g_attn_out', 'g_gmlp_out', 'w_out',
        'g_cross', 'g_mem', 'w_cq', 'w_mk', 'w_mv', 'w_co', 'g_ffn', 'w_peer_q', 'peer_sub_keys', 'peer_u',
        'peer_v', 'g_final']
_OUTS = {"y_p": (1, 512, D), "y_s": (8, 8, D), "swa_k_p": (1, 1, P, KV, HD), "swa_v_p": (1, 1, P, KV, HD),
         "mem_k": (1, 1, NMEM, MHEADS, HD), "mem_v": (1, 1, NMEM, MHEADS, HD),
         "swa_k_s": (1, 8, P, KV, HD), "swa_v_s": (1, 8, P, KV, HD), "sgu_v": (1, 8, 8, HEADS, HD)}


def kernel(**inputs):
    import concourse.bacc as _bacc
    from concourse.bass_utils import run_bass_kernel_spmd as _run

    nc = _bacc.Bacc("TRN2", target_bir_lowering=False, num_devices=1)
    arrays, I, O = {}, {}, {}
    for name in _INS:
        a = np.ascontiguousarray(inputs[name])
        arrays[f"in_{name}"] = a
        I[name] = nc.dram_tensor(f"in_{name}", a.shape, F32, kind="ExternalInput").ap()
    for name, a in shape_tables().items():
        arrays[f"tab_{name}"] = a
        I["tab_" + name] = nc.dram_tensor(f"tab_{name}", a.shape, F32, kind="ExternalInput").ap()
    for name, shape in _OUTS.items():
        O[name] = nc.dram_tensor(f"out_{name}", shape, F32, kind="ExternalOutput").ap()
    hybrid_step(nc, I, O)
    r = _run(nc, [arrays], core_ids=[0])
    return tuple(r.results[0][f"out_{name}"] for name in _OUTS)
```

```python
from contextlib import ExitStack

import numpy as np

import concourse.bass as bass
from concourse import mybir

F32 = mybir.dt.float32
BF16 = mybir.dt.bfloat16
U32 = mybir.dt.uint32
ALU = mybir.AluOpType
ACT = mybir.ActivationFunctionType
AX_X = mybir.AxisListType.X

P = 128
D = 1024
KD = D // P
TILES = 5
NTOK = TILES * P
SAMPLES, SAMPLE_LEN = 8, 8
NS = SAMPLES * SAMPLE_LEN
PAST = 1024
HD = 64
HEADS, KV, GROUP = 8, 2, 4
NMEM = 256
MHEADS = 4
PHEADS, NKEYS, TOPK = 8, 128, 16
EPS = 1e-6
NEG = -1e30
LOWEST = -3.4028235e38
BLOCKS = 4 + 4 * PHEADS
RING = 4
INW = 1792


def shape_tables():
    t = {}
    r = np.arange(P)
    t["ident"] = np.eye(P)
    c = np.arange(2 * P)
    t["band"] = np.where((c[None] > r[:, None]) & (c[None] <= r[:, None] + P), 0.0, NEG)
    t["eps"] = np.full((P, 1), EPS)
    t["iota"] = np.broadcast_to(np.arange(TOPK), (P, TOPK))
    seq, head, tok = r // 32, (r // 8) % 4, r % 8
    t["headsel"] = (head[:, None] == np.arange(4)[None]) * 1.0
    gather = np.zeros((P, 2, P))
    for bg in range(2):
        for m in range(P):
            gather[:, bg, m] = ((bg * 4 + seq) * 8 + tok) == m % NS
    t["gather"] = gather.reshape(P, 2 * P)
    half = HD // 2
    inv = np.float32(10000.0) ** (-np.arange(half, dtype=np.float32) / np.float32(half))
    pos = np.stack([PAST + r % 8] + [i * P + r for i in range(TILES - 1)], 1).astype(np.float32)
    ang = pos[:, :, None] * inv[None, None, :].astype(np.float32)
    rot = np.concatenate([np.cos(ang), np.cos(ang), -np.sin(ang), np.sin(ang)], -1)
    t["rot"] = rot.reshape(P, TILES * 4 * half)
    sm = np.full((P, 2, P + NS), NEG)
    for bg in range(2):
        key = np.arange(P)
        sm[:, bg, :P] = np.where(key[None] > tok[:, None], 0.0, NEG)
        new = np.arange(NS)
        ok = (new[None] // 8 == (bg * 4 + seq)[:, None]) & (new[None] % 8 <= tok[:, None])
        sm[:, bg, P:] = np.where(ok, 0.0, NEG)
    t["smask"] = sm.reshape(P, 2 * (P + NS))
    t["blocks"] = ((r[:, None] // 8 == r[None] // 8) & (r[None] % 8 <= r[:, None] % 8)) * 1.0
    t["tril"] = np.tril(np.ones((P, P)))
    t["fold"] = (r[:, None] % NS == r[None] % NS) * 1.0
    return {k: np.ascontiguousarray(v, dtype=np.float32) for k, v in t.items()}


TABLES = {"ident": P, "band": 2 * P, "eps": 1, "iota": TOPK, "headsel": 4, "gather": 2 * P,
          "rot": TILES * P, "smask": 2 * (P + NS), "blocks": P, "tril": P, "fold": P}


def hybrid_step(nc, I, O):
    ctx = ExitStack()
    with ctx:
        def sb(name, n, dt=F32):
            return ctx.enter_context(nc.sbuf_tensor(name, [P, n], dt))

        def sem(name):
            return ctx.enter_context(nc.semaphore(name))

        x_res = sb("x_res", TILES * D)
        xT = sb("xT", KD * NTOK)
        A = sb("A", 16384)
        R = sb("R", 24960)
        ident = sb("ident", P)
        band = sb("band", 2 * P)
        eps = sb("eps", 1)
        iota = sb("iota", TOPK)
        headsel = sb("headsel", 4)
        gather = sb("gather", 2 * P)
        g_sgu = sb("g_sgu", 512)
        gains = sb("gains", 48)
        sinks = sb("sinks", HEADS)
        sinks_s = sb("sinks_s", KV)
        bias_p, bias_s = gains[:, 32:40], gains[:, 40:48]
        stat = sb("stat", 96)
        ps = ctx.enter_context(nc.psum_tensor("ps", [P, 8 * 512], F32))

        def bank(n, w=512, k=1):
            return ps[:, n * 512:n * 512 + w]

        def v3(ap, a):
            return ap.rearrange("p (a b) -> p a b", a=a)

        def xr(t):
            return x_res[:, bass.ds(t * D, D)] if not isinstance(t, int) else x_res[:, t * D:(t + 1) * D]

        xTv = v3(xT[:, :], KD)
        w_in = v3(A[:, 0:KD * INW], KD)
        rot = v3(A[:, 14336:14336 + TILES * P], TILES)
        tmp = A[:, 15872:16384]
        rows48 = A[0:48, 15000:15128]
        s_sb = v3(A[:, 0:2048], HEADS)
        pT = v3(A[:, 2048:4096], 16)
        w_smp = v3(A[:, 2048:3072], HEADS)
        qT = v3(A[:, 4096:4608], 4)
        wsp = v3(A[:, 5120:6144], HEADS)
        wT_p = v3(A[:, 6144:7168], HEADS)
        wT_s = v3(A[:, 7168:8192], HEADS)
        kc = v3(A[:, 8192:9216], SAMPLES)
        vc = v3(A[:, 9216:10240], SAMPLES)
        kcT = v3(A[:, 10240:11264], SAMPLES)
        smask = v3(A[:, 11264:11648], 2)
        blocks = A[:, 11648:11776]
        tril = A[:, 11776:11904]
        w8 = v3(A[:, 12288:12352], HEADS)
        qTr = v3(A[:, 12352:12608], 2)
        s_smp = v3(A[:, 12608:13376], 4)
        pTc = v3(A[:, 13376:13888], 4)
        pTn = v3(A[:, 13888:14400], 4)
        o_exp = v3(A[:, 14400:15424], 4)
        w_pq = v3(A[:, :], KD)
        w_out = v3(R[:, 0:8192], KD)
        PB = 8192

        def proj(t, a, b):
            return R[:, PB + t * INW + a:PB + t * INW + b]

        mem_x = v3(R[:, PB:PB + 2048], 2)
        mem_T = v3(R[:, PB + 2048:PB + 4096], KD)
        w_mk = v3(R[:, PB + 4096:PB + 6144], KD)
        w_mv = v3(R[:, PB + 6144:PB + 8192], KD)
        mk = v3(R[:, PB + 8192:PB + 8704], 2)
        w_cq = v3(R[:, 17152:19200], KD)
        mkT = v3(R[:, 21120:21632], 2)
        mv = v3(R[:, 21760:22272], 2)
        kT = R[:, 22272:22912]
        xs = [R[:, 22912:23936], R[:, 23936:24960]]
        kmT = R[:, 0:4096].rearrange("p (b c k) -> p b c k", b=SAMPLES, c=2)
        s_c = v3(R[:, 4096:5120], MHEADS)
        pT_c = v3(R[:, 5120:6144], 8)
        qcT = v3(R[:, 6144:6400], 2)
        q_bd = v3(R[:, 7424:7936], 2)
        oT_c = v3(R[:, 7936:8192], 2)
        kmem = R[:, PB:PB + 4096].rearrange("p (b c k) -> p b c k", b=SAMPLES, c=2)
        vmem = R[:, PB + 4096:PB + 8192].rearrange("p (b c k) -> p b c k", b=SAMPLES, c=2)
        o_c = R[:, PB + 8192:PB + 8448]
        o_m = v3(R[:, PB + 8448:PB + 8960], 2)
        w_co = v3(R[:, 2048:4096], 2)
        pT_l = xTv[:, :, 2 * P:3 * P]
        qcT_l = xTv[:, :, 3 * P:4 * P]
        mv_l = v3(g_sgu[:, :], 2)
        oT_l = v3(band[:, :], 2)
        o_l = gather[:, :]
        xn = R[:, 0:5120]
        u_ring = [R[:, 5120 + i * D:5120 + (i + 1) * D] for i in range(RING)]
        v_ring = [R[:, 9216 + i * D:9216 + (i + 1) * D] for i in range(RING)]
        sk_raw = v3(R[:, 10240:12288], 16)
        y_out = [R[:, t * D:(t + 1) * D] for t in range(TILES)]
        skT = R[:, 13312:15360]
        xn_cur = [R[:, 15360 + i * D:15360 + (i + 1) * D] for i in range(2)]
        xT_cur = [v3(R[:, 17408 + i * D:17408 + (i + 1) * D], KD) for i in range(2)]
        g_ffn = g_fin = R[:, 19456:20480]
        fold = R[:, 20480:20608]
        diag = v3(R[:, 20608:21120], RING)
        ss = v3(R[:, 21632:21888], 2)
        ss2 = v3(R[:, 21888:22144], 2)
        cand = R[:, 22144:22400]
        onehot = R[:, 22400:22912]
        cand2 = R[:, 22912:23168]
        q_sb = R[:, 23168:23680]
        qT_sb = v3(R[:, 23680:24192], 4)
        idx = v3(R[:, 24192:24256].bitcast(U32), 4)
        gate = v3(R[:, 24256:24320], 4)
        topv = v3(R[:, 24320:24352], 2)
        topi = v3(R[:, 24352:24384].bitcast(U32), 2)
        bestv = R[:, 24384:24400]
        besti = R[:, 24400:24416].bitcast(U32)
        parts = v3(R[:, 24416:24448].bitcast(U32), 2)
        chosen = v3(R[:, 24448:24480], 2)
        hdot = v3(R[:, 24480:24512], 2)
        hgelu = v3(R[:, 24512:24544], 2)
        coef = v3(R[:, 24544:24576], 2)
        negtop = R[:, 24576:24577]
        esum = R[:, 24577:24578]
        rsum = R[:, 24578:24579]

        ssq = [stat[:, 0:2], stat[:, 2:4]]
        rstd = [stat[:, 4:6], stat[:, 6:8]]
        mx = stat[:, 8:16]
        nmx = stat[:, 16:24]
        rs = stat[:, 24:32]
        es = stat[:, 32:40]
        rden = stat[:, 40:48]
        gv_ss = stat[:, 48:56]
        gv_r = stat[:, 56:64]
        ssq_f = stat[:, 80:85]
        rstd_f = stat[:, 85:90]

        ld_tab, ld_mem, ld_wmkv, ld_small = (sem(n) for n in ("ld_tab", "ld_mem", "ld_wmkv", "ld_small"))
        ld_x = [sem(f"ld_x{t}") for t in range(TILES)]
        ld_win = [sem(f"ld_win{c}") for c in range(4)]
        ld_wout, ld_wc, ld_swa, ld_gating, ld_mcache, ld_wpq, ld_sk, ld_ffn, ld_fin = (
            sem(n) for n in ("ld_wout", "ld_wc", "ld_swa", "ld_gating", "ld_mcache", "ld_wpq", "ld_sk",
                             "ld_ffn", "ld_fin"))
        ld_rot = sem("ld_rot")
        ld_rows, gT_done, gT_out = sem("ld_rows"), sem("gT_done"), sem("gT_out")
        stored = sem("stored")
        y_stored = sem("y_stored")
        std_ready = sem("std_ready")
        xs_ready = sem("xs_ready")
        tr_done = sem("tr_done")
        xT_ready = sem("xT_ready")
        chain_v = sem("chain_v")
        chain_a = sem("chain_a")
        mkv_done, mkv_out, mkT_done, mkT_out = (sem(n) for n in ("mkv_done", "mkv_out", "mkT_done", "mkT_out"))
        pq_done, pkv_done, pgu_done, pgv_done = (sem(n) for n in ("pq_done", "pkv_done", "pgu_done", "pgv_done"))
        q_out, kv_out, gu_out, gv_out = (sem(n) for n in ("q_out", "kv_out", "gu_out", "gv_out"))
        w_masked, wT_done, wT_out = (sem(n) for n in ("w_masked", "wT_done", "wT_out"))
        qkT_done, qkT_out = sem("qkT_done"), sem("qkT_out")
        kcT_done, kcT_out, qTr_out = sem("kcT_done"), sem("kcT_out"), sem("qTr_out")
        sc_done, sc_max, sc_exp, pT_done, pT_out, pv_done, attn_out = (
            sem(n) for n in ("sc_done", "sc_max", "sc_exp", "pT_done", "pT_out", "pv_done", "attn_out"))
        so_exp, so_done = sem("so_exp"), sem("so_done")
        gv_ssq, gv_std, gvn_out, mixed_done, sgu_out = (
            sem(n) for n in ("gv_ssq", "gv_std", "gvn_out", "mixed_done", "sgu_out"))
        wo_done, x1_out = sem("wo_done"), sem("x1_out")
        qc_done, qc_out, kmT_done, kmT_out, qbd_out, qbd_zero = (
            sem(n) for n in ("qc_done", "qc_out", "kmT_done", "kmT_out", "qbd_out", "qbd_zero"))
        c_sc, c_max, c_exp, c_pT, c_pTo, c_pv, c_o, c_oT, c_oTo, c_wo, x2_out = (
            sem(n) for n in ("c_sc", "c_max", "c_exp", "c_pT", "c_pTo", "c_pv", "c_o", "c_oT", "c_oTo",
                             "c_wo", "x2_out"))
        c_sel, c_om = sem("c_sel"), sem("c_om")
        mv_moved, ld_wco = sem("mv_moved"), sem("ld_wco")
        l_sc, l_max, l_exp, l_pT, l_pTo, l_pv, l_o, l_oT, l_oTo, l_wo, l_add = (
            sem(n) for n in ("l_sc", "l_max", "l_exp", "l_pT", "l_pTo", "l_pv", "l_o", "l_oT", "l_oTo", "l_wo",
                             "l_add"))
        f_std, f_tr, f_out = sem("f_std"), sem("f_tr"), sem("f_out")
        skT_done, skT_out = sem("skT_done"), sem("skT_out")
        xn_ready = sem("xn_ready")
        xcur_ready, xTcur_ready = sem("xcur_ready"), sem("xTcur_ready")
        pq_q, pq_qo, pq_t, pq_to, pq_s, pq_so = (sem(n) for n in ("pq_q", "pq_qo", "pq_t", "pq_to", "pq_s", "pq_so"))
        best_ready, gexp_ready, idx_ready = sem("best_ready"), sem("gexp_ready"), sem("idx_ready")
        u_landed = [sem(f"u_landed{i}") for i in range(RING)]
        v_landed = [sem(f"v_landed{i}") for i in range(RING)]
        u_used, v_used = sem("u_used"), sem("v_used")
        gelu_ready, coef_ready, diag_ready, acc_added = (
            sem(n) for n in ("gelu_ready", "coef_ready", "diag_ready", "acc_added"))
        apart_v, apart_p = sem("apart_v"), sem("apart_p")
        fin_std, fin_y = sem("fin_std"), sem("fin_y")

        block = ctx.enter_context(nc.Block())

        N_MIX, N_MRG, N_CRS = 2, 7, 12
        G_MIX, G_MEM, G_MRG, G_CRS = range(4)
        STORES = []

        def chain_of(eng, s):
            state = [0, 0]

            def count(ins):
                ins.then_inc(s, 1)
                state[1] += 1

            def hold():
                eng.wait_ge(s, state[0] + state[1])

            def chain(ins):
                count(ins)
                hold()

            return chain, count, hold, state

        def run_blocks(eng, one):
            for b in range(5):
                one(b, b % 4, True, b >= 1)
            with eng.Fori(5, 30, 4) as b0:
                for j in range(4):
                    one(b0 + j, (5 + j) % 4, True, True)
            for b in range(33, BLOCKS + 1):
                one(b, b % 4, b < BLOCKS, True)

        def norm_bank(n):
            if N_MRG <= n < N_CRS:
                return 6
            return 2 * (n % 2) + (0 if n >= N_CRS else 4)

        CROSS_SLOT = (4, 5, 6, 8, 9, 10, 12, 14)
        FFN_SLOT = {(1, 0): 1, (4, 0): 2, (4, 4): 3, (4, 8): 4}

        def beside(b, k, step, ffn):
            if not isinstance(b, int) or b > 4:
                return
            if b < 4 and k in CROSS_SLOT:
                step(b + 1, CROSS_SLOT.index(k))
            for (fb, fk), t in FFN_SLOT.items():
                if fb == b and fk <= k < fk + 4:
                    ffn(t, k - fk)

        def tile_head(b):
            return (b + 4) // 8, (b + 4) % 8

        @block.sync
        def _(sp):
            def load(dst, src, s):
                sp.dma_start(dst, src).then_inc(s, 16)

            def store(dst, src):
                STORES.append(1)
                sp.dma_start(dst, src).then_inc(stored, 16)

            load(mem_x, I["mem_prompt"][0].rearrange("(t p) d -> p t d", p=P), ld_mem)
            for name, dst in (("ident", ident), ("eps", eps), ("band", band), ("iota", iota),
                              ("headsel", headsel), ("gather", gather)):
                load(dst[:, :], I["tab_" + name][:, :], ld_tab)
            load(w_mk, I["w_mk"][0].rearrange("(k p) n -> p k n", p=P), ld_wmkv)
            load(w_mv, I["w_mv"][0].rearrange("(k p) n -> p k n", p=P), ld_wmkv)
            load(rot, v3(I["tab_rot"][:, :], TILES), ld_rot)
            for t in range(TILES):
                if t == 0:
                    flat = I["x_sample"].rearrange("a b d -> (a b) d")
                    load(xr(0)[0:NS], flat, ld_x[0])
                    load(xr(0)[NS:P], flat, ld_x[0])
                else:
                    load(xr(t), I["x_prompt"][0, (t - 1) * P:t * P, :], ld_x[t])
            win = I["w_in"][0].rearrange("(k p) n -> p k n", p=P)
            for c, (a, b) in enumerate(((0, 512), (512, 768), (768, 1280), (1280, 1792))):
                load(w_in[:, :, a:b], win[:, :, a:b], ld_win[c])
            load(w_out, I["w_out"][0].rearrange("(k p) n -> p k n", p=P), ld_wout)
            load(w_cq, I["w_cq"][0].rearrange("(k p) n -> p k n", p=P), ld_wc)
            load(g_ffn, I["g_ffn"][0:1, :].broadcast_to([P, D]), ld_ffn)
            load(fold, I["tab_fold"][:, :], ld_ffn)
            for name in ("k", "v"):
                store(O[f"swa_{name}_s"][0, :, 0:P - SAMPLE_LEN].rearrange("b w h d -> b (w h d)"),
                      I[f"cache_swa_{name}"][0, :, SAMPLE_LEN:P].rearrange("b w h d -> b (w h d)"))
            sp.wait_ge(mkv_out, 4)
            for j in range(2):
                store(O["mem_k"][0, 0, j * P:(j + 1) * P].rearrange("m h d -> m (h d)"), mk[:, j, :])
                store(O["mem_v"][0, 0, j * P:(j + 1) * P].rearrange("m h d -> m (h d)"), mv[:, j, :])
            sp.wait_ge(pgv_done, TILES)
            sp.wait_ge(kv_out, TILES)
            load(kc, I["cache_swa_k"][0].rearrange("b w h d -> w b (h d)"), ld_swa)
            load(vc, I["cache_swa_v"][0].rearrange("b w h d -> w b (h d)"), ld_swa)
            load(smask, v3(I["tab_smask"][:, :], 2), ld_swa)
            load(wsp, I["w_spatial"][0].rearrange("h t r -> t h r"), ld_gating)
            load(tril, I["tab_tril"][:, :], ld_gating)
            load(blocks, I["tab_blocks"][:, :], ld_gating)
            for c in range(2 * SAMPLES):
                load(w8[c * 8:(c + 1) * 8], I["w_spatial"][0, :, 0:8, 0:8].rearrange("h t r -> t h r"), ld_gating)
            for name, a in (("k", 512), ("v", 640)):
                store(O[f"swa_{name}_p"][0, 0].rearrange("w h d -> w (h d)"), proj(TILES - 1, a, a + P))
                for b in range(SAMPLES):
                    store(O[f"swa_{name}_s"][0, b, P - SAMPLE_LEN:P].rearrange("w h d -> w (h d)"),
                          proj(0, a, a + P)[b * 8:(b + 1) * 8])
            sp.wait_ge(gvn_out, 1)
            store(O["sgu_v"][0].rearrange("b t h d -> (b t) (h d)"), proj(0, 1280, 1792)[0:NS])
            sp.wait_ge(sgu_out, TILES)
            sp.wait_ge(attn_out, TILES)
            load(w_pq, I["w_peer_q"][0].rearrange("(k p) n -> p k n", p=P), ld_wpq)
            sp.wait_ge(xs_ready, N_CRS)
            sp.wait_ge(stored, 16 * len(STORES))
            for b in range(SAMPLES):
                load(kmem[:, b], I["cache_mem_k"][0, b].rearrange("(c p) h d -> p c (h d)", p=P), ld_mcache)
                load(vmem[:, b], I["cache_mem_v"][0, b].rearrange("(c p) h d -> p c (h d)", p=P), ld_mcache)
            sp.wait_ge(kmT_done, 4)
            load(sk_raw, I["peer_sub_keys"][0].rearrange("h c k d -> k (h c) d"), ld_sk)
            sp.wait_ge(c_sc, 1)
            load(w_co, I["w_co"][0].rearrange("(k p) n -> p k n", p=P), ld_wco)
            sp.wait_ge(xn_ready, TILES)
            load(g_fin, I["g_final"].rearrange("(a d) -> a d", a=1).broadcast_to([P, D]), ld_fin)
            for t in range(TILES):
                sp.wait_ge(fin_y, t + 1)
                if t == 0:
                    dst, src = O["y_s"].rearrange("a b d -> (a b) d"), y_out[0][0:NS]
                else:
                    dst, src = O["y_p"][0, (t - 1) * P:t * P], y_out[t]
                sp.dma_start(dst, src).then_inc(y_stored, 16)
            sp.wait_ge(y_stored, 16 * TILES)

        @block.gpsimd
        def _(pool):
            def small(dst, src):
                pool.dma_start(dst, src).then_inc(ld_small, 16)

            for r, name in ((8 * G_MIX, "g_mix"), (8 * G_MEM, "g_mem"), (8 * G_MRG, "g_attn_out"),
                            (8 * G_MRG + 4, "g_gmlp_out"), (8 * G_CRS, "g_cross")):
                src = I[name][0].rearrange("(k p) -> k p", p=P)
                pool.dma_start(rows48[r:r + src.shape[0]], src).then_inc(ld_rows, 16)
            pool.dma_start(rows48[32:40], I["b_spatial"][0]).then_inc(ld_rows, 16)
            pool.dma_start(rows48[40:48].rearrange("h (c t) -> h c t", t=8),
                           I["b_spatial"][0, :, 0:8].unsqueeze(1).broadcast_to([HEADS, 16, 8])).then_inc(ld_rows, 16)
            small(g_sgu[:, :], I["g_sgu"].rearrange("a h d -> a (h d)").broadcast_to([P, 512]))
            small(sinks[:, :], I["attn_sinks"][0:1, :].broadcast_to([P, HEADS]))
            pool.wait_ge(x1_out, TILES)
            pool.memset(q_bd, 0.0).then_inc(qbd_zero, 1)

            def gathers(b, m, u, v):
                if u:
                    pool.wait_ge(idx_ready, b + 1)
                for k in range(TOPK):
                    i = k % RING
                    if u:
                        if k >= RING or not isinstance(b, int) or b > 0:
                            pool.wait_ge(u_used, b * TOPK + (k - RING + 1))
                        pool.sem_inc(apart_p, 1)
                        pool.indirect_dma_start(
                            u_ring[i], None, I["peer_u"][0],
                            bass.IndirectOffsetOnAxis(ap=idx[:, m, k:k + 1], axis=0)).then_inc(u_landed[i], 16)
                    if v:
                        if k >= RING or not isinstance(b, int) or b > 1:
                            pool.wait_ge(v_used, b * TOPK + (k - RING + 1 - TOPK))
                        pool.sem_inc(apart_p, 1)
                        pool.indirect_dma_start(
                            v_ring[i], None, I["peer_v"][0],
                            bass.IndirectOffsetOnAxis(ap=idx[:, (m + 3) % 4, k:k + 1], axis=0)).then_inc(v_landed[i], 16)

            pool.wait_ge(skT_out, 1)
            run_blocks(pool, gathers)

        @block.scalar
        def _(act):
            chain, count, hold, _ = chain_of(act, chain_a)

            def norm(n, src, parts=((0, D),)):
                if n >= 2:
                    act.wait_ge(tr_done, n - 1)
                for j, (a, b) in enumerate(parts):
                    ins = act.activation(xs[n % 2][:, a:b], src[j], ACT.Square, accum_out=ssq[n % 2][:, j:j + 1])
                    count(ins)
                hold()
                w = len(parts)
                act.activation(ssq[n % 2][:, 0:w], ssq[n % 2][:, 0:w], ACT.Sqrt, bias=eps[:, 0:1],
                               scale=1.0 / (parts[0][1] - parts[0][0])).then_inc(std_ready, 1)

            act.wait_ge(ld_mem, 16)
            act.wait_ge(ld_tab, 16 * 6)
            for j in range(2):
                norm(j, [mem_x[:, j, :]])
                if j == 0:
                    act.wait_ge(gT_done, 1)
                    act.activation(gains[:, :], bank(3)[:, 0:48], ACT.Copy).then_inc(gT_out, 1)
            for j in range(2):
                act.wait_ge(mkv_done, j + 1)
                act.activation(mk[:, j, :], bank(j)[:, 0:256], ACT.Copy).then_inc(mkv_out, 1)
                act.activation(mv[:, j, :], bank(j)[:, 256:512], ACT.Copy).then_inc(mkv_out, 1)

            def proj_out(t):
                act.wait_ge(pgu_done, t + 1)
                if t == 0:
                    act.wait_ge(stored, 16 * 6)
                act.activation(proj(t, 768, 1280), bank(2), ACT.Gelu).then_inc(gu_out, 1)
                act.wait_ge(pgv_done, t + 1)
                act.activation(proj(t, 1280, 1792), bank(3), ACT.Gelu).then_inc(gv_out, 1)

            def mix_norm(t):
                act.wait_ge(ld_x[t], 32 if t == 0 else 16)
                norm(N_MIX + t, [xr(t)])

            mix_norm(0)
            act.wait_ge(mkT_done, 1)
            act.activation(mkT[:, :, :], v3(bank(2), 2), ACT.Copy).then_inc(mkT_out, 1)
            mix_norm(1)
            for t in range(TILES):
                if t + 2 < TILES:
                    mix_norm(t + 2)
                proj_out(t)

            def gating_std(t):
                act.wait_ge(gv_ssq, t + 1)
                act.activation(gv_ss, gv_ss, ACT.Sqrt, bias=eps[:, 0:1], scale=1.0 / HD).then_inc(gv_std, 1)

            def qkT_evac(t):
                act.wait_ge(qkT_done, t + 1)
                act.activation(kT[:, t * P:(t + 1) * P], bank(5)[:, 0:P], ACT.Copy).then_inc(qkT_out, 1)
                act.activation(qT, v3(bank(4), 4), ACT.Copy).then_inc(qkT_out, 1)

            gating_std(0)
            act.wait_ge(wT_done, 1)
            act.activation(wT_p, ps[:, 2048:3072].rearrange("p (h t) -> p h t", h=HEADS), ACT.Copy).then_inc(wT_out, 1)
            act.activation(wT_s, ps[:, 3072:4096].rearrange("p (h t) -> p h t", h=HEADS), ACT.Copy).then_inc(wT_out, 1)

            act.wait_ge(kcT_done, 1)
            act.activation(kcT, ps[:, 0:1024].rearrange("p (b k) -> p b k", b=SAMPLES), ACT.Copy).then_inc(kcT_out, 1)
            qkT_evac(0)
            act.wait_ge(sc_max, 1)
            for j in range(4):
                act.activation(s_smp[:, j, :], s_smp[:, j, :], ACT.Exp, bias=nmx[:, j:j + 1],
                               accum_out=rs[:, j:j + 1])
            act.activation(es[:, 0:4], es[:, 0:4], ACT.Exp).then_inc(sc_exp, 1)
            gating_std(1)
            act.wait_ge(pT_done, 1)
            act.activation(pTc, v3(bank(4), 4), ACT.Copy).then_inc(pT_out, 1)
            act.activation(pTn[0:NS], v3(bank(5), 4)[0:NS], ACT.Copy).then_inc(pT_out, 1)
            act.wait_ge(qTr_out, 1)
            qkT_evac(1)

            def merged_norm(t):
                act.wait_ge(attn_out, t + 1)
                act.wait_ge(sgu_out, t + 1)
                norm(N_MRG + t, [proj(t, 0, 512), proj(t, 768, 1280)], ((0, 512), (512, 1024)))

            merged_norm(0)
            for t in range(1, TILES):
                if t + 1 < TILES:
                    qkT_evac(t + 1)
                act.wait_ge(sc_max, t + 1)
                lo = P if t == 1 else 0
                for h in range(HEADS):
                    act.activation(s_sb[:, h, lo:], s_sb[:, h, lo:], ACT.Exp, bias=nmx[:, h:h + 1],
                                   accum_out=rs[:, h:h + 1])
                act.activation(es, es, ACT.Exp).then_inc(sc_exp, 1)
                if t + 1 < TILES:
                    gating_std(t + 1)
                act.wait_ge(pT_done, t + 1)
                act.activation(pT[:, 8:16, :], ps[:, 1024:2048].rearrange("p (a b) -> p a b", a=8), ACT.Copy)\
                   .then_inc(pT_out, 1)
                merged_norm(t)
            for t in range(TILES):
                act.wait_ge(x1_out, t + 1)
                norm(N_CRS + t, [xr(t)])

            act.activation(mv_l, mv, ACT.Copy).then_inc(mv_moved, 1)
            for c in range(2):
                act.wait_ge(qc_done, c + 1)
                act.activation(qcT[:, c, :], bank(2 * c)[:, 0:P], ACT.Copy).then_inc(qc_out, 1)
            for c in range(2):
                act.activation(qcT_l[:, 4 * c:4 * c + 3, :], v3(bank(2 * c)[:, P:512], 3), ACT.Copy)\
                   .then_inc(qc_out, 1)
                act.activation(qcT_l[:, 4 * c + 3, :], bank(2 * c + 1)[:, 0:P], ACT.Copy).then_inc(qc_out, 1)
            for g in range(4):
                act.wait_ge(kmT_done, g + 1)
                act.activation(kmT[:, 2 * g:2 * g + 2], ps[:, (4 + 2 * (g % 2)) * 512:(6 + 2 * (g % 2)) * 512]
                               .rearrange("p (b c k) -> p b c k", b=2, c=2), ACT.Copy).then_inc(kmT_out, 1)
            act.wait_ge(c_max, 1)
            for bg in range(2):
                act.activation(s_c[:, bg, :], bank(0)[:, bg * 256:(bg + 1) * 256], ACT.Exp,
                               bias=nmx[:, bg:bg + 1], scale=0.125, accum_out=rs[:, bg:bg + 1]).then_inc(c_exp, 1)
            act.wait_ge(c_pT, 1)
            act.activation(pT_c[:, 0:4, :], v3(bank(2), 4), ACT.Copy).then_inc(c_pTo, 1)
            act.wait_ge(c_oT, 1)
            act.activation(oT_c, v3(bank(5)[:, 0:256], 2), ACT.Copy).then_inc(c_oTo, 1)
            act.wait_ge(skT_done, 1)
            act.activation(v3(skT, 4), v3(ps[:, 0:2048], 4), ACT.Copy).then_inc(skT_out, 1)

            def ffn(t, part):
                if part == 0:
                    act.wait_ge(*((x2_out, 1) if t == 0 else (l_add, 2 * t)))
                    chain(act.activation(xn[:, t * D:(t + 1) * D], xr(t), ACT.Square,
                                         accum_out=ssq_f[:, t:t + 1]))
                    act.activation(ssq_f[:, t:t + 1], ssq_f[:, t:t + 1], ACT.Sqrt, bias=eps[:, 0:1],
                                   scale=1.0 / D).then_inc(f_std, 1)
                elif part >= 2:
                    h = part - 2
                    act.wait_ge(f_tr, 2 * t + h + 1)
                    act.activation(xTv[:, 4 * h:4 * h + 4, t * P:(t + 1) * P], v3(bank(7), 4), ACT.Copy)\
                       .then_inc(f_out, 1)

            def cross(t, step):
                n = t - 1
                if step < 2:
                    act.wait_ge(l_max, 2 * n + step + 1)
                    for c in range(2):
                        h = 2 * step + c
                        act.activation(s_c[:, h, :], bank(7)[:, c * 256:(c + 1) * 256], ACT.Exp,
                                       bias=nmx[:, h:h + 1], scale=0.125, accum_out=rs[:, h:h + 1])\
                           .then_inc(l_exp, 1)
                elif step < 4:
                    act.wait_ge(l_pT, 2 * n + step - 1)
                    act.activation(pT_l[:, 4 * step - 8:4 * step - 4, :], v3(bank(7), 4), ACT.Copy).then_inc(l_pTo, 1)
                elif step == 5:
                    act.wait_ge(l_oT, n + 1)
                    act.activation(oT_l, v3(bank(7)[:, 0:256], 2), ACT.Copy).then_inc(l_oTo, 1)

            for part in (0, 2, 3):
                ffn(0, part)
            act.wait_ge(ld_ffn, 32)

            def copy_xT(s):
                t = 0 if isinstance(s, int) and s < 4 else tile_head(s)[0]
                act.wait_ge(pq_q, s - 1) if not isinstance(s, int) or s > 1 else None
                if isinstance(t, int):
                    act.wait_ge(f_out, 2 * t + 2)
                src = xTv[:, :, t * P:(t + 1) * P] if isinstance(t, int) else xTv[:, :, bass.ds(t * P, P)]
                act.activation(xT_cur[cur(s)], src, ACT.Copy).then_inc(xTcur_ready, 1)

            cur_m = [0]

            def cur(s):
                return (s if isinstance(s, int) else cur_m[0]) % 2

            def queries_out(s, w):
                act.wait_ge(pq_q, s + 1)
                act.activation(q_sb[:, 0:w], bank(4)[:, 0:w], ACT.Copy).then_inc(pq_qo, 1)

            def queriesT_out(s, w):
                act.wait_ge(pq_t, s + 1)
                act.activation(qT_sb[:, 0:w // P, :], v3(bank(5)[:, 0:w], w // P), ACT.Copy).then_inc(pq_to, 1)

            def scores_out(s):
                act.wait_ge(pq_s, s + 1)
                if not isinstance(s, int) or s > 0:
                    act.wait_ge(best_ready, s)
                act.activation(ss, v3(bank(6)[:, 0:256], 2), ACT.Copy).then_inc(pq_so, 1)

            def gates(s, m):
                act.wait_ge(best_ready, s + 1)
                act.activation(gate[:, m, :], bestv, ACT.Exp, bias=negtop, accum_out=esum).then_inc(gexp_ready, 1)

            def copy_x(b):
                t = 0 if isinstance(b, int) and b < 4 else tile_head(b)[0]
                if not isinstance(b, int) or b > 1:
                    act.wait_ge(u_used, b * TOPK - TOPK)
                if isinstance(t, int):
                    act.wait_ge(xn_ready, t + 1)
                src = xn[:, t * D:(t + 1) * D] if isinstance(t, int) else xn[:, bass.ds(t * D, D)]
                act.activation(xn_cur[cur(b)], src, ACT.Copy).then_inc(xcur_ready, 1)

            for s in range(2):
                copy_xT(s)
                queries_out(s, 512)
                queriesT_out(s, 512)
                scores_out(s)
                gates(s, s)
                if s == 0:
                    copy_x(0)

            def diagonals(b, k0, k1):
                base = fold if isinstance(b, int) and b <= 4 else ident[:, :]
                for k in range(k0, k1):
                    if k >= RING or not isinstance(b, int) or b > 1:
                        act.wait_ge(v_used, b * TOPK + (k - RING + 1 - TOPK))
                    act.activation(diag[:, k % RING, :], base, ACT.Copy,
                                   scale=coef[:, diag_m[0], k:k + 1]).then_inc(diag_ready, 1)

            diag_m = [0]

            def one(b, m, u, v):
                more = u and not (isinstance(b, int) and b + 2 >= BLOCKS)
                w = 512 if isinstance(b, int) and b + 2 < 4 else 256
                if more:
                    cur_m[0] = m + 2
                    copy_xT(b + 2)
                if u and not (isinstance(b, int) and b + 1 >= BLOCKS):
                    cur_m[0] = m + 1
                    copy_x(b + 1)
                diag_m[0] = (m + 1) % 2
                if v:
                    act.wait_ge(coef_ready, b)
                    diagonals(b, 0, 2)
                for k in range(TOPK):
                    if v and k + 2 < TOPK:
                        diagonals(b, k + 2, k + 3)
                    if more and k == 1:
                        queries_out(b + 2, w)
                    if more and k == 3:
                        queriesT_out(b + 2, w)
                    if more and k == 5:
                        scores_out(b + 2)
                    if k == 9 and isinstance(b, int) and b >= 33:
                        final(b - 33)
                    beside(b, k, cross, ffn)
                if u:
                    act.wait_ge(u_used, b * TOPK + TOPK)
                    act.activation(hgelu[:, m % 2, :], hdot[:, m % 2, :], ACT.Gelu).then_inc(gelu_ready, 1)
                if more:
                    gates(b + 2, (m + 2) % 4)

            def final(t):
                act.wait_ge(acc_added, 8 * t + 4)
                act.wait_ge(xcur_ready, 8 * t + 4)
                chain(act.activation(y_out[t], xr(t), ACT.Square, accum_out=stat[:, 64 + t:65 + t]))
                act.activation(stat[:, 64 + t:65 + t], stat[:, 64 + t:65 + t], ACT.Sqrt, bias=eps[:, 0:1],
                               scale=1.0 / D).then_inc(fin_std, 1)

            run_blocks(act, one)
            final(TILES - 1)

        @block.vector
        def _(dve):
            chain, _, _, steps = chain_of(dve, chain_v)

            def scale_rows(n, src, parts=((0, D),)):
                w = len(parts)
                dve.wait_ge(std_ready, n + 1)
                if n >= 2:
                    dve.wait_ge(tr_done, n - 1)
                chain(dve.reciprocal(rstd[n % 2][:, 0:w], ssq[n % 2][:, 0:w]))
                for j, (a, b) in enumerate(parts):
                    ins = dve.tensor_scalar(xs[n % 2][:, a:b], src[j], rstd[n % 2][:, j:j + 1], None, ALU.mult)
                ins.then_inc(xs_ready, 1)

            def take_T(n, dst, g):
                dve.wait_ge(tr_done, n + 1)
                q = norm_bank(n)
                for j in range(2):
                    ins = dve.tensor_tensor(
                        dst[:, 4 * j:4 * j + 4], v3(bank(q + j), 4),
                        gains[:, g * KD + 4 * j:g * KD + 4 * j + 4].unsqueeze(2).broadcast_to([P, 4, P]), ALU.mult)
                ins.then_inc(xT_ready, 1)

            def tile_T(t):
                return xTv[:, :, t * P:(t + 1) * P]

            dve.wait_ge(ld_mem, 16)
            dve.wait_ge(ld_small, 32)
            dve.wait_ge(ld_tab, 16 * 6)
            for kv in range(KV):
                ins = dve.tensor_tensor(tmp[:, kv * 4:kv * 4 + 4], sinks[:, kv * 4:kv * 4 + 4], headsel[:, :], ALU.mult)
            chain(ins)
            chain(dve.tensor_reduce(sinks_s[:, :], v3(tmp[:, 0:8], 2), AX_X, ALU.add))
            dve.wait_ge(gT_out, 1)
            for j in range(2):
                scale_rows(j, [mem_x[:, j, :]])
                take_T(j, mem_T[:, :, j * P:(j + 1) * P], G_MEM)
            def rope(src, dst, t, n):
                r3 = src.rearrange("p (h d) -> p h d", d=HD)
                t3 = tmp[:, 0:n * HD].rearrange("p (h d) -> p h d", d=HD)
                half = HD // 2

                def ang(a, b):
                    return rot[:, t, a:b].unsqueeze(1).broadcast_to([P, n, b - a])

                dve.tensor_tensor(t3[:, :, 0:half], r3[:, :, half:HD], ang(HD, HD + half), ALU.mult)
                dve.tensor_tensor(t3[:, :, half:HD], r3[:, :, 0:half], ang(HD + half, 2 * HD), ALU.mult)
                ang_c = rot[:, t, 0:HD]
                if n == HEADS:
                    o = dst.rearrange("p (a j d) -> p j a d", j=2, d=HD)
                    for j in range(2):
                        ins = dve.tensor_tensor(o[:, j], r3[:, 4 * j:4 * j + 4],
                                                ang_c.unsqueeze(1).broadcast_to([P, 4, HD]), ALU.mult)
                    chain(ins)
                    for j in range(2):
                        ins = dve.tensor_tensor(o[:, j], o[:, j], t3[:, 4 * j:4 * j + 4], ALU.add)
                else:
                    o = dst.rearrange("p (h d) -> p h d", d=HD)
                    chain(dve.tensor_tensor(o, r3, ang_c.unsqueeze(1).broadcast_to([P, n, HD]), ALU.mult))
                    ins = dve.tensor_tensor(o, o, t3, ALU.add)
                return ins

            def mix_rows(t):
                dve.wait_ge(ld_x[t], 32 if t == 0 else 16)
                scale_rows(N_MIX + t, [xr(t)])

            mix_rows(0)
            take_T(N_MIX, tile_T(0), G_MIX)
            mix_rows(1)
            dve.wait_ge(ld_rot, 16)
            for t in range(TILES):
                if t + 1 < TILES:
                    take_T(N_MIX + t + 1, tile_T(t + 1), G_MIX)
                if t + 2 < TILES:
                    mix_rows(t + 2)
                dve.wait_ge(pq_done, t + 1)
                if t == 0:
                    dve.wait_ge(mkT_done, 1)
                    dve.wait_ge(mkv_done, 2)
                ins = rope(bank(0), proj(t, 0, 512), t, HEADS)
                ins.then_inc(q_out, 1)
                dve.wait_ge(q_out, t + 1)
                dve.wait_ge(pkv_done, t + 1)
                chain(dve.tensor_copy(proj(t, 640, 768), bank(1)[:, P:2 * P]))
                ins = rope(bank(1)[:, 0:P], proj(t, 512, 640), t, KV)
                ins.then_inc(kv_out, 1)
                dve.wait_ge(kv_out, t + 1)

            t3 = tmp.rearrange("p (h d) -> p h d", d=HD)

            def gating_squares(t):
                gv = proj(t, 1280, 1792).rearrange("p (h d) -> p h d", d=HD)
                dve.wait_ge(gv_out, t + 1)
                if t >= 2:
                    dve.wait_ge(sgu_out, t - 1)
                chain(dve.tensor_tensor(t3, gv, gv, ALU.mult))
                dve.tensor_reduce(gv_ss, t3, AX_X, ALU.add).then_inc(gv_ssq, 1)

            def gating_values(t):
                gv = proj(t, 1280, 1792).rearrange("p (h d) -> p h d", d=HD)
                dve.wait_ge(gv_std, t + 1)
                chain(dve.reciprocal(gv_r, gv_ss))
                chain(dve.tensor_tensor(gv, gv, gv_r.unsqueeze(2).broadcast_to([P, HEADS, HD]), ALU.mult))
                dve.tensor_tensor(proj(t, 1280, 1792), proj(t, 1280, 1792), g_sgu[:, :], ALU.mult).then_inc(gvn_out, 1)

            def gated(t):
                dve.wait_ge(mixed_done, t + 1)
                if t > 0:
                    dve.wait_ge(gv_ssq, min(t + 2, TILES))
                bias = bias_s if t == 0 else bias_p
                chain(dve.tensor_tensor(t3, v3(bank(6 if t == 0 else 5), HEADS),
                                        bias.unsqueeze(2).broadcast_to([P, HEADS, HD]), ALU.add))
                dve.wait_ge(gu_out, t + 1)
                dve.tensor_tensor(proj(t, 768, 1280), proj(t, 768, 1280), tmp, ALU.mult).then_inc(sgu_out, 1)

            gating_squares(0)
            gating_values(0)
            dve.wait_ge(ld_gating, 16 * 19)
            dve.tensor_tensor(wsp, wsp, tril.unsqueeze(1).broadcast_to([P, HEADS, P]), ALU.mult)
            for h in range(HEADS):
                ins = dve.tensor_tensor(w_smp[:, h, :].rearrange("p (b r) -> p b r", b=16),
                                        blocks.rearrange("p (b r) -> p b r", b=16),
                                        w8[:, h, :].unsqueeze(1).broadcast_to([P, 16, 8]), ALU.mult)
            ins.then_inc(w_masked, 1)

            dve.wait_ge(qkT_out, 2)
            for bg in range(2):
                ins = dve.tensor_copy(qTr[:, bg, :].rearrange("p (b h i) -> p b h i", b=4, h=4),
                                      qT[:, :, bg * 32:(bg + 1) * 32].rearrange("p h (b i) -> p b h i", b=4))
            ins.then_inc(qTr_out, 1)
            gated(0)
            dve.wait_ge(sgu_out, 1)
            dve.wait_ge(sc_done, 1)
            dve.wait_ge(ld_swa, 48)
            for j in range(4):
                ins = dve.scalar_tensor_tensor(s_smp[:, j, :], bank(j // 2)[:, (j % 2) * 192:(j % 2) * 192 + 192],
                                               0.125, smask[:, j % 2, :], ALU.mult, ALU.add)
            chain(ins)
            chain(dve.tensor_reduce(mx[:, 0:4], s_smp, AX_X, ALU.max))
            for kv in range(KV):
                ins = dve.tensor_tensor(mx[:, 2 * kv:2 * kv + 2], mx[:, 2 * kv:2 * kv + 2],
                                        sinks_s[:, kv:kv + 1].broadcast_to([P, 2]), ALU.max)
            chain(ins)
            chain(dve.tensor_scalar(nmx[:, 0:4], mx[:, 0:4], -1.0, None, ALU.mult))
            for kv in range(KV):
                ins = dve.tensor_tensor(es[:, 2 * kv:2 * kv + 2], nmx[:, 2 * kv:2 * kv + 2],
                                        sinks_s[:, kv:kv + 1].broadcast_to([P, 2]), ALU.add)
            ins.then_inc(sc_max, 1)
            gating_squares(1)
            dve.wait_ge(sc_exp, 1)
            chain(dve.tensor_tensor(rs[:, 0:4], rs[:, 0:4], es[:, 0:4], ALU.add))
            chain(dve.reciprocal(rden[:, 0:4], rs[:, 0:4]))
            gating_values(1)
            dve.wait_ge(pv_done, 1)
            for j in range(4):
                for h in range(4):
                    ins = dve.tensor_scalar(o_exp[:, j, h * HD:(h + 1) * HD], bank(2)[:, j * HD:(j + 1) * HD],
                                            rden[:, j:j + 1], headsel[:, h:h + 1], ALU.mult, ALU.mult)
            ins.then_inc(so_exp, 1)
            dve.wait_ge(so_done, 1)
            dve.wait_ge(qkT_done, 1)
            dve.tensor_copy(proj(0, 0, 512), bank(3)).then_inc(attn_out, 1)

            def add_out(n, q, done, out):
                dve.wait_ge(done, n + 1)
                dve.tensor_tensor(xr(n), xr(n), ps[:, q * 512:(q + 2) * 512], ALU.add).then_inc(out, 1)

            def merged_rows(t):
                dve.wait_ge(attn_out, t + 1)
                dve.wait_ge(sgu_out, t + 1)
                scale_rows(N_MRG + t, [proj(t, 0, 512), proj(t, 768, 1280)], ((0, 512), (512, 1024)))

            for t in range(1, TILES):
                lo = P if t == 1 else 0
                merged_rows(t - 1)
                dve.wait_ge(sc_done, t + 1)
                dve.wait_ge(sc_exp, t)
                if t > 1:
                    dve.wait_ge(pT_done, t)
                chain(dve.scalar_tensor_tensor(
                    s_sb[:, :, lo:], v3(ps[:, 0:2048], HEADS)[:, :, lo:], 0.125,
                    band[:, lo:].unsqueeze(1).broadcast_to([P, HEADS, 2 * P - lo]), ALU.mult, ALU.add))
                take_T(N_MRG + t - 1, tile_T(t - 1), G_MRG)
                chain(dve.tensor_reduce(mx, s_sb[:, :, lo:], AX_X, ALU.max))
                chain(dve.tensor_tensor(mx, mx, sinks[:, :], ALU.max))
                chain(dve.tensor_scalar(nmx, mx, -1.0, None, ALU.mult))
                dve.tensor_tensor(es, nmx, sinks[:, :], ALU.add).then_inc(sc_max, 1)
                if t + 1 < TILES:
                    gating_squares(t + 1)
                gated(t)
                add_out(t - 1, 6, wo_done, x1_out)
                if lo == 0:
                    dve.wait_ge(pT_done, t + 1)
                    dve.tensor_copy(pT[:, 0:8, :], ps[:, 0:1024].rearrange("p (a b) -> p a b", a=8)).then_inc(pT_out, 1)
                dve.wait_ge(sc_exp, t + 1)
                chain(dve.tensor_tensor(rs, rs, es, ALU.add))
                chain(dve.reciprocal(rden, rs))
                dve.wait_ge(pv_done, t + 1)
                dve.tensor_tensor(proj(t, 0, 512).rearrange("p (h d) -> p h d", d=HD),
                                  v3(bank(0), HEADS), rden.unsqueeze(2).broadcast_to([P, HEADS, HD]), ALU.mult)\
                   .then_inc(attn_out, 1)
                if t + 1 < TILES:
                    gating_values(t + 1)
            merged_rows(TILES - 1)
            take_T(N_MRG + TILES - 1, tile_T(TILES - 1), G_MRG)
            for t in range(TILES):
                dve.wait_ge(x1_out, t + 1)
                dve.wait_ge(wo_done, t + 1)
                scale_rows(N_CRS + t, [xr(t)])
                if t == 2:
                    add_out(TILES - 1, 6, wo_done, x1_out)
                take_T(N_CRS + t, tile_T(t), G_CRS)

            dve.wait_ge(qc_out, 2)
            dve.wait_ge(qbd_zero, 1)
            for c in range(2):
                for j in range(2):
                    h = 2 * c + j
                    ins = dve.tensor_copy(
                        q_bd[64 * j:64 * j + 64, c, :].rearrange("p (b h i) -> p b h i", b=8, h=4)[:, :, h, :],
                        qcT[64 * j:64 * j + 64, c, 0:NS].rearrange("p (b i) -> p b i", b=8))
            ins.then_inc(qbd_out, 1)
            dve.wait_ge(c_sc, 1)
            chain(dve.tensor_reduce(mx[:, 0:2], v3(ps[:, 0:512], 2), AX_X, ALU.max))
            dve.tensor_scalar(nmx[:, 0:2], mx[:, 0:2], -0.125, None, ALU.mult).then_inc(c_max, 1)
            dve.wait_ge(c_exp, 2)
            chain(dve.reciprocal(rden[:, 0:2], rs[:, 0:2]))
            dve.wait_ge(c_pv, 1)
            for bg in range(2):
                for h in range(MHEADS):
                    ins = dve.tensor_scalar(o_m[:, bg, h * HD:(h + 1) * HD],
                                            bank(4)[:, bg * 256 + h * HD:bg * 256 + (h + 1) * HD],
                                            rden[:, bg:bg + 1], headsel[:, h:h + 1], ALU.mult, ALU.mult)
            ins.then_inc(c_om, 1)
            dve.wait_ge(c_sel, 1)
            dve.tensor_copy(o_c, bank(5)[:, 256:512]).then_inc(c_o, 1)
            add_out(0, 6, c_wo, x2_out)

            def ffn(t, part):
                if part == 1:
                    dve.wait_ge(f_std, t + 1)
                    chain(dve.reciprocal(rstd_f[:, t:t + 1], ssq_f[:, t:t + 1]))
                    dve.scalar_tensor_tensor(xn[:, t * D:(t + 1) * D], xr(t), rstd_f[:, t:t + 1], g_ffn,
                                             ALU.mult, ALU.mult).then_inc(xn_ready, 1)

            def cross(t, step):
                n = t - 1
                if step < 2:
                    w = slice(2 * step, 2 * step + 2)
                    dve.wait_ge(l_sc, 2 * n + step + 1)
                    if n > 0:
                        dve.wait_ge(l_exp, 4 * n)
                    chain(dve.tensor_reduce(mx[:, w], v3(bank(7), 2), AX_X, ALU.max))
                    dve.tensor_scalar(nmx[:, w], mx[:, w], -0.125, None, ALU.mult).then_inc(l_max, 1)
                elif step == 4:
                    dve.wait_ge(l_exp, 4 * n + 4)
                    chain(dve.reciprocal(rden[:, 0:4], rs[:, 0:4]))
                    dve.wait_ge(l_pv, n + 1)
                    for j in range(2):
                        ins = dve.tensor_tensor(o_l.rearrange("p (c j d) -> p j c d", j=2, d=HD)[:, j],
                                                v3(bank(7)[:, j * P:(j + 1) * P], 2),
                                                rden[:, 2 * j:2 * j + 2].unsqueeze(2).broadcast_to([P, 2, HD]),
                                                ALU.mult)
                    ins.then_inc(l_o, 1)
                elif step >= 6:
                    c = step - 6
                    dve.wait_ge(l_wo, 2 * n + c + 1)
                    part = xr(t)[:, c * 512:(c + 1) * 512]
                    dve.tensor_tensor(part, part, bank(7), ALU.add).then_inc(l_add, 1)

            dve.wait_ge(ld_ffn, 32)
            dve.wait_ge(x2_out, 1)
            ffn(0, 1)

            def apart():
                dve.sem_inc(apart_v, 1)

            def top16(values, vals, inds, rest):
                apart()
                chain(dve.max(vals[:, 0:8], values))
                apart()
                dve.max_index(inds[:, 0:8], vals[:, 0:8], values)
                chain(dve.match_replace(rest, vals[:, 0:8], values, LOWEST))
                apart()
                chain(dve.max(vals[:, 8:16], rest))
                apart()
                return dve.max_index(inds[:, 8:16], vals[:, 8:16], rest)

            def top_keys(s, c):
                if c == 0:
                    dve.wait_ge(pq_so, s + 1)
                chain(top16(ss[:, c, :], topv[:, c, :], topi[:, c, :], ss2[:, c, :]))

            def best_pairs(s):
                if not isinstance(s, int) or s > 0:
                    dve.wait_ge(gexp_ready, s)
                c3 = cand.rearrange("p (a b) -> p a b", a=TOPK)
                chain(dve.tensor_tensor(c3, topv[:, 0, :].unsqueeze(2).broadcast_to([P, TOPK, TOPK]),
                                        topv[:, 1, :].unsqueeze(1).broadcast_to([P, TOPK, TOPK]), ALU.add))
                chain(top16(cand, bestv, besti, cand2))
                dve.tensor_scalar(negtop, bestv[:, 0:1], -1.0, None, ALU.mult).then_inc(best_ready, 1)

            def experts_of(s, m):
                dve.tensor_scalar(parts[:, 0, :], besti, 4, None, ALU.logical_shift_right)
                chain(dve.tensor_scalar(parts[:, 1, :], besti, 15, None, ALU.bitwise_and))
                hot = onehot.rearrange("p (a b) -> p a b", b=TOPK)
                chain(dve.tensor_tensor(hot, parts.rearrange("p c k -> p (c k)").unsqueeze(2)
                                        .broadcast_to([P, 2 * TOPK, TOPK]),
                                        iota[:, :].unsqueeze(1).broadcast_to([P, 2 * TOPK, TOPK]), ALU.is_equal))
                hot4 = onehot.rearrange("p (c a b) -> p c a b", c=2, b=TOPK)
                for c in range(2):
                    ins = dve.tensor_tensor(hot4[:, c], hot4[:, c],
                                            topi[:, c, :].unsqueeze(1).broadcast_to([P, TOPK, TOPK]), ALU.mult)
                chain(ins)
                chain(dve.tensor_reduce(chosen.rearrange("p c k -> p (c k)"), hot, AX_X, ALU.add))
                if not isinstance(s, int) or s >= 4:
                    dve.wait_ge(v_landed[3], 64 * (s - 3))
                dve.scalar_tensor_tensor(idx[:, m, :], chosen[:, 0, :], float(NKEYS), chosen[:, 1, :],
                                         ALU.mult, ALU.add).then_inc(idx_ready, 1)

            def finish_gates(s, m):
                dve.wait_ge(gexp_ready, s + 1)
                chain(dve.reciprocal(rsum, esum))
                chain(dve.tensor_scalar(gate[:, m, :], gate[:, m, :], rsum, None, ALU.mult))

            for c in range(2):
                top_keys(0, c)
            best_pairs(0)
            experts_of(0, 0)
            finish_gates(0, 0)

            def add_acc(b, m):
                s = b - 2
                dve.wait_ge(v_used, s * TOPK + TOPK)
                t = 0 if isinstance(s, int) and s < 4 else tile_head(s)[0]
                q = 2 * (m % 2)
                ins = dve.tensor_tensor(xr(t), xr(t), ps[:, q * 512:(q + 2) * 512], ALU.add)
                ins.then_inc(acc_added, 1)

            def add_last(b, m):
                if not isinstance(b, int) or b >= 3:
                    dve.wait_ge(acc_added, b - 2)
                add_acc(b, m)

            def one(b, m, u, v):
                more = u and not (isinstance(b, int) and b + 2 >= BLOCKS)
                if u:
                    dve.wait_ge(xcur_ready, b + 1)
                    for k in range(TOPK):
                        dve.wait_ge(u_landed[k % RING], b * 64 + 16 * (k // RING + 1))
                        dve.tensor_tensor_reduce(u_ring[k % RING], u_ring[k % RING], xn_cur[m % 2], 1.0, 0.0, ALU.mult,
                                                 ALU.add, hdot[:, m % 2, k:k + 1]).then_inc(u_used, 1)
                        if isinstance(b, int) and b == 0 and k == 1:
                            for c in range(2):
                                top_keys(1, c)
                        if isinstance(b, int) and b == 0 and k == 2:
                            best_pairs(1)
                            experts_of(1, 1)
                        gates_at = 4 if isinstance(b, int) and b == 0 else 1
                        if k == gates_at and not (isinstance(b, int) and b + 1 >= BLOCKS):
                            finish_gates(b + 1, (m + 1) % 4)
                        if k == 3 and (not isinstance(b, int) or b >= 2):
                            add_last(b, m)
                        if more and k in (5, 7):
                            top_keys(b + 2, (k - 5) // 2)
                        if more and k == 9:
                            best_pairs(b + 2)
                        if more and k == 11:
                            experts_of(b + 2, (m + 2) % 4)
                        if k == 12 and isinstance(b, int) and b >= 33:
                            final(b - 33)
                        beside(b, k, cross, ffn)
                    dve.wait_ge(gelu_ready, b + 1)
                    dve.tensor_tensor(coef[:, m % 2, :], hgelu[:, m % 2, :], gate[:, m, :], ALU.mult)\
                       .then_inc(coef_ready, 1)
                else:
                    add_last(b, m)
                    final(b - 33)

            def final(t):
                dve.wait_ge(ld_fin, 16)
                dve.wait_ge(fin_std, t + 1)
                c = stat[:, 72 + t:73 + t]
                chain(dve.reciprocal(c, stat[:, 64 + t:65 + t]))
                dve.scalar_tensor_tensor(y_out[t], xr(t), c, g_fin, ALU.mult, ALU.mult).then_inc(fin_y, 1)

            for b in range(5):
                one(b, b % 4, True, b >= 1)
            start, steps[1] = steps[1], 0
            with dve.Fori(5, 30, 4) as b0:
                steps[0] = b0 * CHAIN_PER_BLOCK + (start - 5 * CHAIN_PER_BLOCK)
                for j in range(4):
                    one(b0 + j, (5 + j) % 4, True, True)
                assert steps[1] == 4 * CHAIN_PER_BLOCK, steps
            steps[:] = [0, start + 28 * CHAIN_PER_BLOCK]
            for b in range(33, BLOCKS + 1):
                one(b, b % 4, b < BLOCKS, True)
            dve.wait_ge(acc_added, BLOCKS - 1)
            add_acc(BLOCKS + 1, (BLOCKS + 1) % 4)
            final(TILES - 1)

        @block.tensor
        def _(pe):
            def transposes(n):
                pe.wait_ge(xs_ready, n + 1)
                if n >= 2:
                    pe.wait_ge(xT_ready, n - 1)
                q = norm_bank(n)
                for k in range(KD):
                    ins = pe.transpose(bank(q + k // 4)[:, (k % 4) * P:(k % 4 + 1) * P],
                                       xs[n % 2][:, k * P:(k + 1) * P], ident[:, :])
                ins.then_inc(tr_done, 1)

            def product(out, lhs, rhs, n=KD):
                for k in range(n):
                    ins = pe.matmul(out, lhs(k), rhs(k), start=(k == 0), stop=(k == n - 1))
                return ins

            pe.wait_ge(ld_tab, 16 * 6)
            pe.wait_ge(ld_rows, 16 * 7)
            pe.transpose(bank(3)[:, 0:48], rows48, ident[0:48, 0:48]).then_inc(gT_done, 1)
            for j in range(2):
                transposes(j)
                pe.wait_ge(xT_ready, j + 1)
                if j == 0:
                    pe.wait_ge(ld_wmkv, 32)
                product(bank(j)[:, 0:256], lambda k: mem_T[:, k, j * P:(j + 1) * P], lambda k: w_mk[:, k, :])
                product(bank(j)[:, 256:512], lambda k: mem_T[:, k, j * P:(j + 1) * P], lambda k: w_mv[:, k, :]).then_inc(mkv_done, 1)
            transposes(N_MIX)
            for t in range(TILES):
                if t == 0:
                    pe.wait_ge(mkv_out, 4)
                    for c in range(2):
                        for j in range(2):
                            ins = pe.transpose(bank(2)[:, c * 256 + j * P:c * 256 + (j + 1) * P],
                                               mk[:, j, c * P:(c + 1) * P], ident[:, :])
                    ins.then_inc(mkT_done, 1)
                    pe.wait_ge(mkT_out, 1)
                if t + 1 < TILES:
                    transposes(N_MIX + t + 1)
                pe.wait_ge(xT_ready, N_MIX + t + 1)
                for c, (a, b, done, out) in enumerate(((0, 512, pq_done, q_out), (512, 768, pkv_done, kv_out),
                                                       (768, 1280, pgu_done, gu_out), (1280, 1792, pgv_done, gv_out))):
                    if t == 0:
                        pe.wait_ge(ld_win[c], 16)
                    else:
                        pe.wait_ge(out, t)
                    product(bank(c)[:, 0:b - a], lambda k: xTv[:, k, t * P:(t + 1) * P],
                            lambda k: w_in[:, k, a:b]).then_inc(done, 1)

            pe.wait_ge(w_masked, 1)
            for n, w in enumerate((wsp, w_smp)):
                for h in range(HEADS):
                    ins = pe.transpose(ps[:, 2048 + n * 1024 + h * P:2048 + n * 1024 + (h + 1) * P], w[:, h, :],
                                       ident[:, :])
            ins.then_inc(wT_done, 1)

            pe.wait_ge(ld_swa, 48)
            pe.wait_ge(kv_out, TILES)
            pe.wait_ge(q_out, TILES)
            for b in range(SAMPLES):
                ins = pe.transpose(ps[:, b * P:(b + 1) * P], kc[:, b, :], ident[:, :])
            ins.then_inc(kcT_done, 1)

            def heads_T(t):
                for a in range(4):
                    pe.transpose(bank(4)[:, a * P:(a + 1) * P], proj(t, a * P, (a + 1) * P), ident[:, :])
                pe.transpose(bank(5)[:, 0:P], proj(t, 512, 640), ident[:, :]).then_inc(qkT_done, 1)

            pe.wait_ge(wT_out, 2)
            heads_T(0)

            def gating(t, out):
                pe.wait_ge(gvn_out, t + 1)
                for h in range(HEADS):
                    ins = pe.matmul(out[:, h * HD:(h + 1) * HD], (wT_s if t == 0 else wT_p)[:, h, :],
                                    proj(t, 1280 + h * HD, 1280 + (h + 1) * HD), start=True, stop=True)
                ins.then_inc(mixed_done, 1)

            gating(0, bank(6))
            pe.wait_ge(kcT_out, 1)
            pe.wait_ge(qTr_out, 1)
            for j in range(4):
                kv, bg = j // 2, j % 2
                rows = slice(64 * kv, 64 * kv + 64)
                o = bank(j // 2)[:, (j % 2) * 192:(j % 2) * 192 + 192]
                ins = pe.matmul(o[:, P:P + NS], qTr[rows, bg, :], kT[rows, 0:NS], start=True, stop=True)
                for s in range(4):
                    ins = pe.matmul(o[32 * s:32 * s + 32, 0:P], qTr[rows, bg, 32 * s:32 * s + 32],
                                    kcT[rows, bg * 4 + s, :], start=True, stop=True)
            ins.then_inc(sc_done, 1)
            pe.wait_ge(sc_exp, 1)
            for j in range(4):
                pe.transpose(bank(4)[:, j * P:(j + 1) * P], s_smp[:, j, 0:P], ident[:, :])
                ins = pe.transpose(bank(5)[0:NS, j * P:(j + 1) * P], s_smp[:, j, P:P + NS], ident[:, :])
            ins.then_inc(pT_done, 1)
            pe.wait_ge(pT_out, 2)
            heads_T(1)
            pe.wait_ge(gu_out, TILES)
            pe.wait_ge(gv_out, TILES)
            for j in range(4):
                kv, bg = j // 2, j % 2
                o = bank(2)[:, j * HD:(j + 1) * HD]
                pe.matmul(o, pTn[0:NS, j, :], proj(0, 640 + kv * HD, 640 + (kv + 1) * HD)[0:NS],
                          start=True, stop=False, skip_group_check=True)
                for s in range(4):
                    ins = pe.matmul(o[32 * s:32 * s + 32], pTc[:, j, 32 * s:32 * s + 32],
                                    vc[:, bg * 4 + s, kv * HD:(kv + 1) * HD], start=False, stop=(s == 3),
                                    skip_group_check=True)
            ins.then_inc(pv_done, 1)
            pe.wait_ge(so_exp, 1)
            for kv in range(KV):
                for bg in range(2):
                    ins = pe.matmul(bank(3)[:, kv * 256:(kv + 1) * 256], v3(gather[:, :], 2)[:, bg, :],
                                    o_exp[:, kv * 2 + bg, :], start=(bg == 0), stop=(bg == 1))
            ins.then_inc(so_done, 1)

            def out_half(t, c):
                return product(bank(6 + c), lambda k: xTv[:, k, t * P:(t + 1) * P],
                               lambda k: w_out[:, k, c * 512:(c + 1) * 512])

            def merged_T(t):
                if t > 0:
                    pe.wait_ge(x1_out, t)
                transposes(N_MRG + t)

            for t in range(1, TILES):
                lo = P if t == 1 else 0
                pe.wait_ge(qkT_out, 2 * t + 2)
                pe.wait_ge(attn_out, t)
                for h in range(HEADS):
                    rows = slice(64 * (h // 4), 64 * (h // 4) + 64)
                    ins = pe.matmul(ps[:, h * 256 + lo:(h + 1) * 256], qT[rows, h % 4, :],
                                    kT[rows, (t - 1) * P + lo:(t + 1) * P], start=True, stop=True)
                ins.then_inc(sc_done, 1)
                if t + 1 < TILES:
                    pe.wait_ge(sgu_out, t)
                    heads_T(t + 1)
                merged_T(t - 1)
                pe.wait_ge(xT_ready, N_MRG + t)
                if t == 1:
                    pe.wait_ge(ld_wout, 16)
                out_half(t - 1, 0)
                out_half(t - 1, 1).then_inc(wo_done, 1)
                pe.wait_ge(qkT_out, 2 * min(t + 2, TILES))
                gating(t, bank(5))
                pe.wait_ge(sc_exp, t + 1)
                for h in range(HEADS):
                    for c in range(2):
                        if c * P >= lo:
                            ins = pe.transpose(ps[:, (c * 8 + h) * P:(c * 8 + h + 1) * P],
                                               s_sb[:, h, c * P:(c + 1) * P], ident[:, :])
                ins.then_inc(pT_done, 1)
                pe.wait_ge(pT_out, 2 * t + 1)
                for h in range(HEADS):
                    kv = h // 4
                    for c in range(2):
                        if c * P < lo:
                            continue
                        vt = t - 1 + c
                        ins = pe.matmul(bank(0)[:, h * HD:(h + 1) * HD], pT[:, c * 8 + h, :],
                                        proj(vt, 640 + kv * HD, 640 + (kv + 1) * HD),
                                        start=(c * P == lo), stop=(c == 1))
                ins.then_inc(pv_done, 1)
            merged_T(TILES - 1)
            pe.wait_ge(xT_ready, N_MRG + TILES)
            out_half(TILES - 1, 0)
            transposes(N_CRS)
            out_half(TILES - 1, 1).then_inc(wo_done, 1)
            for t in range(1, TILES):
                transposes(N_CRS + t)

            pe.wait_ge(ld_wc, 16)
            pe.wait_ge(xT_ready, N_CRS + TILES)
            for c in range(2):
                product(bank(2 * c), lambda k: w_cq[:, k, c * P:(c + 1) * P], lambda k: xTv[:, k, 0:512])
                product(bank(2 * c + 1)[:, 0:P], lambda k: w_cq[:, k, c * P:(c + 1) * P],
                        lambda k: xTv[:, k, 512:640]).then_inc(qc_done, 1)
            pe.wait_ge(ld_mcache, 16 * 16)
            for g in range(4):
                if g >= 2:
                    pe.wait_ge(kmT_out, g - 1)
                for b in range(2):
                    for c in range(2):
                        for j in range(2):
                            o = (4 + 2 * (g % 2)) * 512 + (b * 2 + c) * 256 + j * P
                            ins = pe.transpose(ps[:, o:o + P], kmem[:, 2 * g + b, j, c * P:(c + 1) * P], ident[:, :])
                ins.then_inc(kmT_done, 1)
            pe.wait_ge(qc_out, 6)
            pe.wait_ge(qbd_out, 1)
            pe.wait_ge(kmT_out, 4)
            for b in range(SAMPLES):
                for c in range(2):
                    ins = pe.matmul(bank(0)[32 * (b % 4):32 * (b % 4) + 32, (b // 4) * 256:(b // 4 + 1) * 256],
                                    q_bd[:, c, b * 32:(b + 1) * 32], kmT[:, b, c, :], start=(c == 0), stop=(c == 1))
            ins.then_inc(c_sc, 1)
            pe.wait_ge(c_exp, 2)
            for bg in range(2):
                for c in range(2):
                    ins = pe.transpose(bank(2)[:, (bg * 2 + c) * P:(bg * 2 + c + 1) * P],
                                       s_c[:, bg, c * P:(c + 1) * P], ident[:, :])
            ins.then_inc(c_pT, 1)
            pe.wait_ge(c_pTo, 1)
            for b in range(SAMPLES):
                r = 32 * (b % 4)
                for c in range(2):
                    ins = pe.matmul(bank(4)[r:r + 32, (b // 4) * 256:(b // 4 + 1) * 256],
                                    pT_c[:, (b // 4) * 2 + c, r:r + 32], vmem[:, b, c, :], start=(c == 0),
                                    stop=(c == 1))
            ins.then_inc(c_pv, 1)
            pe.wait_ge(ld_sk, 16)
            for n in range(16):
                ins = pe.transpose(ps[:, n * P:(n + 1) * P], sk_raw[:, n, :], ident[:, :])
            ins.then_inc(skT_done, 1)
            pe.wait_ge(c_om, 1)
            for bg in range(2):
                ins = pe.matmul(bank(5)[:, 256:512], v3(gather[:, :], 2)[:, bg, :], o_m[:, bg, :],
                                start=(bg == 0), stop=(bg == 1))
            ins.then_inc(c_sel, 1)
            pe.wait_ge(c_o, 1)
            for c in range(2):
                ins = pe.transpose(bank(5)[:, c * P:(c + 1) * P], o_c[:, c * P:(c + 1) * P], ident[:, :])
            ins.then_inc(c_oT, 1)
            pe.wait_ge(c_oTo, 1)
            pe.wait_ge(ld_wco, 16)
            for c in range(2):
                ins = product(bank(6 + c), lambda k: oT_c[:, k, :], lambda k: w_co[:, k, c * 512:(c + 1) * 512], 2)
            ins.then_inc(c_wo, 1)

            def ffn(t, part):
                if part < 2:
                    return
                h = part - 2
                pe.wait_ge(xn_ready, t + 1)
                if 2 * t + h > 0:
                    pe.wait_ge(f_out, 2 * t + h)
                for k in range(4):
                    ins = pe.transpose(bank(7)[:, k * P:(k + 1) * P],
                                       xn[:, t * D + (4 * h + k) * P:t * D + (4 * h + k + 1) * P], ident[:, :])
                ins.then_inc(f_tr, 1)

            def cross(t, step):
                n = t - 1
                if step < 2:
                    if step == 0:
                        pe.wait_ge(f_out, 2 if t == 1 else 4)
                        if n > 0:
                            pe.wait_ge(l_add, 2 * n)
                    else:
                        pe.wait_ge(l_exp, 4 * n + 2)
                    rows = slice(64 * step, 64 * step + 64)
                    for c in range(2):
                        ins = pe.matmul(bank(7)[:, c * 256:(c + 1) * 256], qcT_l[rows, 4 * c + n, :], mkT[rows, c, :],
                                        start=True, stop=True)
                    ins.then_inc(l_sc, 1)
                elif step < 4:
                    if step == 2:
                        pe.wait_ge(l_exp, 4 * n + 4)
                    else:
                        pe.wait_ge(l_pTo, 2 * n + 1)
                    for i in range(4):
                        ins = pe.transpose(bank(7)[:, i * P:(i + 1) * P],
                                           s_c[:, 2 * step - 4 + i // 2, (i % 2) * P:(i % 2 + 1) * P], ident[:, :])
                    ins.then_inc(l_pT, 1)
                elif step == 4:
                    pe.wait_ge(l_pTo, 2 * n + 2)
                    pe.wait_ge(mv_moved, 1)
                    for i in range(MHEADS):
                        h = 2 * (i % 2) + i // 2
                        for c in range(2):
                            ins = pe.matmul(bank(7)[:, i * HD:(i + 1) * HD], pT_l[:, i * 2 + c, :],
                                            mv_l[:, c, h * HD:(h + 1) * HD], start=(c == 0), stop=(c == 1))
                    ins.then_inc(l_pv, 1)
                elif step == 5:
                    pe.wait_ge(l_o, n + 1)
                    for c in range(2):
                        ins = pe.transpose(bank(7)[:, c * P:(c + 1) * P], o_l[:, c * P:(c + 1) * P], ident[:, :])
                    ins.then_inc(l_oT, 1)
                else:
                    c = step - 6
                    if c == 0:
                        pe.wait_ge(l_oTo, n + 1)
                    else:
                        pe.wait_ge(l_add, 2 * n + 1)
                    product(bank(7), lambda k: oT_l[:, k, :], lambda k: w_co[:, k, c * 512:(c + 1) * 512], 2)\
                        .then_inc(l_wo, 1)

            pe.wait_ge(x2_out, 1)
            ffn(0, 2)
            ffn(0, 3)

            pe.wait_ge(ld_wpq, 16)
            pe.wait_ge(skT_out, 1)

            def heads_of(s):
                return (s, s + 4) if isinstance(s, int) and s < 4 else (tile_head(s)[1],)

            def q_mm(s, m):
                pe.wait_ge(xTcur_ready, s + 1)
                if not isinstance(s, int) or s > 0:
                    pe.wait_ge(pq_qo, s)
                for j, h in enumerate(heads_of(s)):
                    for k in range(KD):
                        rhs = w_pq[:, k, h * 256:(h + 1) * 256] if isinstance(h, int) else w_pq[:, k, bass.ds(h * 256, 256)]
                        ins = pe.matmul(bank(4)[:, j * 256:(j + 1) * 256], xT_cur[m % 2][:, k, :], rhs,
                                        start=(k == 0), stop=(k == KD - 1))
                ins.then_inc(pq_q, 1)

            def q_T(s):
                pe.wait_ge(pq_qo, s + 1)
                if not isinstance(s, int) or s > 0:
                    pe.wait_ge(pq_to, s)
                for j in range(2 * len(heads_of(s))):
                    ins = pe.transpose(bank(5)[:, j * P:(j + 1) * P], q_sb[:, j * P:(j + 1) * P], ident[:, :])
                ins.then_inc(pq_t, 1)

            def scores(s):
                pe.wait_ge(pq_to, s + 1)
                if not isinstance(s, int) or s > 0:
                    pe.wait_ge(pq_so, s)
                hs = heads_of(s)
                for j, h in enumerate(hs):
                    r = slice(0, P) if len(hs) == 1 else slice(j * NS, (j + 1) * NS)
                    for c in range(2):
                        rhs = (skT[:, (2 * h + c) * P:(2 * h + c + 1) * P] if isinstance(h, int)
                               else skT[:, bass.ds(h * 256 + c * P, P)])
                        ins = pe.matmul(bank(6)[r, c * P:(c + 1) * P], qT_sb[:, 2 * j + c, r], rhs, start=True, stop=True)
                ins.then_inc(pq_s, 1)

            for s in range(2):
                q_mm(s, s)
                q_T(s)
                scores(s)

            def experts(b, m, k0, k1):
                q = 2 * ((m + 1) % 2)
                if k0 == 0 and (not isinstance(b, int) or b >= 3):
                    pe.wait_ge(acc_added, b - 2)
                for k in range(k0, k1):
                    pe.wait_ge(diag_ready, b * TOPK + (k + 1 - TOPK))
                    pe.wait_ge(v_landed[k % RING], b * 64 + 16 * (k // RING + 1) - 64)
                    for c in range(2):
                        ins = pe.matmul(bank(q + c), diag[:, k % RING, :], v_ring[k % RING][:, c * 512:(c + 1) * 512],
                                        start=(k == 0), stop=(k == TOPK - 1))
                    ins.then_inc(v_used, 1)

            def one(b, m, u, v):
                more = u and not (isinstance(b, int) and b + 2 >= BLOCKS)
                if more:
                    q_mm(b + 2, m + 2)
                for k in range(TOPK):
                    if v:
                        experts(b, m, k, k + 1)
                    if more and k == 1:
                        q_T(b + 2)
                    if more and k == 3:
                        scores(b + 2)
                    beside(b, k, cross, ffn)

            run_blocks(pe, one)


CHAIN_PER_BLOCK = 19

_INS = ['x_prompt', 'x_sample', 'mem_prompt', 'cache_swa_k', 'cache_swa_v', 'cache_mem_k', 'cache_mem_v',
        'g_mix', 'w_in', 'attn_sinks', 'g_sgu', 'w_spatial', 'b_spatial', 'g_attn_out', 'g_gmlp_out', 'w_out',
        'g_cross', 'g_mem', 'w_cq', 'w_mk', 'w_mv', 'w_co', 'g_ffn', 'w_peer_q', 'peer_sub_keys', 'peer_u',
        'peer_v', 'g_final']
_OUTS = {"y_p": (1, 512, D), "y_s": (8, 8, D), "swa_k_p": (1, 1, P, KV, HD), "swa_v_p": (1, 1, P, KV, HD),
         "mem_k": (1, 1, NMEM, MHEADS, HD), "mem_v": (1, 1, NMEM, MHEADS, HD),
         "swa_k_s": (1, 8, P, KV, HD), "swa_v_s": (1, 8, P, KV, HD), "sgu_v": (1, 8, 8, HEADS, HD)}


def kernel(**inputs):
    import concourse.bacc as _bacc
    from concourse.bass_utils import run_bass_kernel_spmd as _run

    nc = _bacc.Bacc("TRN2", target_bir_lowering=False, num_devices=1)
    arrays, I, O = {}, {}, {}
    for name in _INS:
        a = np.ascontiguousarray(inputs[name])
        arrays[f"in_{name}"] = a
        I[name] = nc.dram_tensor(f"in_{name}", a.shape, F32, kind="ExternalInput").ap()
    for name, a in shape_tables().items():
        arrays[f"tab_{name}"] = a
        I["tab_" + name] = nc.dram_tensor(f"tab_{name}", a.shape, F32, kind="ExternalInput").ap()
    for name, shape in _OUTS.items():
        O[name] = nc.dram_tensor(f"out_{name}", shape, F32, kind="ExternalOutput").ap()
    hybrid_step(nc, I, O)
    r = _run(nc, [arrays], core_ids=[0])
    return tuple(r.results[0][f"out_{name}"] for name in _OUTS)
```

```python
from contextlib import ExitStack

import numpy as np

import concourse.bass as bass
from concourse import mybir

F32 = mybir.dt.float32
BF16 = mybir.dt.bfloat16
U32 = mybir.dt.uint32
ALU = mybir.AluOpType
ACT = mybir.ActivationFunctionType
AX_X = mybir.AxisListType.X

P = 128
D = 1024
KD = D // P
TILES = 5
NTOK = TILES * P
SAMPLES, SAMPLE_LEN = 8, 8
NS = SAMPLES * SAMPLE_LEN
PAST = 1024
HD = 64
HEADS, KV, GROUP = 8, 2, 4
NMEM = 256
MHEADS = 4
PHEADS, NKEYS, TOPK = 8, 128, 16
EPS = 1e-6
NEG = -1e30
LOWEST = -3.4028235e38
BLOCKS = 4 + 4 * PHEADS
RING = 4
INW = 1792


def shape_tables():
    t = {}
    r = np.arange(P)
    t["ident"] = np.eye(P)
    c = np.arange(2 * P)
    t["band"] = np.where((c[None] > r[:, None]) & (c[None] <= r[:, None] + P), 0.0, NEG)
    t["eps"] = np.full((P, 1), EPS)
    t["iota"] = np.broadcast_to(np.arange(TOPK), (P, TOPK))
    seq, head, tok = r // 32, (r // 8) % 4, r % 8
    t["headsel"] = (head[:, None] == np.arange(4)[None]) * 1.0
    gather = np.zeros((P, 2, P))
    for bg in range(2):
        for m in range(P):
            gather[:, bg, m] = ((bg * 4 + seq) * 8 + tok) == m % NS
    t["gather"] = gather.reshape(P, 2 * P)
    half = HD // 2
    inv = np.float32(10000.0) ** (-np.arange(half, dtype=np.float32) / np.float32(half))
    pos = np.stack([PAST + r % 8] + [i * P + r for i in range(TILES - 1)], 1).astype(np.float32)
    ang = pos[:, :, None] * inv[None, None, :].astype(np.float32)
    rot = np.concatenate([np.cos(ang), np.cos(ang), -np.sin(ang), np.sin(ang)], -1)
    t["rot"] = rot.reshape(P, TILES * 4 * half)
    sm = np.full((P, 2, P + NS), NEG)
    for bg in range(2):
        key = np.arange(P)
        sm[:, bg, :P] = np.where(key[None] > tok[:, None], 0.0, NEG)
        new = np.arange(NS)
        ok = (new[None] // 8 == (bg * 4 + seq)[:, None]) & (new[None] % 8 <= tok[:, None])
        sm[:, bg, P:] = np.where(ok, 0.0, NEG)
    t["smask"] = sm.reshape(P, 2 * (P + NS))
    t["blocks"] = ((r[:, None] // 8 == r[None] // 8) & (r[None] % 8 <= r[:, None] % 8)) * 1.0
    t["tril"] = np.tril(np.ones((P, P)))
    t["fold"] = (r[:, None] % NS == r[None] % NS) * 1.0
    return {k: np.ascontiguousarray(v, dtype=np.float32) for k, v in t.items()}


def hybrid_step(nc, I, O):
    ctx = ExitStack()
    with ctx:
        def sb(name, n, dt=F32):
            return ctx.enter_context(nc.sbuf_tensor(name, [P, n], dt))

        def sem(name):
            return ctx.enter_context(nc.semaphore(name))

        x_res = sb("x_res", TILES * D)
        xT = sb("xT", KD * NTOK)
        A = sb("A", 16384)
        R = sb("R", 24960)
        ident = sb("ident", P)
        band = sb("band", 2 * P)
        eps = sb("eps", 1)
        iota = sb("iota", TOPK)
        headsel = sb("headsel", 4)
        gather = sb("gather", 2 * P)
        g_sgu = sb("g_sgu", 512)
        gains = sb("gains", 48)
        sinks = sb("sinks", HEADS)
        sinks_s = sb("sinks_s", KV)
        bias_p, bias_s = gains[:, 32:40], gains[:, 40:48]
        stat = sb("stat", 112)
        ps = ctx.enter_context(nc.psum_tensor("ps", [P, 8 * 512], F32))

        def bank(n, w=512, k=1):
            return ps[:, n * 512:n * 512 + w]

        def v3(ap, a):
            return ap.rearrange("p (a b) -> p a b", a=a)

        def xr(t):
            return x_res[:, bass.ds(t * D, D)] if not isinstance(t, int) else x_res[:, t * D:(t + 1) * D]

        xTv = v3(xT[:, :], KD)
        w_in = v3(A[:, 0:KD * INW], KD)
        rot = v3(A[:, 14336:14336 + TILES * P], TILES)
        tmp = A[:, 15872:16384]
        rows48 = A[0:48, 15000:15128]
        s_sb = v3(A[:, 0:2048], HEADS)
        pT = v3(A[:, 2048:4096], 16)
        qT = v3(A[:, 4096:4608], 4)
        wT_p = v3(A[:, 6144:7168], HEADS)
        wT_s = v3(A[:, 7168:8192], HEADS)
        kc = v3(R[:, 19200:20224], SAMPLES)
        vc = v3(A[:, 9216:10240], SAMPLES)
        kcT = v3(A[:, 10240:11264], SAMPLES)
        smask = v3(A[:, 11264:11648], 2)
        qTr = v3(A[:, 12352:12608], 2)
        s_smp = v3(A[:, 12608:13376], 4)
        pTc = v3(A[:, 13376:13888], 4)
        pTn = v3(A[:, 13888:14400], 4)
        o_exp = v3(A[:, 14400:15424], 4)
        w_pq = v3(A[:, :], KD)
        wsp = v3(R[:, 17152:18176], HEADS)
        w_smp = v3(R[:, 18176:19200], HEADS)
        tril = R[:, 20608:20736]
        blocks = R[:, 20736:20864]
        w8 = v3(R[:, 20864:20928], HEADS)
        w_out = v3(R[:, 0:8192], KD)
        PB = 8192

        def proj(t, a, b):
            return R[:, PB + t * INW + a:PB + t * INW + b]

        mem_x = v3(R[:, PB:PB + 2048], 2)
        mem_T = v3(R[:, PB + 2048:PB + 4096], KD)
        w_mk = v3(R[:, PB + 4096:PB + 6144], KD)
        w_mv = v3(R[:, PB + 6144:PB + 8192], KD)
        mk = v3(R[:, PB + 8192:PB + 8704], 2)
        w_cq = v3(R[:, 17152:19200], KD)
        mkT = v3(R[:, 21120:21632], 2)
        mv = v3(R[:, 21760:22272], 2)
        kT = R[:, 22272:22912]
        xs = [R[:, 22912:23936], R[:, 23936:24960]]
        kmT = A[:, 8192:12288].rearrange("p (b c k) -> p b c k", b=SAMPLES, c=2)
        s_c = v3(R[:, 4096:5120], MHEADS)
        s_cs = v3(A[:, 12544:13056], 2)
        pT_c = v3(A[:, 13056:13568], 4)
        qcT = v3(A[:, 12288:12544], 2)
        q_bd = v3(R[:, 22272:22784], 2)
        oT_c = v3(R[:, 7936:8192], 2)
        kmem = R[:, PB:PB + 4096].rearrange("p (b c k) -> p b c k", b=SAMPLES, c=2)
        vmem = R[:, PB + 4096:PB + 8192].rearrange("p (b c k) -> p b c k", b=SAMPLES, c=2)
        o_c = R[:, PB + 8192:PB + 8448]
        o_m = v3(R[:, PB + 8448:PB + 8960], 2)
        w_co = v3(R[:, 2048:4096], 2)
        pT_l = xTv[:, :, 2 * P:3 * P]
        qcT_l = xTv[:, :, 3 * P:4 * P]
        mv_l = v3(g_sgu[:, :], 2)
        oT_l = v3(band[:, :], 2)
        o_l = gather[:, :]
        xn = R[:, 0:5120]
        u_ring = [R[:, 5120 + i * D:5120 + (i + 1) * D] for i in range(RING)]
        v_ring = [R[:, 9216 + i * D:9216 + (i + 1) * D] for i in range(RING)]
        sk_raw = v3(R[:, 10240:12288], 16)
        y_out = [R[:, t * D:(t + 1) * D] for t in range(TILES)]
        skT = R[:, 13312:15360]
        xn_cur = [R[:, 15360 + i * D:15360 + (i + 1) * D] for i in range(2)]
        xT_cur = [v3(R[:, 17408 + i * D:17408 + (i + 1) * D], KD) for i in range(2)]
        g_ffn = g_fin = R[:, 19456:20480]
        fold = R[:, 20480:20608]
        diag = v3(R[:, 20608:21120], RING)
        ss = v3(R[:, 21632:21888], 2)
        ss2 = v3(R[:, 21888:22144], 2)
        cand = R[:, 22144:22400]
        onehot = R[:, 22400:22912]
        cand2 = R[:, 22912:23168]
        q_sb = R[:, 23168:23680]
        qT_sb = v3(R[:, 23680:24192], 4)
        idx = v3(R[:, 24192:24256].bitcast(U32), 4)
        gate = v3(R[:, 24256:24320], 4)
        topv = v3(R[:, 24320:24352], 2)
        topi = v3(R[:, 24352:24384].bitcast(U32), 2)
        bestv = R[:, 24384:24400]
        besti = R[:, 24400:24416].bitcast(U32)
        parts = v3(R[:, 24416:24448].bitcast(U32), 2)
        chosen = v3(R[:, 24448:24480], 2)
        hdot = v3(R[:, 24480:24512], 2)
        hgelu = v3(R[:, 24512:24544], 2)
        coef = v3(R[:, 24544:24576], 2)
        negtop = R[:, 24576:24577]
        esum = R[:, 24577:24578]
        rsum = R[:, 24578:24579]

        ssq = [stat[:, 0:2], stat[:, 2:4]]
        rstd = [stat[:, 4:6], stat[:, 6:8]]
        mx = stat[:, 8:16]
        nmx = stat[:, 16:24]
        rs = stat[:, 24:32]
        es = stat[:, 32:40]
        rden = stat[:, 40:48]
        gv_ss = stat[:, 48:56]
        gv_r = stat[:, 56:64]
        ssq_f = stat[:, 80:85]
        rstd_f = stat[:, 85:90]
        spread = stat[:, 96:112]

        ld_tab, ld_mem, ld_wmkv, ld_small = (sem(n) for n in ("ld_tab", "ld_mem", "ld_wmkv", "ld_small"))
        ld_x = [sem(f"ld_x{t}") for t in range(TILES)]
        ld_win = [sem(f"ld_win{c}") for c in range(4)]
        ld_wout, ld_wc, ld_swa, ld_gating, ld_wpq, ld_sk, ld_ffn, ld_fin = (
            sem(n) for n in ("ld_wout", "ld_wc", "ld_swa", "ld_gating", "ld_wpq", "ld_sk",
                             "ld_ffn", "ld_fin"))
        ld_kc = sem("ld_kc")
        ld_rot, ld_late = sem("ld_rot"), sem("ld_late")
        ld_rows, gT_done, gT_out = sem("ld_rows"), sem("gT_done"), sem("gT_out")
        stored, mem_stored = sem("stored"), sem("mem_stored")
        y_stored = sem("y_stored")
        std_ready = sem("std_ready")
        xs_ready = sem("xs_ready")
        tr_done = sem("tr_done")
        xT_ready = sem("xT_ready")
        chain_v = sem("chain_v")
        chain_a = sem("chain_a")
        mkv_done, mkv_out, mkT_done, mkT_out = (sem(n) for n in ("mkv_done", "mkv_out", "mkT_done", "mkT_out"))
        pq_done, pkv_done, pgu_done, pgv_done = (sem(n) for n in ("pq_done", "pkv_done", "pgu_done", "pgv_done"))
        q_out, kv_out, gu_out, gv_out = (sem(n) for n in ("q_out", "kv_out", "gu_out", "gv_out"))
        w_masked, wT_done, wT_out = (sem(n) for n in ("w_masked", "wT_done", "wT_out"))
        qkT_done, qkT_out = sem("qkT_done"), sem("qkT_out")
        kcT_done, kcT_out, qTr_out = sem("kcT_done"), sem("kcT_out"), sem("qTr_out")
        sc_done, sc_max, sc_exp, pT_done, pT_out, pv_done, attn_out = (
            sem(n) for n in ("sc_done", "sc_max", "sc_exp", "pT_done", "pT_out", "pv_done", "attn_out"))
        so_exp, so_done = sem("so_exp"), sem("so_done")
        gv_ssq, gv_std, gvn_out, mixed_done, sgu_out = (
            sem(n) for n in ("gv_ssq", "gv_std", "gvn_out", "mixed_done", "sgu_out"))
        wo_done, x1_out = sem("wo_done"), sem("x1_out")
        qc_done, qc_out, kmT_done, kmT_out, qbd_out, qbd_zero = (
            sem(n) for n in ("qc_done", "qc_out", "kmT_done", "kmT_out", "qbd_out", "qbd_zero"))
        c_sc, c_max, c_exp, c_pT, c_pTo, c_pv, c_o, c_oT, c_oTo, c_wo, x2_out = (
            sem(n) for n in ("c_sc", "c_max", "c_exp", "c_pT", "c_pTo", "c_pv", "c_o", "c_oT", "c_oTo",
                             "c_wo", "x2_out"))
        c_sel, c_om = sem("c_sel"), sem("c_om")
        ld_mcache_k, ld_mcache_v = sem("ld_mcache_k"), sem("ld_mcache_v")
        mv_moved, ld_wco = sem("mv_moved"), sem("ld_wco")
        l_sc, l_max, l_exp, l_pT, l_pTo, l_pv, l_o, l_oT, l_oTo, l_wo, l_add = (
            sem(n) for n in ("l_sc", "l_max", "l_exp", "l_pT", "l_pTo", "l_pv", "l_o", "l_oT", "l_oTo", "l_wo",
                             "l_add"))
        f_std, f_tr, f_out = sem("f_std"), sem("f_tr"), sem("f_out")
        skT_done, skT_out = sem("skT_done"), sem("skT_out")
        xn_ready = sem("xn_ready")
        xcur_ready, xTcur_ready = sem("xcur_ready"), sem("xTcur_ready")
        pq_q, pq_qo, pq_t, pq_to, pq_s, pq_so = (sem(n) for n in ("pq_q", "pq_qo", "pq_t", "pq_to", "pq_s", "pq_so"))
        best_ready, gexp_ready, idx_ready = sem("best_ready"), sem("gexp_ready"), sem("idx_ready")
        u_landed = [sem(f"u_landed{i}") for i in range(RING)]
        v_landed = [sem(f"v_landed{i}") for i in range(RING)]
        u_used, v_used = sem("u_used"), sem("v_used")
        gelu_ready, coef_ready, diag_ready, acc_added = (
            sem(n) for n in ("gelu_ready", "coef_ready", "diag_ready", "acc_added"))
        apart_v, apart_p = sem("apart_v"), sem("apart_p")
        fin_std, fin_y = sem("fin_std"), sem("fin_y")

        block = ctx.enter_context(nc.Block())

        N_MIX = 2
        N_MRG = (7, 8, 9, 10, 12)
        N_CRS = (11, 13, 14, 15, 16)
        G_MIX, G_MEM, G_MRG, G_CRS = range(4)
        STORES = []

        def chain_of(eng, s):
            state = [0, 0]

            def count(ins):
                ins.then_inc(s, 1)
                state[1] += 1

            def hold():
                eng.wait_ge(s, state[0] + state[1])

            def chain(ins):
                count(ins)
                hold()

            return chain, count, hold, state

        def run_blocks(eng, one):
            for b in range(5):
                one(b, b % 4, True, b >= 1)
            with eng.Fori(5, 30, 4) as b0:
                for j in range(4):
                    one(b0 + j, (5 + j) % 4, True, True)
            for b in range(33, BLOCKS + 1):
                one(b, b % 4, b < BLOCKS, True)

        def norm_bank(n):
            return 6 if n in N_MRG else 2 if n in N_CRS else 4 + 2 * (n % 2)

        CROSS_SLOT = (4, 5, 6, 7, 9, 10, 11, 12)
        FFN_SLOT = {(1, 0): 1, (4, 0): 2, (4, 4): 3, (4, 8): 4}

        def beside(b, k, step, ffn):
            if not isinstance(b, int) or b > 4:
                return
            if b < 4 and k in CROSS_SLOT:
                step(b + 1, CROSS_SLOT.index(k))
            for (fb, fk), t in FFN_SLOT.items():
                if fb == b and fk <= k < fk + 4:
                    ffn(t, k - fk)

        def km_bank(g):
            return 4 if g % 2 == 0 else 2

        def tile_head(b):
            return (b + 4) // 8, (b + 4) % 8

        @block.sync
        def _(sp):
            def load(dst, src, s):
                sp.dma_start(dst, src).then_inc(s, 16)

            def store(dst, src):
                STORES.append(1)
                sp.dma_start(dst, src).then_inc(stored, 16)

            load(ident[:, :], I["tab_ident"][:, :], ld_tab)
            load(eps[:, :], I["tab_eps"][:, :], ld_tab)
            load(mem_x, I["mem_prompt"][0].rearrange("(t p) d -> p t d", p=P), ld_mem)
            for row, name in ((8 * G_MIX, "g_mix"), (8 * G_MEM, "g_mem"), (8 * G_MRG, "g_attn_out"),
                              (8 * G_MRG + 4, "g_gmlp_out"), (8 * G_CRS, "g_cross")):
                src = I[name][0].rearrange("(k p) -> k p", p=P)
                load(rows48[row:row + src.shape[0]], src, ld_rows)
            load(rows48[32:40], I["b_spatial"][0], ld_rows)
            load(rows48[40:48].rearrange("h (c t) -> h c t", t=8),
                 I["b_spatial"][0, :, 0:8].unsqueeze(1).broadcast_to([HEADS, 16, 8]), ld_rows)
            load(w_mk, I["w_mk"][0].rearrange("(k p) n -> p k n", p=P), ld_wmkv)
            load(w_mv, I["w_mv"][0].rearrange("(k p) n -> p k n", p=P), ld_wmkv)
            flat = I["x_sample"].rearrange("a b d -> (a b) d")
            load(xr(0)[0:NS], flat, ld_x[0])
            load(xr(0)[NS:P], flat, ld_x[0])
            win = I["w_in"][0].rearrange("(k p) n -> p k n", p=P)
            for c, (a, b) in enumerate(((0, 512), (512, 768), (768, 1280), (1280, 1792))):
                load(w_in[:, :, a:b], win[:, :, a:b], ld_win[c])
                if c == 0:
                    load(xr(1), I["x_prompt"][0, 0:P, :], ld_x[1])
                    load(rot, v3(I["tab_rot"][:, :], TILES), ld_rot)
            for t in range(2, TILES):
                load(xr(t), I["x_prompt"][0, (t - 1) * P:t * P, :], ld_x[t])
            for name, dst in (("band", band), ("iota", iota), ("headsel", headsel), ("gather", gather)):
                load(dst[:, :], I["tab_" + name][:, :], ld_late)
            load(wsp, I["w_spatial"][0].rearrange("h t r -> t h r"), ld_gating)
            load(tril, I["tab_tril"][:, :], ld_gating)
            load(blocks, I["tab_blocks"][:, :], ld_gating)
            for c in range(2 * SAMPLES):
                load(w8[c * 8:(c + 1) * 8], I["w_spatial"][0, :, 0:8, 0:8].rearrange("h t r -> t h r"), ld_gating)
            load(kc, I["cache_swa_k"][0].rearrange("b w h d -> w b (h d)"), ld_kc)
            load(w_out, I["w_out"][0].rearrange("(k p) n -> p k n", p=P), ld_wout)
            load(fold, I["tab_fold"][:, :], ld_ffn)
            for name in ("k", "v"):
                store(O[f"swa_{name}_s"][0, :, 0:P - SAMPLE_LEN].rearrange("b w h d -> b (w h d)"),
                      I[f"cache_swa_{name}"][0, :, SAMPLE_LEN:P].rearrange("b w h d -> b (w h d)"))
            sp.wait_ge(mkv_out, 4)
            for j in range(2):
                for name, rows in (("mem_k", mk), ("mem_v", mv)):
                    sp.dma_start(O[name][0, 0, j * P:(j + 1) * P].rearrange("m h d -> m (h d)"), rows[:, j, :])\
                      .then_inc(mem_stored, 16)
            sp.wait_ge(pgv_done, TILES)
            sp.wait_ge(kv_out, TILES)
            load(vc, I["cache_swa_v"][0].rearrange("b w h d -> w b (h d)"), ld_swa)
            load(smask, v3(I["tab_smask"][:, :], 2), ld_swa)
            sp.wait_ge(kcT_done, 1)
            load(g_ffn, I["g_ffn"][0:1, :].broadcast_to([P, D]), ld_ffn)
            sp.wait_ge(wT_done, 1)
            load(w_cq, I["w_cq"][0].rearrange("(k p) n -> p k n", p=P), ld_wc)
            for name, a in (("k", 512), ("v", 640)):
                store(O[f"swa_{name}_p"][0, 0].rearrange("w h d -> w (h d)"), proj(TILES - 1, a, a + P))
                for b in range(SAMPLES):
                    store(O[f"swa_{name}_s"][0, b, P - SAMPLE_LEN:P].rearrange("w h d -> w (h d)"),
                          proj(0, a, a + P)[b * 8:(b + 1) * 8])
            sp.wait_ge(gvn_out, 1)
            store(O["sgu_v"][0].rearrange("b t h d -> (b t) (h d)"), proj(0, 1280, 1792)[0:NS])
            sp.wait_ge(xs_ready, N_MRG[TILES - 1] + 1)
            sp.wait_ge(stored, 16 * len(STORES))
            sp.wait_ge(mem_stored, 16 * 4)
            for name, rows in (("k", kmem), ("v", vmem)):
                for b in range(SAMPLES):
                    load(rows[:, b], I[f"cache_mem_{name}"][0, b].rearrange("(c p) h d -> p c (h d)", p=P),
                         ld_mcache_k if name == "k" else ld_mcache_v)
            sp.wait_ge(sgu_out, TILES)
            sp.wait_ge(attn_out, TILES)
            wpq = I["w_peer_q"][0].rearrange("(k p) n -> p k n", p=P)
            load(w_pq[:, 0:4], wpq[:, 0:4], ld_wpq)
            sp.wait_ge(kmT_done, 4)
            load(sk_raw, I["peer_sub_keys"][0].rearrange("h c k d -> k (h c) d"), ld_sk)
            sp.wait_ge(wo_done, TILES)
            load(w_co, I["w_co"][0].rearrange("(k p) n -> p k n", p=P), ld_wco)
            sp.wait_ge(c_pv, 1)
            load(w_pq[:, 4:8], wpq[:, 4:8], ld_wpq)
            sp.wait_ge(xn_ready, TILES)
            load(g_fin, I["g_final"].rearrange("(a d) -> a d", a=1).broadcast_to([P, D]), ld_fin)
            for t in range(TILES):
                sp.wait_ge(fin_y, t + 1)
                if t == 0:
                    dst, src = O["y_s"].rearrange("a b d -> (a b) d"), y_out[0][0:NS]
                else:
                    dst, src = O["y_p"][0, (t - 1) * P:t * P], y_out[t]
                sp.dma_start(dst, src).then_inc(y_stored, 16)
            sp.wait_ge(y_stored, 16 * TILES)

        @block.gpsimd
        def _(pool):
            def small(dst, src):
                pool.dma_start(dst, src).then_inc(ld_small, 16)

            small(g_sgu[:, :], I["g_sgu"].rearrange("a h d -> a (h d)").broadcast_to([P, 512]))
            small(sinks[:, :], I["attn_sinks"][0:1, :].broadcast_to([P, HEADS]))
            pool.wait_ge(sc_done, TILES)
            pool.memset(q_bd, 0.0).then_inc(qbd_zero, 1)

            def gather_v(b, m, k):
                if k >= RING or not isinstance(b, int) or b > 1:
                    pool.wait_ge(v_used, b * TOPK + (k - RING + 1 - TOPK))
                pool.sem_inc(apart_p, 1)
                pool.indirect_dma_start(
                    v_ring[k % RING], None, I["peer_v"][0],
                    bass.IndirectOffsetOnAxis(ap=idx[:, (m + 3) % 4, k:k + 1], axis=0)).then_inc(v_landed[k % RING], 16)

            def gathers(b, m, u, v):
                if u:
                    pool.wait_ge(idx_ready, b + 1)
                for k in range(TOPK):
                    i = k % RING
                    if u:
                        if k >= RING or not isinstance(b, int) or b > 0:
                            pool.wait_ge(u_used, b * TOPK + (k - RING + 1))
                        pool.sem_inc(apart_p, 1)
                        pool.indirect_dma_start(
                            u_ring[i], None, I["peer_u"][0],
                            bass.IndirectOffsetOnAxis(ap=idx[:, m, k:k + 1], axis=0)).then_inc(u_landed[i], 16)
                    if v and not (isinstance(b, int) and b == 1 and k < RING):
                        gather_v(b, m, k)
                    if isinstance(b, int) and b == 0 and k == RING - 1:
                        for first in range(RING):
                            gather_v(1, 1, first)

            pool.wait_ge(skT_out, 1)
            run_blocks(pool, gathers)

        @block.scalar
        def _(act):
            chain, count, hold, _ = chain_of(act, chain_a)

            def norm(n, src, parts=((0, D),)):
                if n >= 2:
                    act.wait_ge(tr_done, n - 1)
                for j, (a, b) in enumerate(parts):
                    ins = act.activation(xs[n % 2][:, a:b], src[j], ACT.Square, accum_out=ssq[n % 2][:, j:j + 1])
                    count(ins)
                hold()
                w = len(parts)
                act.activation(ssq[n % 2][:, 0:w], ssq[n % 2][:, 0:w], ACT.Sqrt, bias=eps[:, 0:1],
                               scale=1.0 / (parts[0][1] - parts[0][0])).then_inc(std_ready, 1)

            act.wait_ge(ld_mem, 16)
            act.wait_ge(ld_tab, 32)
            for j in range(2):
                norm(j, [mem_x[:, j, :]])
            act.wait_ge(gT_done, 1)
            act.activation(gains[:, :], bank(3)[:, 0:48], ACT.Copy).then_inc(gT_out, 1)

            def mix_norm(t):
                act.wait_ge(ld_x[t], 32 if t == 0 else 16)
                norm(N_MIX + t, [xr(t)])

            def mem_out(j):
                act.wait_ge(mkv_done, j + 1)
                act.activation(mk[:, j, :], bank(j)[:, 0:256], ACT.Copy).then_inc(mkv_out, 1)
                act.activation(mv[:, j, :], bank(j)[:, 256:512], ACT.Copy).then_inc(mkv_out, 1)

            def proj_out(t):
                act.wait_ge(pgu_done, t + 1)
                if t == TILES - 1:
                    act.wait_ge(mem_stored, 16 * 4)
                act.activation(proj(t, 768, 1280), bank(2), ACT.Gelu).then_inc(gu_out, 1)
                act.wait_ge(pgv_done, t + 1)
                act.activation(proj(t, 1280, 1792), bank(3), ACT.Gelu).then_inc(gv_out, 1)

            mix_norm(0)
            mem_out(0)
            mix_norm(1)
            mem_out(1)
            for t in range(TILES):
                if t == 0:
                    act.wait_ge(mkT_done, 1)
                    act.activation(mkT[:, :, :], v3(bank(3), 2), ACT.Copy).then_inc(mkT_out, 1)
                if t + 2 < TILES:
                    mix_norm(t + 2)
                proj_out(t)

            def gating_std(t):
                act.wait_ge(gv_ssq, t + 1)
                act.activation(gv_ss, gv_ss, ACT.Sqrt, bias=eps[:, 0:1], scale=1.0 / HD).then_inc(gv_std, 1)

            def qkT_evac(t):
                act.wait_ge(qkT_done, t + 1)
                q = 2 if t == 0 else 4
                act.activation(kT[:, t * P:(t + 1) * P], bank(q + 1)[:, 0:P], ACT.Copy).then_inc(qkT_out, 1)
                act.activation(qT, v3(bank(q), 4), ACT.Copy).then_inc(qkT_out, 1)

            act.wait_ge(kcT_done, 1)
            act.activation(kcT, ps[:, 0:1024].rearrange("p (b k) -> p b k", b=SAMPLES), ACT.Copy).then_inc(kcT_out, 1)
            qkT_evac(0)
            gating_std(0)
            act.wait_ge(wT_done, 1)
            act.activation(wT_p, ps[:, 2048:3072].rearrange("p (h t) -> p h t", h=HEADS), ACT.Copy).then_inc(wT_out, 1)
            act.activation(wT_s, ps[:, 3072:4096].rearrange("p (h t) -> p h t", h=HEADS), ACT.Copy).then_inc(wT_out, 1)

            act.wait_ge(sc_max, 1)
            for j in range(4):
                act.activation(s_smp[:, j, :], s_smp[:, j, :], ACT.Exp, bias=nmx[:, j:j + 1],
                               accum_out=rs[:, j:j + 1])
            act.activation(es[:, 0:4], es[:, 0:4], ACT.Exp).then_inc(sc_exp, 1)
            act.wait_ge(pT_done, 1)
            act.activation(pTc, v3(bank(4), 4), ACT.Copy).then_inc(pT_out, 1)
            act.activation(pTn[0:NS], v3(bank(5), 4)[0:NS], ACT.Copy).then_inc(pT_out, 1)
            act.wait_ge(qTr_out, 1)
            qkT_evac(1)
            gating_std(1)

            def merged_norm(t):
                act.wait_ge(attn_out, t + 1)
                act.wait_ge(sgu_out, t + 1)
                norm(N_MRG[t], [proj(t, 0, 512), proj(t, 768, 1280)], ((0, 512), (512, 1024)))

            def cross_norm(t):
                act.wait_ge(x1_out, t + 1)
                norm(N_CRS[t], [xr(t)])

            merged_norm(0)
            for t in range(1, TILES):
                if t + 1 < TILES:
                    qkT_evac(t + 1)
                act.wait_ge(sc_max, t + 1)
                lo = P if t == 1 else 0
                for h in range(HEADS):
                    act.activation(s_sb[:, h, lo:], s_sb[:, h, lo:], ACT.Exp, bias=nmx[:, h:h + 1],
                                   accum_out=rs[:, h:h + 1])
                act.activation(es, es, ACT.Exp).then_inc(sc_exp, 1)
                if t + 1 < TILES:
                    gating_std(t + 1)
                act.wait_ge(pT_done, t + 1)
                act.activation(pT[:, 8:16, :], ps[:, 1024:2048].rearrange("p (a b) -> p a b", a=8), ACT.Copy)\
                   .then_inc(pT_out, 1)
                if t == TILES - 1:
                    cross_norm(0)
                merged_norm(t)
            cross_norm(1)
            act.wait_ge(qc_done, 1)
            act.activation(qcT, v3(bank(1)[:, 0:256], 2), ACT.Copy).then_inc(qc_out, 1)
            for g in range(4):
                act.wait_ge(kmT_done, g + 1)
                act.activation(kmT[:, 2 * g:2 * g + 2], ps[:, km_bank(g) * 512:(km_bank(g) + 2) * 512]
                               .rearrange("p (b c k) -> p b c k", b=2, c=2), ACT.Copy).then_inc(kmT_out, 1)
            cross_norm(2)
            act.wait_ge(c_max, 1)
            for bg in range(2):
                act.activation(s_cs[:, bg, :], bank(0)[:, bg * 256:(bg + 1) * 256], ACT.Exp,
                               bias=nmx[:, bg:bg + 1], scale=0.125, accum_out=rs[:, bg:bg + 1]).then_inc(c_exp, 1)
            act.wait_ge(c_pT, 1)
            act.activation(pT_c, v3(bank(1), 4), ACT.Copy).then_inc(c_pTo, 1)
            cross_norm(3)
            act.wait_ge(skT_done, 1)
            act.activation(v3(skT, 4), v3(ps[:, 0:2048], 4), ACT.Copy).then_inc(skT_out, 1)
            cross_norm(4)
            act.wait_ge(c_oT, 1)
            act.activation(oT_c, v3(bank(5)[:, 0:256], 2), ACT.Copy).then_inc(c_oTo, 1)
            act.activation(mv_l, mv, ACT.Copy).then_inc(mv_moved, 1)

            def ffn(t, part):
                if part == 0:
                    act.wait_ge(*((x2_out, 1) if t == 0 else (l_add, 2 * t)))
                    chain(act.activation(xn[:, t * D:(t + 1) * D], xr(t), ACT.Square,
                                         accum_out=ssq_f[:, t:t + 1]))
                    act.activation(ssq_f[:, t:t + 1], ssq_f[:, t:t + 1], ACT.Sqrt, bias=eps[:, 0:1],
                                   scale=1.0 / D).then_inc(f_std, 1)
                elif part >= 2:
                    h = part - 2
                    act.wait_ge(f_tr, 2 * t + h + 1)
                    act.activation(xTv[:, 4 * h:4 * h + 4, t * P:(t + 1) * P], v3(bank(7), 4), ACT.Copy)\
                       .then_inc(f_out, 1)

            def cross(t, step):
                n = t - 1
                if step < 2:
                    act.wait_ge(l_max, 2 * n + step + 1)
                    for c in range(2):
                        h = 2 * step + c
                        act.activation(s_c[:, h, :], bank(7)[:, c * 256:(c + 1) * 256], ACT.Exp,
                                       bias=nmx[:, h:h + 1], scale=0.125, accum_out=rs[:, h:h + 1])\
                           .then_inc(l_exp, 1)
                elif step < 4:
                    act.wait_ge(l_pT, 2 * n + step - 1)
                    act.activation(pT_l[:, 4 * step - 8:4 * step - 4, :], v3(bank(7), 4), ACT.Copy).then_inc(l_pTo, 1)
                elif step == 5:
                    act.wait_ge(l_oT, n + 1)
                    act.activation(oT_l, v3(bank(7)[:, 0:256], 2), ACT.Copy).then_inc(l_oTo, 1)

            for part in (0, 2, 3):
                ffn(0, part)
            act.wait_ge(ld_ffn, 32)

            def copy_xT(s):
                t = tile_head(s)[0]
                act.wait_ge(pq_q, s - 1)
                if isinstance(t, int):
                    act.wait_ge(f_out, 2 * t + 2)
                src = xTv[:, :, t * P:(t + 1) * P] if isinstance(t, int) else xTv[:, :, bass.ds(t * P, P)]
                act.activation(xT_cur[cur(s)], src, ACT.Copy).then_inc(xTcur_ready, 1)

            cur_m = [0]

            def cur(s):
                return (s if isinstance(s, int) else cur_m[0]) % 2

            def queries_out(s, w):
                act.wait_ge(pq_q, s + 1)
                act.activation(q_sb[:, 0:w], bank(4)[:, 0:w], ACT.Copy).then_inc(pq_qo, 1)

            def queriesT_out(s, w):
                act.wait_ge(pq_t, s + 1)
                act.activation(qT_sb[:, 0:w // P, :], v3(bank(5)[:, 0:w], w // P), ACT.Copy).then_inc(pq_to, 1)

            def scores_out(s):
                act.wait_ge(pq_s, s + 1)
                if not isinstance(s, int) or s > 0:
                    act.wait_ge(best_ready, s)
                act.activation(ss, v3(bank(6)[:, 0:256], 2), ACT.Copy).then_inc(pq_so, 1)

            def gates(s, m):
                act.wait_ge(best_ready, s + 1)
                act.activation(gate[:, m, :], bestv, ACT.Exp, bias=negtop, accum_out=esum).then_inc(gexp_ready, 1)

            def copy_x(b):
                t = tile_head(b)[0]
                if not isinstance(b, int) or b > 5:
                    act.wait_ge(u_used, b * TOPK - TOPK)
                if isinstance(t, int):
                    act.wait_ge(xn_ready, t + 1)
                src = xn[:, t * D:(t + 1) * D] if isinstance(t, int) else xn[:, bass.ds(t * D, D)]
                act.activation(xn_cur[cur(b)], src, ACT.Copy).then_inc(xcur_ready, 1)

            for s in range(2):
                queries_out(s, 512)
                queriesT_out(s, 512)
                scores_out(s)
                if s == 0:
                    gates(s, s)
            act.wait_ge(qc_done, 5)
            for c in range(2):
                act.activation(qcT_l[:, 4 * c:4 * c + 3, :], v3(bank(2 * c)[:, 0:3 * P], 3), ACT.Copy)\
                   .then_inc(qc_out, 1)
                act.activation(qcT_l[:, 4 * c + 3, :], bank(2 * c + 1)[:, 0:P], ACT.Copy).then_inc(qc_out, 1)

            def diagonals(b, k0, k1):
                base = fold if isinstance(b, int) and b <= 4 else ident[:, :]
                for k in range(k0, k1):
                    if k >= RING or not isinstance(b, int) or b > 1:
                        act.wait_ge(v_used, b * TOPK + (k - RING + 1 - TOPK))
                    act.activation(diag[:, k % RING, :], base, ACT.Copy,
                                   scale=coef[:, diag_m[0], k:k + 1]).then_inc(diag_ready, 1)

            diag_m = [0]

            def one(b, m, u, v):
                more = u and not (isinstance(b, int) and b + 2 >= BLOCKS)
                w = 512 if isinstance(b, int) and b + 2 < 4 else 256
                first = isinstance(b, int) and b == 0
                if more and not (isinstance(b, int) and b + 2 < 4):
                    cur_m[0] = m + 2
                    copy_xT(b + 2)
                if u and not (isinstance(b, int) and (b + 1 < 4 or b + 1 >= BLOCKS)):
                    cur_m[0] = m + 1
                    copy_x(b + 1)
                diag_m[0] = (m + 1) % 2
                if v:
                    act.wait_ge(coef_ready, b)
                    diagonals(b, 0, 2)
                for k in range(TOPK):
                    if v and k + 2 < TOPK:
                        diagonals(b, k + 2, k + 3)
                    if more and k == (12 if first else 1):
                        queries_out(b + 2, w)
                    if more and k == (14 if first else 3):
                        queriesT_out(b + 2, w)
                    if k == 3 and isinstance(b, int) and b < 2:
                        gates(b + 1, b + 1)
                    if more and k == (15 if first else 5):
                        scores_out(b + 2)
                    if k == 9 and isinstance(b, int) and b >= 33:
                        final(b - 33)
                    beside(b, k, cross, ffn)
                if u:
                    act.wait_ge(u_used, b * TOPK + TOPK)
                    act.activation(hgelu[:, m % 2, :], hdot[:, m % 2, :], ACT.Gelu).then_inc(gelu_ready, 1)
                if more and not first:
                    gates(b + 2, (m + 2) % 4)

            def final(t):
                act.wait_ge(acc_added, 8 * t + 4)
                act.wait_ge(u_used, TOPK * (8 * t + 4))
                chain(act.activation(y_out[t], xr(t), ACT.Square, accum_out=stat[:, 64 + t:65 + t]))
                act.activation(stat[:, 64 + t:65 + t], stat[:, 64 + t:65 + t], ACT.Sqrt, bias=eps[:, 0:1],
                               scale=1.0 / D).then_inc(fin_std, 1)

            run_blocks(act, one)
            final(TILES - 1)

        @block.vector
        def _(dve):
            chain, _, _, steps = chain_of(dve, chain_v)

            def scale_rows(n, src, parts=((0, D),)):
                w = len(parts)
                dve.wait_ge(std_ready, n + 1)
                if n >= 2:
                    dve.wait_ge(tr_done, n - 1)
                chain(dve.reciprocal(rstd[n % 2][:, 0:w], ssq[n % 2][:, 0:w]))
                for j, (a, b) in enumerate(parts):
                    ins = dve.tensor_scalar(xs[n % 2][:, a:b], src[j], rstd[n % 2][:, j:j + 1], None, ALU.mult)
                ins.then_inc(xs_ready, 1)

            def take_T(n, dst, g):
                dve.wait_ge(tr_done, n + 1)
                q = norm_bank(n)
                for j in range(2):
                    ins = dve.tensor_tensor(
                        dst[:, 4 * j:4 * j + 4], v3(bank(q + j), 4),
                        gains[:, g * KD + 4 * j:g * KD + 4 * j + 4].unsqueeze(2).broadcast_to([P, 4, P]), ALU.mult)
                ins.then_inc(xT_ready, 1)

            def tile_T(t):
                return xTv[:, :, t * P:(t + 1) * P]

            def sample_sinks():
                dve.wait_ge(ld_small, 32)
                dve.wait_ge(ld_late, 64)
                for kv in range(KV):
                    ins = dve.tensor_tensor(tmp[:, kv * 4:kv * 4 + 4], sinks[:, kv * 4:kv * 4 + 4], headsel[:, :],
                                            ALU.mult)
                chain(ins)
                chain(dve.tensor_reduce(sinks_s[:, :], v3(tmp[:, 0:8], 2), AX_X, ALU.add))

            def mask_gating():
                dve.wait_ge(ld_gating, 16 * 19)
                dve.tensor_tensor(wsp, wsp, tril.unsqueeze(1).broadcast_to([P, HEADS, P]), ALU.mult)
                for h in range(HEADS):
                    ins = dve.tensor_tensor(w_smp[:, h, :].rearrange("p (b r) -> p b r", b=16),
                                            blocks.rearrange("p (b r) -> p b r", b=16),
                                            w8[:, h, :].unsqueeze(1).broadcast_to([P, 16, 8]), ALU.mult)
                ins.then_inc(w_masked, 1)

            dve.wait_ge(ld_mem, 16)
            for j in range(2):
                scale_rows(j, [mem_x[:, j, :]])
            dve.wait_ge(gT_out, 1)
            for j in range(2):
                take_T(j, mem_T[:, :, j * P:(j + 1) * P], G_MEM)

            def rope(src, dst, t, n):
                r3 = src.rearrange("p (h d) -> p h d", d=HD)
                t3 = tmp[:, 0:n * HD].rearrange("p (h d) -> p h d", d=HD)
                half = HD // 2

                def ang(a, b):
                    return rot[:, t, a:b].unsqueeze(1).broadcast_to([P, n, b - a])

                dve.tensor_tensor(t3[:, :, 0:half], r3[:, :, half:HD], ang(HD, HD + half), ALU.mult)
                dve.tensor_tensor(t3[:, :, half:HD], r3[:, :, 0:half], ang(HD + half, 2 * HD), ALU.mult)
                ang_c = rot[:, t, 0:HD]
                if n == HEADS:
                    o = dst.rearrange("p (a j d) -> p j a d", j=2, d=HD)
                    for j in range(2):
                        ins = dve.tensor_tensor(o[:, j], r3[:, 4 * j:4 * j + 4],
                                                ang_c.unsqueeze(1).broadcast_to([P, 4, HD]), ALU.mult)
                    chain(ins)
                    for j in range(2):
                        ins = dve.tensor_tensor(o[:, j], o[:, j], t3[:, 4 * j:4 * j + 4], ALU.add)
                else:
                    o = dst.rearrange("p (h d) -> p h d", d=HD)
                    chain(dve.tensor_tensor(o, r3, ang_c.unsqueeze(1).broadcast_to([P, n, HD]), ALU.mult))
                    ins = dve.tensor_tensor(o, o, t3, ALU.add)
                return ins

            def mix_rows(t):
                dve.wait_ge(ld_x[t], 32 if t == 0 else 16)
                scale_rows(N_MIX + t, [xr(t)])

            mix_rows(0)
            take_T(N_MIX, tile_T(0), G_MIX)
            mix_rows(1)
            dve.wait_ge(ld_rot, 16)
            for t in range(TILES):
                if t + 1 < TILES:
                    take_T(N_MIX + t + 1, tile_T(t + 1), G_MIX)
                if t + 2 < TILES:
                    mix_rows(t + 2)
                dve.wait_ge(pq_done, t + 1)
                if t == 0:
                    dve.wait_ge(mkv_done, 2)
                ins = rope(bank(0), proj(t, 0, 512), t, HEADS)
                ins.then_inc(q_out, 1)
                dve.wait_ge(q_out, t + 1)
                dve.wait_ge(pkv_done, t + 1)
                chain(dve.tensor_copy(proj(t, 640, 768), bank(1)[:, P:2 * P]))
                ins = rope(bank(1)[:, 0:P], proj(t, 512, 640), t, KV)
                ins.then_inc(kv_out, 1)
                dve.wait_ge(kv_out, t + 1)
                if t == 1:
                    sample_sinks()
                if t == 2:
                    mask_gating()

            t3 = tmp.rearrange("p (h d) -> p h d", d=HD)

            def gating_squares(t):
                gv = proj(t, 1280, 1792).rearrange("p (h d) -> p h d", d=HD)
                dve.wait_ge(gv_out, t + 1)
                if t >= 2:
                    dve.wait_ge(sgu_out, t - 1)
                chain(dve.tensor_tensor(t3, gv, gv, ALU.mult))
                dve.tensor_reduce(gv_ss, t3, AX_X, ALU.add).then_inc(gv_ssq, 1)

            def gating_values(t):
                gv = proj(t, 1280, 1792).rearrange("p (h d) -> p h d", d=HD)
                dve.wait_ge(gv_std, t + 1)
                chain(dve.reciprocal(gv_r, gv_ss))
                chain(dve.tensor_tensor(gv, gv, gv_r.unsqueeze(2).broadcast_to([P, HEADS, HD]), ALU.mult))
                dve.tensor_tensor(proj(t, 1280, 1792), proj(t, 1280, 1792), g_sgu[:, :], ALU.mult).then_inc(gvn_out, 1)

            def gated(t):
                dve.wait_ge(mixed_done, t + 1)
                dve.wait_ge(gv_ssq, min(t + 2, TILES))
                bias = bias_s if t == 0 else bias_p
                chain(dve.tensor_tensor(t3, v3(bank(6 if t == 0 else 5), HEADS),
                                        bias.unsqueeze(2).broadcast_to([P, HEADS, HD]), ALU.add))
                dve.wait_ge(gu_out, t + 1)
                dve.tensor_tensor(proj(t, 768, 1280), proj(t, 768, 1280), tmp, ALU.mult).then_inc(sgu_out, 1)

            gating_squares(0)
            dve.wait_ge(qkT_out, 2)
            for bg in range(2):
                ins = dve.tensor_copy(qTr[:, bg, :].rearrange("p (b h i) -> p b h i", b=4, h=4),
                                      qT[:, :, bg * 32:(bg + 1) * 32].rearrange("p h (b i) -> p b h i", b=4))
            ins.then_inc(qTr_out, 1)
            dve.wait_ge(sc_done, 1)
            dve.wait_ge(ld_swa, 32)
            for j in range(4):
                ins = dve.scalar_tensor_tensor(s_smp[:, j, :], bank(j // 2)[:, (j % 2) * 192:(j % 2) * 192 + 192],
                                               0.125, smask[:, j % 2, :], ALU.mult, ALU.add)
            chain(ins)
            chain(dve.tensor_reduce(mx[:, 0:4], s_smp, AX_X, ALU.max))
            for kv in range(KV):
                ins = dve.tensor_tensor(mx[:, 2 * kv:2 * kv + 2], mx[:, 2 * kv:2 * kv + 2],
                                        sinks_s[:, kv:kv + 1].broadcast_to([P, 2]), ALU.max)
            chain(ins)
            chain(dve.tensor_scalar(nmx[:, 0:4], mx[:, 0:4], -1.0, None, ALU.mult))
            for kv in range(KV):
                ins = dve.tensor_tensor(es[:, 2 * kv:2 * kv + 2], nmx[:, 2 * kv:2 * kv + 2],
                                        sinks_s[:, kv:kv + 1].broadcast_to([P, 2]), ALU.add)
            ins.then_inc(sc_max, 1)
            gating_values(0)
            gating_squares(1)
            dve.wait_ge(sc_exp, 1)
            chain(dve.tensor_tensor(rs[:, 0:4], rs[:, 0:4], es[:, 0:4], ALU.add))
            chain(dve.reciprocal(rden[:, 0:4], rs[:, 0:4]))
            chain(dve.tensor_tensor(spread.rearrange("p (j h) -> p j h", h=4),
                                    rden[:, 0:4].unsqueeze(2).broadcast_to([P, 4, 4]),
                                    headsel[:, :].unsqueeze(1).broadcast_to([P, 4, 4]), ALU.mult))
            gated(0)
            dve.wait_ge(pv_done, 1)
            dve.tensor_tensor(o_exp.rearrange("p j (h d) -> p j h d", d=HD),
                              v3(bank(2)[:, 0:256], 4).unsqueeze(2).broadcast_to([P, 4, 4, HD]),
                              spread.rearrange("p (j h) -> p j h", h=4).unsqueeze(3).broadcast_to([P, 4, 4, HD]),
                              ALU.mult).then_inc(so_exp, 1)
            dve.wait_ge(so_done, 1)
            dve.wait_ge(qkT_done, 1)
            dve.tensor_copy(proj(0, 0, 512), bank(3)).then_inc(attn_out, 1)
            gating_values(1)

            def add_out(n, q, done, out):
                dve.wait_ge(done, n + 1)
                dve.tensor_tensor(xr(n), xr(n), ps[:, q * 512:(q + 2) * 512], ALU.add).then_inc(out, 1)

            def merged_rows(t):
                dve.wait_ge(attn_out, t + 1)
                dve.wait_ge(sgu_out, t + 1)
                scale_rows(N_MRG[t], [proj(t, 0, 512), proj(t, 768, 1280)], ((0, 512), (512, 1024)))

            def cross_rows(t):
                dve.wait_ge(x1_out, t + 1)
                dve.wait_ge(wo_done, t + 1)
                scale_rows(N_CRS[t], [xr(t)])

            def cross_take(t):
                take_T(N_CRS[t], tile_T(t), G_CRS)

            for t in range(1, TILES):
                lo = P if t == 1 else 0
                merged_rows(t - 1)
                dve.wait_ge(sc_done, t + 1)
                dve.wait_ge(sc_exp, t)
                if t > 1:
                    dve.wait_ge(pT_done, t)
                chain(dve.scalar_tensor_tensor(
                    s_sb[:, :, lo:], v3(ps[:, 0:2048], HEADS)[:, :, lo:], 0.125,
                    band[:, lo:].unsqueeze(1).broadcast_to([P, HEADS, 2 * P - lo]), ALU.mult, ALU.add))
                take_T(N_MRG[t - 1], tile_T(t - 1), G_MRG)
                chain(dve.tensor_reduce(mx, s_sb[:, :, lo:], AX_X, ALU.max))
                chain(dve.tensor_tensor(mx, mx, sinks[:, :], ALU.max))
                chain(dve.tensor_scalar(nmx, mx, -1.0, None, ALU.mult))
                dve.tensor_tensor(es, nmx, sinks[:, :], ALU.add).then_inc(sc_max, 1)
                if t + 1 < TILES:
                    gating_squares(t + 1)
                add_out(t - 1, 6, wo_done, x1_out)
                if lo == 0:
                    dve.wait_ge(pT_done, t + 1)
                    dve.tensor_copy(pT[:, 0:8, :], ps[:, 0:1024].rearrange("p (a b) -> p a b", a=8)).then_inc(pT_out, 1)
                dve.wait_ge(sc_exp, t + 1)
                chain(dve.tensor_tensor(rs, rs, es, ALU.add))
                chain(dve.reciprocal(rden, rs))
                gated(t)
                if t == TILES - 1:
                    cross_rows(0)
                dve.wait_ge(pv_done, t + 1)
                dve.tensor_tensor(proj(t, 0, 512).rearrange("p (h d) -> p h d", d=HD),
                                  v3(bank(0), HEADS), rden.unsqueeze(2).broadcast_to([P, HEADS, HD]), ALU.mult)\
                   .then_inc(attn_out, 1)
                if t + 1 < TILES:
                    gating_values(t + 1)
            cross_take(0)
            merged_rows(TILES - 1)
            take_T(N_MRG[TILES - 1], tile_T(TILES - 1), G_MRG)
            cross_rows(1)
            dve.wait_ge(qc_out, 1)
            dve.wait_ge(qbd_zero, 1)
            for c in range(2):
                for j in range(2):
                    h = 2 * c + j
                    ins = dve.tensor_copy(
                        q_bd[64 * j:64 * j + 64, c, :].rearrange("p (b h i) -> p b h i", b=8, h=4)[:, :, h, :],
                        qcT[64 * j:64 * j + 64, c, 0:NS].rearrange("p (b i) -> p b i", b=8))
            ins.then_inc(qbd_out, 1)
            dve.wait_ge(c_sc, 1)
            chain(dve.tensor_reduce(mx[:, 0:2], v3(ps[:, 0:512], 2), AX_X, ALU.max))
            dve.tensor_scalar(nmx[:, 0:2], mx[:, 0:2], -0.125, None, ALU.mult).then_inc(c_max, 1)
            cross_take(1)
            cross_rows(2)
            add_out(TILES - 1, 6, wo_done, x1_out)
            cross_take(2)
            dve.wait_ge(c_exp, 2)
            chain(dve.reciprocal(rden[:, 0:2], rs[:, 0:2]))
            chain(dve.tensor_tensor(spread[:, 0:8].rearrange("p (g h) -> p g h", h=4),
                                    rden[:, 0:2].unsqueeze(2).broadcast_to([P, 2, 4]),
                                    headsel[:, :].unsqueeze(1).broadcast_to([P, 2, 4]), ALU.mult))
            dve.wait_ge(c_pv, 1)
            dve.tensor_tensor(o_m.rearrange("p g (h d) -> p (g h) d", d=HD), v3(bank(4), 8),
                              spread[:, 0:8].unsqueeze(2).broadcast_to([P, 8, HD]), ALU.mult).then_inc(c_om, 1)
            cross_rows(3)
            dve.wait_ge(c_sel, 1)
            dve.tensor_copy(o_c, bank(5)[:, 256:512]).then_inc(c_o, 1)
            cross_take(3)
            cross_rows(4)
            add_out(0, 6, c_wo, x2_out)

            def ffn(t, part):
                if part == 1:
                    dve.wait_ge(f_std, t + 1)
                    chain(dve.reciprocal(rstd_f[:, t:t + 1], ssq_f[:, t:t + 1]))
                    dve.scalar_tensor_tensor(xn[:, t * D:(t + 1) * D], xr(t), rstd_f[:, t:t + 1], g_ffn,
                                             ALU.mult, ALU.mult).then_inc(xn_ready, 1)

            def cross(t, step):
                n = t - 1
                if step < 2:
                    w = slice(2 * step, 2 * step + 2)
                    dve.wait_ge(l_sc, 2 * n + step + 1)
                    if n > 0:
                        dve.wait_ge(l_exp, 4 * n)
                    chain(dve.tensor_reduce(mx[:, w], v3(bank(7), 2), AX_X, ALU.max))
                    dve.tensor_scalar(nmx[:, w], mx[:, w], -0.125, None, ALU.mult).then_inc(l_max, 1)
                elif step == 4:
                    dve.wait_ge(l_exp, 4 * n + 4)
                    chain(dve.reciprocal(rden[:, 0:4], rs[:, 0:4]))
                    dve.wait_ge(l_pv, n + 1)
                    for j in range(2):
                        ins = dve.tensor_tensor(o_l.rearrange("p (c j d) -> p j c d", j=2, d=HD)[:, j],
                                                v3(bank(7)[:, j * P:(j + 1) * P], 2),
                                                rden[:, 2 * j:2 * j + 2].unsqueeze(2).broadcast_to([P, 2, HD]),
                                                ALU.mult)
                    ins.then_inc(l_o, 1)
                elif step >= 6:
                    c = step - 6
                    dve.wait_ge(l_wo, 2 * n + c + 1)
                    part = xr(t)[:, c * 512:(c + 1) * 512]
                    dve.tensor_tensor(part, part, bank(7), ALU.add).then_inc(l_add, 1)

            dve.wait_ge(ld_ffn, 32)
            dve.wait_ge(x2_out, 1)
            ffn(0, 1)
            cross_take(4)

            def apart():
                dve.sem_inc(apart_v, 1)

            def top16(values, vals, inds, rest):
                apart()
                chain(dve.max(vals[:, 0:8], values))
                apart()
                dve.max_index(inds[:, 0:8], vals[:, 0:8], values)
                chain(dve.match_replace(rest, vals[:, 0:8], values, LOWEST))
                apart()
                chain(dve.max(vals[:, 8:16], rest))
                apart()
                return dve.max_index(inds[:, 8:16], vals[:, 8:16], rest)

            def top_keys(s, c):
                if c == 0:
                    dve.wait_ge(pq_so, s + 1)
                chain(top16(ss[:, c, :], topv[:, c, :], topi[:, c, :], ss2[:, c, :]))

            def best_pairs(s):
                if not isinstance(s, int) or s > 0:
                    dve.wait_ge(gexp_ready, s)
                c3 = cand.rearrange("p (a b) -> p a b", a=TOPK)
                chain(dve.tensor_tensor(c3, topv[:, 0, :].unsqueeze(2).broadcast_to([P, TOPK, TOPK]),
                                        topv[:, 1, :].unsqueeze(1).broadcast_to([P, TOPK, TOPK]), ALU.add))
                chain(top16(cand, bestv, besti, cand2))
                dve.tensor_scalar(negtop, bestv[:, 0:1], -1.0, None, ALU.mult).then_inc(best_ready, 1)

            def experts_of(s, m):
                dve.tensor_scalar(parts[:, 0, :], besti, 4, None, ALU.logical_shift_right)
                chain(dve.tensor_scalar(parts[:, 1, :], besti, 15, None, ALU.bitwise_and))
                hot = onehot.rearrange("p (a b) -> p a b", b=TOPK)
                chain(dve.tensor_tensor(hot, parts.rearrange("p c k -> p (c k)").unsqueeze(2)
                                        .broadcast_to([P, 2 * TOPK, TOPK]),
                                        iota[:, :].unsqueeze(1).broadcast_to([P, 2 * TOPK, TOPK]), ALU.is_equal))
                hot4 = onehot.rearrange("p (c a b) -> p c a b", c=2, b=TOPK)
                for c in range(2):
                    ins = dve.tensor_tensor(hot4[:, c], hot4[:, c],
                                            topi[:, c, :].unsqueeze(1).broadcast_to([P, TOPK, TOPK]), ALU.mult)
                chain(ins)
                chain(dve.tensor_reduce(chosen.rearrange("p c k -> p (c k)"), hot, AX_X, ALU.add))
                if not isinstance(s, int) or s >= 4:
                    dve.wait_ge(v_landed[3], 64 * (s - 3))
                dve.scalar_tensor_tensor(idx[:, m, :], chosen[:, 0, :], float(NKEYS), chosen[:, 1, :],
                                         ALU.mult, ALU.add).then_inc(idx_ready, 1)

            def finish_gates(s, m):
                dve.wait_ge(gexp_ready, s + 1)
                chain(dve.reciprocal(rsum, esum))
                chain(dve.tensor_scalar(gate[:, m, :], gate[:, m, :], rsum, None, ALU.mult))

            for c in range(2):
                top_keys(0, c)
            best_pairs(0)
            experts_of(0, 0)
            finish_gates(0, 0)

            def add_acc(b, m):
                s = b - 2
                dve.wait_ge(v_used, s * TOPK + TOPK)
                t = 0 if isinstance(s, int) and s < 4 else tile_head(s)[0]
                q = 2 * (m % 2)
                ins = dve.tensor_tensor(xr(t), xr(t), ps[:, q * 512:(q + 2) * 512], ALU.add)
                ins.then_inc(acc_added, 1)

            def add_last(b, m):
                if not isinstance(b, int) or b >= 3:
                    dve.wait_ge(acc_added, b - 2)
                add_acc(b, m)

            def one(b, m, u, v):
                more = u and not (isinstance(b, int) and b + 2 >= BLOCKS)
                if u:
                    sample = isinstance(b, int) and b < 4
                    if sample:
                        dve.wait_ge(xn_ready, 1)
                    else:
                        dve.wait_ge(xcur_ready, b - 3)
                    if isinstance(b, int) and b == 0:
                        for c in range(2):
                            top_keys(1, c)
                    for k in range(TOPK):
                        dve.wait_ge(u_landed[k % RING], b * 64 + 16 * (k // RING + 1))
                        rows = xn[:, 0:D] if sample else xn_cur[m % 2]
                        dve.tensor_tensor_reduce(u_ring[k % RING], u_ring[k % RING], rows, 1.0, 0.0, ALU.mult,
                                                 ALU.add, hdot[:, m % 2, k:k + 1]).then_inc(u_used, 1)
                        if isinstance(b, int) and b == 0 and k == 2:
                            best_pairs(1)
                            experts_of(1, 1)
                        if isinstance(b, int) and b == 1 and k < 2:
                            top_keys(2, k)
                        if isinstance(b, int) and b == 1 and k == 2:
                            best_pairs(2)
                        if isinstance(b, int) and b == 1 and k == 3:
                            experts_of(2, 2)
                        gates_at = 4 if isinstance(b, int) and b < 2 else 1
                        if k == gates_at and not (isinstance(b, int) and b + 1 >= BLOCKS):
                            finish_gates(b + 1, (m + 1) % 4)
                        if k == 3 and (not isinstance(b, int) or b >= 2):
                            add_last(b, m)
                        pick = more and not (isinstance(b, int) and b == 0)
                        if pick and k in (5, 7):
                            top_keys(b + 2, (k - 5) // 2)
                        if pick and k == 9:
                            best_pairs(b + 2)
                        if pick and k == 11:
                            experts_of(b + 2, (m + 2) % 4)
                        if k == 12 and isinstance(b, int) and b >= 33:
                            final(b - 33)
                        beside(b, k, cross, ffn)
                    dve.wait_ge(gelu_ready, b + 1)
                    dve.tensor_tensor(coef[:, m % 2, :], hgelu[:, m % 2, :], gate[:, m, :], ALU.mult)\
                       .then_inc(coef_ready, 1)
                else:
                    add_last(b, m)
                    final(b - 33)

            def final(t):
                dve.wait_ge(ld_fin, 16)
                dve.wait_ge(fin_std, t + 1)
                c = stat[:, 72 + t:73 + t]
                chain(dve.reciprocal(c, stat[:, 64 + t:65 + t]))
                dve.scalar_tensor_tensor(y_out[t], xr(t), c, g_fin, ALU.mult, ALU.mult).then_inc(fin_y, 1)

            for b in range(5):
                one(b, b % 4, True, b >= 1)
            start, steps[1] = steps[1], 0
            with dve.Fori(5, 30, 4) as b0:
                steps[0] = b0 * CHAIN_PER_BLOCK + (start - 5 * CHAIN_PER_BLOCK)
                for j in range(4):
                    one(b0 + j, (5 + j) % 4, True, True)
                assert steps[1] == 4 * CHAIN_PER_BLOCK, steps
            steps[:] = [0, start + 28 * CHAIN_PER_BLOCK]
            for b in range(33, BLOCKS + 1):
                one(b, b % 4, b < BLOCKS, True)
            dve.wait_ge(acc_added, BLOCKS - 1)
            add_acc(BLOCKS + 1, (BLOCKS + 1) % 4)
            final(TILES - 1)

        @block.tensor
        def _(pe):
            def transposes(n):
                pe.wait_ge(xs_ready, n + 1)
                if n >= 2:
                    pe.wait_ge(xT_ready, n if n > N_MRG[TILES - 1] else n - 1)
                q = norm_bank(n)
                for k in range(KD):
                    ins = pe.transpose(bank(q + k // 4)[:, (k % 4) * P:(k % 4 + 1) * P],
                                       xs[n % 2][:, k * P:(k + 1) * P], ident[:, :])
                ins.then_inc(tr_done, 1)

            def product(out, lhs, rhs, n=KD):
                for k in range(n):
                    ins = pe.matmul(out, lhs(k), rhs(k), start=(k == 0), stop=(k == n - 1))
                return ins

            pe.wait_ge(ld_tab, 32)
            pe.wait_ge(ld_rows, 16 * 7)
            pe.transpose(bank(3)[:, 0:48], rows48, ident[0:48, 0:48]).then_inc(gT_done, 1)
            transposes(0)
            transposes(1)
            for j in range(2):
                pe.wait_ge(xT_ready, j + 1)
                if j == 0:
                    pe.wait_ge(ld_wmkv, 32)
                product(bank(j)[:, 0:256], lambda k: mem_T[:, k, j * P:(j + 1) * P], lambda k: w_mk[:, k, :])
                product(bank(j)[:, 256:512], lambda k: mem_T[:, k, j * P:(j + 1) * P], lambda k: w_mv[:, k, :])\
                    .then_inc(mkv_done, 1)
                transposes(N_MIX + j)
            for t in range(TILES):
                if 1 < t + 1 < TILES:
                    transposes(N_MIX + t + 1)
                pe.wait_ge(xT_ready, N_MIX + t + 1)
                for c, (a, b, done, out) in enumerate(((0, 512, pq_done, q_out), (512, 768, pkv_done, kv_out),
                                                       (768, 1280, pgu_done, gu_out), (1280, 1792, pgv_done, gv_out))):
                    if t == 0:
                        pe.wait_ge(ld_win[c], 16)
                        if c == 0:
                            pe.wait_ge(mkv_out, 4)
                        if c == 2:
                            for half in range(2):
                                for j in range(2):
                                    ins = pe.transpose(bank(3)[:, half * 256 + j * P:half * 256 + (j + 1) * P],
                                                       mk[:, j, half * P:(half + 1) * P], ident[:, :])
                            ins.then_inc(mkT_done, 1)
                        if c == 3:
                            pe.wait_ge(mkT_out, 1)
                    else:
                        pe.wait_ge(out, t)
                    product(bank(c)[:, 0:b - a], lambda k: xTv[:, k, t * P:(t + 1) * P],
                            lambda k: w_in[:, k, a:b]).then_inc(done, 1)

            pe.wait_ge(w_masked, 1)
            for n, w in enumerate((wsp, w_smp)):
                for h in range(HEADS):
                    ins = pe.transpose(ps[:, 2048 + n * 1024 + h * P:2048 + n * 1024 + (h + 1) * P], w[:, h, :],
                                       ident[:, :])
            ins.then_inc(wT_done, 1)

            pe.wait_ge(ld_kc, 16)
            pe.wait_ge(kv_out, TILES)
            pe.wait_ge(q_out, TILES)
            for b in range(SAMPLES):
                ins = pe.transpose(ps[:, b * P:(b + 1) * P], kc[:, b, :], ident[:, :])
            ins.then_inc(kcT_done, 1)

            def heads_T(t):
                q = 2 if t == 0 else 4
                for a in range(4):
                    pe.transpose(bank(q)[:, a * P:(a + 1) * P], proj(t, a * P, (a + 1) * P), ident[:, :])
                pe.transpose(bank(q + 1)[:, 0:P], proj(t, 512, 640), ident[:, :]).then_inc(qkT_done, 1)

            pe.wait_ge(gu_out, TILES)
            pe.wait_ge(gv_out, TILES)
            heads_T(0)

            def gating(t, out):
                pe.wait_ge(gvn_out, t + 1)
                for h in range(HEADS):
                    ins = pe.matmul(out[:, h * HD:(h + 1) * HD], (wT_s if t == 0 else wT_p)[:, h, :],
                                    proj(t, 1280 + h * HD, 1280 + (h + 1) * HD), start=True, stop=True)
                ins.then_inc(mixed_done, 1)

            pe.wait_ge(kcT_out, 1)
            pe.wait_ge(qTr_out, 1)
            for j in range(4):
                kv, bg = j // 2, j % 2
                rows = slice(64 * kv, 64 * kv + 64)
                o = bank(j // 2)[:, (j % 2) * 192:(j % 2) * 192 + 192]
                ins = pe.matmul(o[:, P:P + NS], qTr[rows, bg, :], kT[rows, 0:NS], start=True, stop=True)
                for s in range(4):
                    ins = pe.matmul(o[32 * s:32 * s + 32, 0:P], qTr[rows, bg, 32 * s:32 * s + 32],
                                    kcT[rows, bg * 4 + s, :], start=True, stop=True)
            ins.then_inc(sc_done, 1)
            pe.wait_ge(sc_exp, 1)
            for j in range(4):
                pe.transpose(bank(4)[:, j * P:(j + 1) * P], s_smp[:, j, 0:P], ident[:, :])
                ins = pe.transpose(bank(5)[0:NS, j * P:(j + 1) * P], s_smp[:, j, P:P + NS], ident[:, :])
            ins.then_inc(pT_done, 1)
            pe.wait_ge(wT_out, 2)
            gating(0, bank(6))
            pe.wait_ge(pT_out, 2)
            heads_T(1)
            pe.wait_ge(ld_swa, 32)
            for j in range(4):
                kv, bg = j // 2, j % 2
                o = bank(2)[:, j * HD:(j + 1) * HD]
                pe.matmul(o, pTn[0:NS, j, :], proj(0, 640 + kv * HD, 640 + (kv + 1) * HD)[0:NS],
                          start=True, stop=False, skip_group_check=True)
                for s in range(4):
                    ins = pe.matmul(o[32 * s:32 * s + 32], pTc[:, j, 32 * s:32 * s + 32],
                                    vc[:, bg * 4 + s, kv * HD:(kv + 1) * HD], start=False, stop=(s == 3),
                                    skip_group_check=True)
            ins.then_inc(pv_done, 1)
            pe.wait_ge(so_exp, 1)
            for kv in range(KV):
                for bg in range(2):
                    ins = pe.matmul(bank(3)[:, kv * 256:(kv + 1) * 256], v3(gather[:, :], 2)[:, bg, :],
                                    o_exp[:, kv * 2 + bg, :], start=(bg == 0), stop=(bg == 1))
            ins.then_inc(so_done, 1)

            def out_half(t, c):
                return product(bank(6 + c), lambda k: xTv[:, k, t * P:(t + 1) * P],
                               lambda k: w_out[:, k, c * 512:(c + 1) * 512])

            def merged_T(t):
                if t > 0:
                    pe.wait_ge(x1_out, t)
                transposes(N_MRG[t])

            for t in range(1, TILES):
                lo = P if t == 1 else 0
                pe.wait_ge(qkT_out, 2 * t + 2)
                pe.wait_ge(attn_out, t)
                for h in range(HEADS):
                    rows = slice(64 * (h // 4), 64 * (h // 4) + 64)
                    ins = pe.matmul(ps[:, h * 256 + lo:(h + 1) * 256], qT[rows, h % 4, :],
                                    kT[rows, (t - 1) * P + lo:(t + 1) * P], start=True, stop=True)
                ins.then_inc(sc_done, 1)
                merged_T(t - 1)
                if t + 1 < TILES:
                    pe.wait_ge(sgu_out, t)
                    heads_T(t + 1)
                pe.wait_ge(xT_ready, N_MRG[t - 1] + 1)
                if t == 1:
                    pe.wait_ge(ld_wout, 16)
                out_half(t - 1, 0)
                out_half(t - 1, 1).then_inc(wo_done, 1)
                pe.wait_ge(sc_exp, t + 1)
                for h in range(HEADS):
                    for c in range(2):
                        if c * P >= lo:
                            ins = pe.transpose(ps[:, (c * 8 + h) * P:(c * 8 + h + 1) * P],
                                               s_sb[:, h, c * P:(c + 1) * P], ident[:, :])
                ins.then_inc(pT_done, 1)
                pe.wait_ge(qkT_out, 2 * min(t + 2, TILES))
                gating(t, bank(5))
                pe.wait_ge(pT_out, 2 * t + 1)
                for h in range(HEADS):
                    kv = h // 4
                    for c in range(2):
                        if c * P < lo:
                            continue
                        vt = t - 1 + c
                        ins = pe.matmul(bank(0)[:, h * HD:(h + 1) * HD], pT[:, c * 8 + h, :],
                                        proj(vt, 640 + kv * HD, 640 + (kv + 1) * HD),
                                        start=(c * P == lo), stop=(c == 1))
                ins.then_inc(pv_done, 1)

            def sample_queries(c):
                return product(bank(1)[:, c * P:(c + 1) * P], lambda k: w_cq[:, k, c * P:(c + 1) * P],
                               lambda k: xTv[:, k, 0:P])

            transposes(N_CRS[0])
            pe.wait_ge(ld_wc, 16)
            pe.wait_ge(xT_ready, N_CRS[0] + 1)
            sample_queries(0)
            merged_T(TILES - 1)
            sample_queries(1).then_inc(qc_done, 1)
            pe.wait_ge(xT_ready, N_MRG[TILES - 1] + 1)
            out_half(TILES - 1, 0)
            pe.wait_ge(ld_mcache_k, 16 * SAMPLES)
            for g in range(4):
                if g >= 2:
                    pe.wait_ge(kmT_out, g - 1)
                for b in range(2):
                    for c in range(2):
                        for j in range(2):
                            o = km_bank(g) * 512 + (b * 2 + c) * 256 + j * P
                            ins = pe.transpose(ps[:, o:o + P], kmem[:, 2 * g + b, j, c * P:(c + 1) * P], ident[:, :])
                ins.then_inc(kmT_done, 1)
            pe.wait_ge(qbd_out, 1)
            pe.wait_ge(kmT_out, 4)
            for b in range(SAMPLES):
                for c in range(2):
                    ins = pe.matmul(bank(0)[32 * (b % 4):32 * (b % 4) + 32, (b // 4) * 256:(b // 4 + 1) * 256],
                                    q_bd[:, c, b * 32:(b + 1) * 32], kmT[:, b, c, :], start=(c == 0), stop=(c == 1))
            ins.then_inc(c_sc, 1)
            transposes(N_CRS[1])
            out_half(TILES - 1, 1).then_inc(wo_done, 1)
            transposes(N_CRS[2])
            pe.wait_ge(c_exp, 2)
            for bg in range(2):
                for c in range(2):
                    ins = pe.transpose(bank(1)[:, (bg * 2 + c) * P:(bg * 2 + c + 1) * P],
                                       s_cs[:, bg, c * P:(c + 1) * P], ident[:, :])
            ins.then_inc(c_pT, 1)
            pe.wait_ge(c_pTo, 1)
            pe.wait_ge(ld_mcache_v, 16 * SAMPLES)
            for b in range(SAMPLES):
                r = 32 * (b % 4)
                for c in range(2):
                    ins = pe.matmul(bank(4)[r:r + 32, (b // 4) * 256:(b // 4 + 1) * 256],
                                    pT_c[:, (b // 4) * 2 + c, r:r + 32], vmem[:, b, c, :], start=(c == 0),
                                    stop=(c == 1))
            ins.then_inc(c_pv, 1)
            pe.wait_ge(ld_sk, 16)
            pe.wait_ge(xT_ready, N_CRS[2] + 1)
            for n in range(16):
                ins = pe.transpose(ps[:, n * P:(n + 1) * P], sk_raw[:, n, :], ident[:, :])
            ins.then_inc(skT_done, 1)
            pe.wait_ge(c_om, 1)
            for bg in range(2):
                ins = pe.matmul(bank(5)[:, 256:512], v3(gather[:, :], 2)[:, bg, :], o_m[:, bg, :],
                                start=(bg == 0), stop=(bg == 1))
            ins.then_inc(c_sel, 1)
            pe.wait_ge(skT_out, 1)
            transposes(N_CRS[3])
            pe.wait_ge(c_o, 1)
            for c in range(2):
                ins = pe.transpose(bank(5)[:, c * P:(c + 1) * P], o_c[:, c * P:(c + 1) * P], ident[:, :])
            ins.then_inc(c_oT, 1)
            pe.wait_ge(c_oTo, 1)
            pe.wait_ge(ld_wco, 16)
            for c in range(2):
                ins = product(bank(6 + c), lambda k: oT_c[:, k, :], lambda k: w_co[:, k, c * 512:(c + 1) * 512], 2)
            ins.then_inc(c_wo, 1)

            def prompt_queries(c, last):
                pe.wait_ge(xT_ready, N_CRS[3 + last] + 1)
                cols = slice(4 * P, 5 * P) if last else slice(P, 4 * P)
                product(bank(2 * c + last)[:, 0:cols.stop - cols.start], lambda k: w_cq[:, k, c * P:(c + 1) * P],
                        lambda k: xTv[:, k, cols]).then_inc(qc_done, 1)

            prompt_queries(0, 0)

            def ffn(t, part):
                if part < 2:
                    return
                h = part - 2
                pe.wait_ge(xn_ready, t + 1)
                if 2 * t + h > 0:
                    pe.wait_ge(f_out, 2 * t + h)
                for k in range(4):
                    ins = pe.transpose(bank(7)[:, k * P:(k + 1) * P],
                                       xn[:, t * D + (4 * h + k) * P:t * D + (4 * h + k + 1) * P], ident[:, :])
                ins.then_inc(f_tr, 1)

            def cross(t, step):
                n = t - 1
                if step < 2:
                    if step == 0:
                        pe.wait_ge(qc_out, 5)
                        pe.wait_ge(f_out, 2 if t == 1 else 4)
                        if n > 0:
                            pe.wait_ge(l_add, 2 * n)
                    else:
                        pe.wait_ge(l_exp, 4 * n + 2)
                    rows = slice(64 * step, 64 * step + 64)
                    for c in range(2):
                        ins = pe.matmul(bank(7)[:, c * 256:(c + 1) * 256], qcT_l[rows, 4 * c + n, :], mkT[rows, c, :],
                                        start=True, stop=True)
                    ins.then_inc(l_sc, 1)
                elif step < 4:
                    if step == 2:
                        pe.wait_ge(l_exp, 4 * n + 4)
                    else:
                        pe.wait_ge(l_pTo, 2 * n + 1)
                    for i in range(4):
                        ins = pe.transpose(bank(7)[:, i * P:(i + 1) * P],
                                           s_c[:, 2 * step - 4 + i // 2, (i % 2) * P:(i % 2 + 1) * P], ident[:, :])
                    ins.then_inc(l_pT, 1)
                elif step == 4:
                    pe.wait_ge(l_pTo, 2 * n + 2)
                    pe.wait_ge(mv_moved, 1)
                    for i in range(MHEADS):
                        h = 2 * (i % 2) + i // 2
                        for c in range(2):
                            ins = pe.matmul(bank(7)[:, i * HD:(i + 1) * HD], pT_l[:, i * 2 + c, :],
                                            mv_l[:, c, h * HD:(h + 1) * HD], start=(c == 0), stop=(c == 1))
                    ins.then_inc(l_pv, 1)
                elif step == 5:
                    pe.wait_ge(l_o, n + 1)
                    for c in range(2):
                        ins = pe.transpose(bank(7)[:, c * P:(c + 1) * P], o_l[:, c * P:(c + 1) * P], ident[:, :])
                    ins.then_inc(l_oT, 1)
                else:
                    c = step - 6
                    if c == 0:
                        pe.wait_ge(l_oTo, n + 1)
                    else:
                        pe.wait_ge(l_add, 2 * n + 1)
                    product(bank(7), lambda k: oT_l[:, k, :], lambda k: w_co[:, k, c * 512:(c + 1) * 512], 2)\
                        .then_inc(l_wo, 1)

            pe.wait_ge(x2_out, 1)
            ffn(0, 2)
            transposes(N_CRS[4])
            ffn(0, 3)

            pe.wait_ge(ld_wpq, 32)
            pe.wait_ge(skT_out, 1)

            def heads_of(s):
                return (s, s + 4) if isinstance(s, int) and s < 4 else (tile_head(s)[1],)

            def q_mm(s, m, first=0, end=None):
                sample = isinstance(s, int) and s < 4
                if first == 0:
                    if sample:
                        pe.wait_ge(f_out, 2)
                    else:
                        pe.wait_ge(xTcur_ready, s - 3)
                    if not isinstance(s, int) or s > 0:
                        pe.wait_ge(pq_qo, s)
                steps = [(j, h, k) for j, h in enumerate(heads_of(s)) for k in range(KD)]
                for j, h, k in steps[first:end]:
                    rhs = w_pq[:, k, h * 256:(h + 1) * 256] if isinstance(h, int) else w_pq[:, k, bass.ds(h * 256, 256)]
                    ins = pe.matmul(bank(4)[:, j * 256:(j + 1) * 256],
                                    xTv[:, k, 0:P] if sample else xT_cur[m % 2][:, k, :], rhs,
                                    start=(k == 0), stop=(k == KD - 1))
                if end is None or end == len(steps):
                    ins.then_inc(pq_q, 1)

            def q_T(s):
                pe.wait_ge(pq_qo, s + 1)
                if not isinstance(s, int) or s > 0:
                    pe.wait_ge(pq_to, s)
                for j in range(2 * len(heads_of(s))):
                    ins = pe.transpose(bank(5)[:, j * P:(j + 1) * P], q_sb[:, j * P:(j + 1) * P], ident[:, :])
                ins.then_inc(pq_t, 1)

            def scores(s):
                pe.wait_ge(pq_to, s + 1)
                if not isinstance(s, int) or s > 0:
                    pe.wait_ge(pq_so, s)
                hs = heads_of(s)
                for j, h in enumerate(hs):
                    r = slice(0, P) if len(hs) == 1 else slice(j * NS, (j + 1) * NS)
                    for c in range(2):
                        rhs = (skT[:, (2 * h + c) * P:(2 * h + c + 1) * P] if isinstance(h, int)
                               else skT[:, bass.ds(h * 256 + c * P, P)])
                        ins = pe.matmul(bank(6)[r, c * P:(c + 1) * P], qT_sb[:, 2 * j + c, r], rhs, start=True, stop=True)
                ins.then_inc(pq_s, 1)

            for s in range(2):
                q_mm(s, s)
                q_T(s)
                scores(s)
            prompt_queries(0, 1)
            prompt_queries(1, 0)
            prompt_queries(1, 1)

            def experts(b, m, k0, k1):
                q = 2 * ((m + 1) % 2)
                if k0 == 0 and (not isinstance(b, int) or b >= 3):
                    pe.wait_ge(acc_added, b - 2)
                for k in range(k0, k1):
                    pe.wait_ge(diag_ready, b * TOPK + (k + 1 - TOPK))
                    pe.wait_ge(v_landed[k % RING], b * 64 + 16 * (k // RING + 1) - 64)
                    for c in range(2):
                        ins = pe.matmul(bank(q + c), diag[:, k % RING, :], v_ring[k % RING][:, c * 512:(c + 1) * 512],
                                        start=(k == 0), stop=(k == TOPK - 1))
                    ins.then_inc(v_used, 1)

            def one(b, m, u, v):
                more = u and not (isinstance(b, int) and b + 2 >= BLOCKS)
                first = isinstance(b, int) and b == 0
                if more and not first:
                    q_mm(b + 2, m + 2)
                for k in range(TOPK):
                    if v:
                        experts(b, m, k, k + 1)
                    if more and k == (12 if first else 1):
                        q_T(b + 2)
                    if more and k == (14 if first else 3):
                        scores(b + 2)
                    beside(b, k, cross, ffn)
                    if first and 4 <= k < 12:
                        q_mm(2, 2, 2 * (k - 4), 2 * (k - 3))

            run_blocks(pe, one)


CHAIN_PER_BLOCK = 19

_INS = ['x_prompt', 'x_sample', 'mem_prompt', 'cache_swa_k', 'cache_swa_v', 'cache_mem_k', 'cache_mem_v',
        'g_mix', 'w_in', 'attn_sinks', 'g_sgu', 'w_spatial', 'b_spatial', 'g_attn_out', 'g_gmlp_out', 'w_out',
        'g_cross', 'g_mem', 'w_cq', 'w_mk', 'w_mv', 'w_co', 'g_ffn', 'w_peer_q', 'peer_sub_keys', 'peer_u',
        'peer_v', 'g_final']
_OUTS = {"y_p": (1, 512, D), "y_s": (8, 8, D), "swa_k_p": (1, 1, P, KV, HD), "swa_v_p": (1, 1, P, KV, HD),
         "mem_k": (1, 1, NMEM, MHEADS, HD), "mem_v": (1, 1, NMEM, MHEADS, HD),
         "swa_k_s": (1, 8, P, KV, HD), "swa_v_s": (1, 8, P, KV, HD), "sgu_v": (1, 8, 8, HEADS, HD)}


def kernel(**inputs):
    import concourse.bacc as _bacc
    from concourse.bass_utils import run_bass_kernel_spmd as _run

    nc = _bacc.Bacc("TRN2", target_bir_lowering=False, num_devices=1)
    arrays, I, O = {}, {}, {}
    for name in _INS:
        a = np.ascontiguousarray(inputs[name])
        arrays[f"in_{name}"] = a
        I[name] = nc.dram_tensor(f"in_{name}", a.shape, F32, kind="ExternalInput").ap()
    for name, a in shape_tables().items():
        arrays[f"tab_{name}"] = a
        I["tab_" + name] = nc.dram_tensor(f"tab_{name}", a.shape, F32, kind="ExternalInput").ap()
    for name, shape in _OUTS.items():
        O[name] = nc.dram_tensor(f"out_{name}", shape, F32, kind="ExternalOutput").ap()
    hybrid_step(nc, I, O)
    r = _run(nc, [arrays], core_ids=[0])
    return tuple(r.results[0][f"out_{name}"] for name in _OUTS)
```
